# Optimizing a Trainium2 kernel written in Bass

```python
import math
import jax, jax.numpy as jnp
from jax import lax
import numpy as np

D_MODEL = 1024
BATCH = 1
SEQ = 256
DEPTH = 2

N_A_LAYERS = (DEPTH + 1) // 2
N_B_LAYERS = DEPTH // 2
DIFF_HEAD_DIM = 64
DIFF_V_DIM = 2 * DIFF_HEAD_DIM
DIFF_HEADS = D_MODEL // DIFF_V_DIM
MOBA_HEAD_DIM = 64
MOBA_HEADS = D_MODEL // MOBA_HEAD_DIM
MOBA_BLOCK = 256
MOBA_TOPK = 3
D_FF = 4 * D_MODEL
REL_BUCKETS = 32
REL_MAX_DIST = 128
REL_HEADS = 2 * DIFF_HEADS
Q_BLOCK = 128
DEEPNORM_ALPHA = (2 * DEPTH) ** 0.25
DEEPNORM_BETA = (8 * DEPTH) ** -0.25
LN_EPS = 1e-5


def rel_bucket(rel):
    n = jnp.maximum(rel, 0)
    max_exact = REL_BUCKETS // 2
    nf = jnp.maximum(n, max_exact).astype(jnp.float32)
    large = max_exact + (jnp.log(nf / max_exact) / math.log(REL_MAX_DIST / max_exact)
                         * (REL_BUCKETS - max_exact)).astype(jnp.int32)
    large = jnp.minimum(large, REL_BUCKETS - 1)
    return jnp.where(n < max_exact, n, large)

def layer_norm(x, g, b):
    xf = x.astype(jnp.float32)
    mu = jnp.mean(xf, axis=-1, keepdims=True)
    var = jnp.mean(jnp.square(xf - mu), axis=-1, keepdims=True)
    y = (xf - mu) * lax.rsqrt(var + LN_EPS) * g.astype(jnp.float32) + b.astype(jnp.float32)
    return y.astype(x.dtype)

def diff_lambda_init(layer):
    return 0.8 - 0.6 * math.exp(-0.3 * layer)

def squared_relu_mlp(x, w_up, w_down):
    return jnp.square(jax.nn.relu(x @ w_up)) @ w_down

def diff_attention(x, w_in, lam_p, subln_g, w_out, rel_bias, lam_init):
    B, S, _ = x.shape
    H, dh, dv = DIFF_HEADS, DIFF_HEAD_DIM, DIFF_V_DIM
    qkv = x @ w_in
    q, k, v = jnp.split(qkv, [2 * H * dh, 4 * H * dh], axis=-1)
    q = q.reshape(B, S, H, 2, dh) * (dh ** -0.5)
    k = k.reshape(B, S, H, 2, dh)
    v = v.reshape(B, S, H, dv)
    lf = lam_p.astype(jnp.float32)
    lam = jnp.exp(jnp.sum(lf[0] * lf[1])) - jnp.exp(jnp.sum(lf[2] * lf[3])) + lam_init
    kpos = jnp.arange(S)

    def block(i):
        q_blk = lax.dynamic_slice_in_dim(q, i * Q_BLOCK, Q_BLOCK, axis=1)
        qpos = i * Q_BLOCK + jnp.arange(Q_BLOCK)
        rel = qpos[:, None] - kpos[None, :]
        bias = rel_bias[rel_bucket(rel)].astype(jnp.float32)
        bias = bias.reshape(Q_BLOCK, S, H, 2).transpose(2, 3, 0, 1)
        s = jnp.einsum('bqhmd,bkhmd->bhmqk', q_blk, k).astype(jnp.float32) + bias
        s = jnp.where(rel >= 0, s, -jnp.inf)
        p = jax.nn.softmax(s, axis=-1)
        a = p[:, :, 0] - lam * p[:, :, 1]
        return jnp.einsum('bhqk,bkhe->bqhe', a.astype(v.dtype), v)

    o = lax.map(block, jnp.arange(S // Q_BLOCK))
    o = o.transpose(1, 0, 2, 3, 4).reshape(B, S, H, dv).astype(jnp.float32)
    o = o * lax.rsqrt(jnp.mean(o * o, axis=-1, keepdims=True) + LN_EPS)
    o = o * subln_g.astype(jnp.float32) * (1.0 - lam_init)
    return o.reshape(B, S, H * dv).astype(x.dtype) @ w_out

def shared_kv(x, w_kv):
    B, S, _ = x.shape
    H, dh, L = MOBA_HEADS, MOBA_HEAD_DIM, MOBA_BLOCK
    k, v = jnp.split(x @ w_kv, 2, axis=-1)
    k = k.reshape(B, S, H, dh).transpose(0, 2, 1, 3)
    v = v.reshape(B, S, H, dh).transpose(0, 2, 1, 3)
    n_blk = -(-S // L)
    pad = n_blk * L - S
    k = jnp.pad(k, ((0, 0), (0, 0), (0, pad), (0, 0)))
    v = jnp.pad(v, ((0, 0), (0, 0), (0, pad), (0, 0)))
    k_blocks = k.reshape(B, H, n_blk, L, dh)
    v_blocks = v.reshape(B, H, n_blk, L, dh)
    k_mean = jnp.mean(k_blocks.astype(jnp.float32), axis=3)
    return k_blocks, v_blocks, k_mean

def moba_attention(x, w_q, w_out, k_blocks, v_blocks, k_mean, rel_bias):
    B, S, _ = x.shape
    H, dh, L = MOBA_HEADS, MOBA_HEAD_DIM, MOBA_BLOCK
    n_blk = k_blocks.shape[2]
    topk = min(MOBA_TOPK, n_blk)
    scale = dh ** -0.5
    q = (x @ w_q).reshape(B, S, H, dh).transpose(0, 2, 1, 3)
    bi = jnp.arange(B)[:, None, None]
    hi = jnp.arange(H)[None, :, None]
    blk_ids = jnp.arange(n_blk)
    offs = jnp.arange(L)

    def block(i):
        q_c = lax.dynamic_slice_in_dim(q, i * Q_BLOCK, Q_BLOCK, axis=2)
        qpos = i * Q_BLOCK + jnp.arange(Q_BLOCK)
        own = (i * Q_BLOCK) // L
        g = jnp.einsum('bhqd,bhnd->bhqn', q_c.astype(jnp.float32), k_mean)
        past = blk_ids[None, :] < (qpos // L)[:, None]
        g = jnp.where(past, g, -jnp.inf)
        g_val, sel = lax.top_k(g, topk)
        sel_ok = jnp.isfinite(g_val)
        k_own = lax.dynamic_index_in_dim(k_blocks, own, axis=2, keepdims=False)
        v_own = lax.dynamic_index_in_dim(v_blocks, own, axis=2, keepdims=False)
        rel_own = qpos[:, None] - (own * L + offs)[None, :]
        b_own = rel_bias[rel_bucket(rel_own)].astype(jnp.float32).transpose(2, 0, 1)
        s_own = jnp.einsum('bhqd,bhkd->bhqk', q_c, k_own).astype(jnp.float32) * scale + b_own
        logits = [jnp.where(rel_own >= 0, s_own, -jnp.inf)]
        for j in range(topk):
            idx = sel[..., j]
            k_sel = k_blocks[bi, hi, idx]
            rel = qpos[:, None] - (idx[..., None] * L + offs)
            b_sel = rel_bias[rel_bucket(rel), hi[..., None]].astype(jnp.float32)
            s = jnp.einsum('bhqd,bhqkd->bhqk', q_c, k_sel).astype(jnp.float32) * scale + b_sel
            logits.append(jnp.where(sel_ok[..., j, None], s, -jnp.inf))
        p = jax.nn.softmax(jnp.concatenate(logits, axis=-1), axis=-1).astype(v_blocks.dtype)
        o = jnp.einsum('bhqk,bhkd->bhqd', p[..., :L], v_own)
        for j in range(topk):
            v_sel = v_blocks[bi, hi, sel[..., j]]
            o = o + jnp.einsum('bhqk,bhqkd->bhqd', p[..., (j + 1) * L:(j + 2) * L], v_sel)
        return o

    o = lax.map(block, jnp.arange(S // Q_BLOCK))
    o = o.transpose(1, 0, 3, 2, 4).reshape(B, S, H * dh)
    return o @ w_out

def first_inputs(seed: int = 0) -> dict:
    key = jax.random.key(seed)
    ks = jax.random.split(key, 20)
    f32 = jnp.float32
    D = D_MODEL
    s_in = D ** -0.5
    w_qk_a = jax.random.normal(ks[1], (N_A_LAYERS, D, 4 * D_MODEL // 2), f32) * s_in
    w_v_a = jax.random.normal(ks[2], (N_A_LAYERS, D, DIFF_HEADS * DIFF_V_DIM), f32) * s_in * DEEPNORM_BETA
    w_k_sh = jax.random.normal(ks[5], (D, MOBA_HEADS * MOBA_HEAD_DIM), f32) * s_in
    w_v_sh = jax.random.normal(ks[6], (D, MOBA_HEADS * MOBA_HEAD_DIM), f32) * s_in * DEEPNORM_BETA
    return {
        'x': jax.random.normal(ks[0], (BATCH, SEQ, D), f32),
        'w_in_a': jnp.concatenate([w_qk_a, w_v_a], axis=-1),
        'lam_a': jax.random.normal(ks[3], (N_A_LAYERS, 4, DIFF_HEAD_DIM), f32) * 0.1,
        'subln_a': 1.0 + 0.02 * jax.random.normal(ks[4], (N_A_LAYERS, DIFF_V_DIM), f32),
        'w_out_a': jax.random.normal(ks[7], (N_A_LAYERS, D, D), f32) * s_in * DEEPNORM_BETA,
        'w_kv_shared': jnp.concatenate([w_k_sh, w_v_sh], axis=-1),
        'w_q_b': jax.random.normal(ks[8], (N_B_LAYERS, D, MOBA_HEADS * MOBA_HEAD_DIM), f32) * s_in,
        'w_out_b': jax.random.normal(ks[9], (N_B_LAYERS, D, D), f32) * s_in * DEEPNORM_BETA,
        'rel_bias': jax.random.normal(ks[10], (REL_BUCKETS, REL_HEADS), f32) * 0.5,
        'ln1_g': 1.0 + 0.02 * jax.random.normal(ks[11], (DEPTH, D), f32),
        'ln1_b': 0.02 * jax.random.normal(ks[12], (DEPTH, D), f32),
        'ln2_g': 1.0 + 0.02 * jax.random.normal(ks[13], (DEPTH, D), f32),
        'ln2_b': 0.02 * jax.random.normal(ks[14], (DEPTH, D), f32),
        'w_up': jax.random.normal(ks[15], (DEPTH, D, D_FF), f32) * s_in,
        'w_down': jax.random.normal(ks[16], (DEPTH, D_FF, D), f32) * (D_FF ** -0.5) * DEEPNORM_BETA,
    }

def first_block(x, w_in_a, lam_a, subln_a, w_out_a, w_kv_shared, w_q_b, w_out_b, rel_bias,
              ln1_g, ln1_b, ln2_g, ln2_b, w_up, w_down):
    h = x
    kv = None
    for layer in range(DEPTH):
        if layer < N_A_LAYERS:
            mix = diff_attention(h, w_in_a[layer], lam_a[layer], subln_a[layer], w_out_a[layer],
                                 rel_bias, diff_lambda_init(layer))
        else:
            if kv is None:
                kv = shared_kv(h, w_kv_shared)
            j = layer - N_A_LAYERS
            mix = moba_attention(h, w_q_b[j], w_out_b[j], kv[0], kv[1], kv[2], rel_bias)
        h = layer_norm(DEEPNORM_ALPHA * h + mix, ln1_g[layer], ln1_b[layer])
        h = layer_norm(DEEPNORM_ALPHA * h + squared_relu_mlp(h, w_up[layer], w_down[layer]),
                       ln2_g[layer], ln2_b[layer])
    return h


DEPTH_2 = 1

RET_HEADS = 4
RET_DK = 256
RET_DV = 256
RET_CHUNK = 128
MLA_HEADS = 8
MLA_NOPE = 128
MLA_ROPE = 64
MLA_V = 128
MLA_Q_LORA = 384
MLA_KV_LORA = 256
ATTN_BLOCK = 128
ROPE_THETA = 10000.0
N_GROUPS = 4
EXPERTS_PER_GROUP = 8
TOP_K = 2
D_EXPERT = 256
EPS = 1e-6

RET_QK_W = RET_HEADS * RET_DK
RET_V_W = RET_HEADS * RET_DV
MLA_V_W = MLA_HEADS * MLA_V
SPLITS = [RET_QK_W, RET_QK_W, RET_V_W, RET_V_W, MLA_Q_LORA, MLA_KV_LORA, MLA_ROPE, D_MODEL, D_MODEL]
IN_W = sum(SPLITS)


def rmsnorm(x, g):
    xf = x.astype(jnp.float32)
    y = xf * lax.rsqrt(jnp.mean(xf * xf, axis=-1, keepdims=True) + EPS)
    return (y * g.astype(jnp.float32)).astype(x.dtype)

def modulate(x, shift, scale):
    return x * (1.0 + scale) + shift

def rope_tables(pos, dim):
    inv = ROPE_THETA ** (-jnp.arange(0, dim, 2, dtype=jnp.float32) / dim)
    ang = pos[:, None] * inv[None, :]
    return jnp.cos(ang), jnp.sin(ang)

def apply_rope(x, cos, sin):
    x1, x2 = jnp.split(x.astype(jnp.float32), 2, axis=-1)
    cos = cos[None, :, None, :]
    sin = sin[None, :, None, :]
    return jnp.concatenate([x1 * cos - x2 * sin, x2 * cos + x1 * sin], axis=-1).astype(x.dtype)

def retention(q, k, v):
    b, s, h, dk = q.shape
    dv = v.shape[-1]
    c = RET_CHUNK
    n = s // c
    log_gamma = jnp.log1p(-jnp.exp2(-5.0 - jnp.arange(h, dtype=jnp.float32)))
    idx = jnp.arange(c, dtype=jnp.float32)
    rel = idx[:, None] - idx[None, :]
    decay_in = jnp.where(rel[None] >= 0, jnp.exp(log_gamma[:, None, None] * jnp.maximum(rel, 0.0)[None]), 0.0)
    xi = jnp.exp(log_gamma[:, None] * (idx[None, :] + 1.0))
    zeta = jnp.exp(log_gamma[:, None] * (c - 1.0 - idx[None, :]))
    chunk_decay = jnp.exp(log_gamma * c)

    def to_chunks(t):
        return t.astype(jnp.float32).reshape(b, n, c, h, t.shape[-1]).transpose(1, 0, 2, 3, 4)

    qc = to_chunks(q)
    kc = to_chunks(k) * (dk ** -0.5)
    vc = to_chunks(v)

    def step(state, inp):
        qi, ki, vi = inp
        scores = jnp.einsum('bihd,bjhd->bhij', qi, ki) * decay_in[None]
        y = jnp.einsum('bhij,bjhe->bihe', scores, vi) + jnp.einsum('bihd,hi,bhde->bihe', qi, xi, state)
        state = state * chunk_decay[None, :, None, None] + jnp.einsum('bjhd,hj,bjhe->bhde', ki, zeta, vi)
        return state, y

    state0 = jnp.zeros((b, h, dk, dv), jnp.float32)
    _, ys = lax.scan(step, state0, (qc, kc, vc))
    return ys.transpose(1, 0, 2, 3, 4).reshape(b, s, h, dv)

def head_norm(y):
    mu = jnp.mean(y, axis=-1, keepdims=True)
    var = jnp.mean(jnp.square(y - mu), axis=-1, keepdims=True)
    return (y - mu) * lax.rsqrt(var + EPS)

def mla(c_q, c_kv, k_pe, q_norm, kv_norm, w_uq, w_ukv, cos, sin):
    b, s, _ = c_q.shape
    q = (rmsnorm(c_q, q_norm) @ w_uq).reshape(b, s, MLA_HEADS, MLA_NOPE + MLA_ROPE)
    q_nope, q_pe = q[..., :MLA_NOPE], q[..., MLA_NOPE:]
    q_pe = apply_rope(q_pe, cos, sin)
    kv = (rmsnorm(c_kv, kv_norm) @ w_ukv).reshape(b, s, MLA_HEADS, MLA_NOPE + MLA_V)
    k_nope, v = kv[..., :MLA_NOPE], kv[..., MLA_NOPE:]
    k_pe = apply_rope(k_pe[:, :, None, :], cos, sin)[:, :, 0, :]
    scale = (MLA_NOPE + MLA_ROPE) ** -0.5
    outs = []
    for blk in range(s // ATTN_BLOCK):
        lo = blk * ATTN_BLOCK
        hi = lo + ATTN_BLOCK
        scores = (jnp.einsum('bqhd,bkhd->bhqk', q_nope[:, lo:hi], k_nope[:, :hi])
                  + jnp.einsum('bqhr,bkr->bhqk', q_pe[:, lo:hi], k_pe[:, :hi])).astype(jnp.float32) * scale
        mask = (lo + jnp.arange(ATTN_BLOCK))[:, None] >= jnp.arange(hi)[None, :]
        p = jax.nn.softmax(jnp.where(mask, scores, -jnp.inf), axis=-1).astype(v.dtype)
        outs.append(jnp.einsum('bhqk,bkhd->bqhd', p, v[:, :hi]))
    return jnp.concatenate(outs, axis=1).reshape(b, s, MLA_V_W)

def token_mixer(u, w_in, w_ret_o, q_norm, kv_norm, w_uq, w_ukv, w_mla_o, w_out, ret_rope, mla_rope):
    b, s, _ = u.shape
    proj = u @ w_in
    offs = np.cumsum(SPLITS)[:-1].tolist()
    rq, rk, rv, rg, c_q, c_kv, k_pe, gate_ret, gate_mla = jnp.split(proj, offs, axis=-1)
    rq = apply_rope(rq.reshape(b, s, RET_HEADS, RET_DK), *ret_rope)
    rk = apply_rope(rk.reshape(b, s, RET_HEADS, RET_DK), *ret_rope)
    rv = rv.reshape(b, s, RET_HEADS, RET_DV)
    y_ret = head_norm(retention(rq, rk, rv)).reshape(b, s, RET_V_W).astype(u.dtype)
    y_ret = (jax.nn.silu(rg) * y_ret) @ w_ret_o
    y_mla = mla(c_q, c_kv, k_pe, q_norm, kv_norm, w_uq, w_ukv, *mla_rope) @ w_mla_o
    merged = jax.nn.sigmoid(gate_ret) * y_ret + jax.nn.sigmoid(gate_mla) * y_mla
    return merged @ w_out

def hier_moe(u, w_grp, b_grp, w_exp, b_exp, w1, w3, w2):
    b, s, d = u.shape
    t = u.reshape(-1, d)
    n_tok = t.shape[0]
    grp_logits = (t @ w_grp).astype(jnp.float32) + b_grp.astype(jnp.float32)
    grp_prob = jax.nn.softmax(grp_logits, axis=-1)
    _, g_sel = lax.top_k(grp_logits, 1)
    p_grp = jnp.take_along_axis(grp_prob, g_sel, axis=-1)
    exp_logits = ((t @ w_exp).astype(jnp.float32) + b_exp.astype(jnp.float32)).reshape(n_tok, N_GROUPS, EXPERTS_PER_GROUP)
    in_grp = jnp.take_along_axis(exp_logits, g_sel[:, :, None], axis=1)[:, 0]
    top_val, top_idx = lax.top_k(in_grp, TOP_K)
    top_w = jax.nn.softmax(top_val, axis=-1) * p_grp
    exp_w = jnp.sum(jax.nn.one_hot(top_idx, EXPERTS_PER_GROUP, dtype=jnp.float32) * top_w[..., None], axis=1)
    gate = jax.nn.one_hot(g_sel[:, 0], N_GROUPS, dtype=jnp.float32)[:, :, None] * exp_w[:, None, :]
    out = jnp.zeros_like(t)
    for gi in range(N_GROUPS):
        hid = jax.nn.silu(jnp.einsum('td,edf->tef', t, w1[gi])) * jnp.einsum('td,edf->tef', t, w3[gi])
        hid = hid * gate[:, gi, :, None].astype(hid.dtype)
        out = out + jnp.einsum('tef,efd->td', hid, w2[gi])
    return out.reshape(b, s, d)

def second_inputs(seed: int = 0) -> dict:
    key = jax.random.key(seed)
    ks = jax.random.split(key, 24)
    L = DEPTH_2
    G, E, F = N_GROUPS, EXPERTS_PER_GROUP, D_EXPERT

    def nrm(k, shape, fan_in, scale=1.0):
        return jax.random.normal(k, shape, jnp.float32) * (scale * fan_in ** -0.5)

    def gain(k, shape):
        return 1.0 + 0.02 * jax.random.normal(k, shape, jnp.float32)

    return {
        "x": jax.random.normal(ks[0], (BATCH, SEQ, D_MODEL), jnp.float32),
        "c": jax.random.normal(ks[1], (BATCH, D_MODEL), jnp.float32),
        "w_ada": nrm(ks[2], (L, D_MODEL, 6 * D_MODEL), D_MODEL, 0.5),
        "b_ada": 0.02 * jax.random.normal(ks[3], (L, 6 * D_MODEL), jnp.float32),
        "norm1": gain(ks[4], (L, D_MODEL)),
        "norm2": gain(ks[5], (L, D_MODEL)),
        "w_in": nrm(ks[6], (L, D_MODEL, IN_W), D_MODEL),
        "w_ret_o": nrm(ks[7], (L, RET_V_W, D_MODEL), RET_V_W),
        "q_norm": gain(ks[8], (L, MLA_Q_LORA)),
        "kv_norm": gain(ks[9], (L, MLA_KV_LORA)),
        "w_uq": nrm(ks[10], (L, MLA_Q_LORA, MLA_HEADS * (MLA_NOPE + MLA_ROPE)), MLA_Q_LORA),
        "w_ukv": nrm(ks[11], (L, MLA_KV_LORA, MLA_HEADS * (MLA_NOPE + MLA_V)), MLA_KV_LORA),
        "w_mla_o": nrm(ks[12], (L, MLA_V_W, D_MODEL), MLA_V_W),
        "w_out": nrm(ks[13], (L, D_MODEL, D_MODEL), D_MODEL),
        "w_grp": nrm(ks[14], (L, D_MODEL, G), D_MODEL),
        "b_grp": 0.01 * jax.random.normal(ks[15], (L, G), jnp.float32),
        "w_exp": nrm(ks[16], (L, D_MODEL, G * E), D_MODEL),
        "b_exp": 0.01 * jax.random.normal(ks[17], (L, G * E), jnp.float32),
        "w1": nrm(ks[18], (L, G, E, D_MODEL, F), D_MODEL),
        "w3": nrm(ks[19], (L, G, E, D_MODEL, F), D_MODEL),
        "w2": nrm(ks[20], (L, G, E, F, D_MODEL), F),
        "final_norm": gain(ks[21], (D_MODEL,)),
    }

def second_block(x, c, w_ada, b_ada, norm1, norm2, w_in, w_ret_o, q_norm, kv_norm, w_uq, w_ukv, w_mla_o, w_out,
              w_grp, b_grp, w_exp, b_exp, w1, w3, w2, final_norm):
    s = x.shape[1]
    pos = jnp.arange(s, dtype=jnp.float32)
    ret_rope = rope_tables(pos, RET_DK)
    mla_rope = rope_tables(pos, MLA_ROPE)
    c_act = jax.nn.silu(c)
    h = x
    for l in range(DEPTH_2):
        mod = (c_act @ w_ada[l] + b_ada[l])[:, None, :]
        sh1, sc1, g1, sh2, sc2, g2 = jnp.split(mod, 6, axis=-1)
        u = modulate(rmsnorm(h, norm1[l]), sh1, sc1)
        h = h + g1 * token_mixer(u, w_in[l], w_ret_o[l], q_norm[l], kv_norm[l], w_uq[l], w_ukv[l],
                                 w_mla_o[l], w_out[l], ret_rope, mla_rope)
        u = modulate(rmsnorm(h, norm2[l]), sh2, sc2)
        h = h + g2 * hier_moe(u, w_grp[l], b_grp[l], w_exp[l], b_exp[l], w1[l], w3[l], w2[l])
    return rmsnorm(h, final_norm)


def setup_inputs(seed=0):
    out = dict(first_inputs(seed))
    for name, value in second_inputs(seed + 1).items():
        if name != "x":
            out[name + "_2"] = value
    return out


def reference(
    x, w_in_a, lam_a, subln_a, w_out_a, w_kv_shared, w_q_b, w_out_b, rel_bias, ln1_g, ln1_b,
    ln2_g, ln2_b, w_up, w_down, c_2, w_ada_2, b_ada_2, norm1_2, norm2_2, w_in_2, w_ret_o_2,
    q_norm_2, kv_norm_2, w_uq_2, w_ukv_2, w_mla_o_2, w_out_2, w_grp_2, b_grp_2, w_exp_2,
    b_exp_2, w1_2, w3_2, w2_2, final_norm_2,
):
    x = first_block(
        x, w_in_a, lam_a, subln_a, w_out_a, w_kv_shared, w_q_b, w_out_b, rel_bias, ln1_g, ln1_b,
        ln2_g, ln2_b, w_up, w_down,
    )
    return second_block(
        x, c_2, w_ada_2, b_ada_2, norm1_2, norm2_2, w_in_2, w_ret_o_2, q_norm_2, kv_norm_2,
        w_uq_2, w_ukv_2, w_mla_o_2, w_out_2, w_grp_2, b_grp_2, w_exp_2, b_exp_2, w1_2, w3_2,
        w2_2, final_norm_2,
    )


_drawn_inputs = setup_inputs


def setup_inputs(seed=0):
    import zlib

    import numpy as np

    out = dict(_drawn_inputs(seed))
    spreads = {}
    factors = {'lam_a': 8.0,
     'subln_a': 7.066,
     'b_ada_2': 2.784,
     'norm1_2': 6.261,
     'norm2_2': 4.839,
     'q_norm_2': 8.0,
     'kv_norm_2': 8.0,
     'b_grp_2': 6.046,
     'b_exp_2': 5.93,
     'final_norm_2': 2.834}
    for name, (base, spread) in spreads.items():
        noise = np.random.default_rng([zlib.crc32(name.encode()), seed]).standard_normal(out[name].shape)
        drawn = base * np.exp(spread * noise) if base else spread * noise
        out[name] = __import__('jax').numpy.asarray(drawn.astype(out[name].dtype))
    for name, factor in factors.items():
        out[name] = (out[name] * factor).astype(out[name].dtype)
    return out
```

```python
import math
from contextlib import ExitStack

import numpy as np

import concourse.bass as bass
from concourse import mybir

D = 1024
KT = D // 128
SEQ = 256
QT = SEQ // 128
D_FF = 4096
PAIRS = D_FF // 256
RING = 6
EXPERTS = 32
SLOTS = 64
ROUNDS = SEQ // SLOTS
STEPS = EXPERTS // 2
ALPHA = (2 * 2) ** 0.25
NEG = -1e30
LN_EPS = 1e-5
EPS = 1e-6
MLA_SCALE = (128 + 64) ** -0.5

CONST_WIDTHS = [("ident", 128), ("cos_ret", 256), ("sin_ret", 256), ("cos_mla", 256), ("sin_mla", 256),
                ("decay", 1024), ("tri", 128), ("ones", 128), ("iota", 64), ("mask", 384), ("order", 8)]
CONST_AT = {}
_at = 0
for _name, _w in CONST_WIDTHS:
    CONST_AT[_name] = (_at, _at + _w)
    _at += _w
CONST_COLS = _at

VEC = {}
_at = 0
for _name, _rows in [("ln1_g", 16), ("ln1_b", 16), ("ln2_g", 16), ("ln2_b", 16), ("norm1_2", 8), ("norm2_2", 8),
                     ("q_norm_2", 3), ("kv_norm_2", 2), ("subln_a", 1), ("c_2", 8)]:
    VEC[_name] = (_at, _rows)
    _at += _rows
VEC_ROWS = _at

B_ATT = [0, 48]
B_MLP = [16, 64]
B_C = 96
B_RQK = 100
B_UQ = 108
B_UKV = 111
B_RV = 113
B_RG = 117
B_GR = 121
B_RO = 125
B_GM = 129
B_MO = 133
B_WO = 137
B_MOE = 141
TP_LATENTS = 56


def program(nc, A):
    f32, i32 = mybir.dt.float32, mybir.dt.int32
    ALU, ACT, AX = mybir.AluOpType, mybir.ActivationFunctionType, mybir.AxisListType
    ctx = ExitStack()
    with ctx:
        def sb(name, shape, dt=f32):
            return ctx.enter_context(nc.sbuf_tensor(name, shape, dt))

        consts = sb("consts", [128, CONST_COLS])
        ring = sb("ring", [128, RING, 2048])
        h_tm = sb("h_tm", [128, QT, D])
        x_t = sb("x_t", [128, KT, SEQ])
        v_tm = sb("v_tm", [128, QT, D])
        q_t = sb("q_t", [128, KT, SEQ])
        k_t = sb("k_t", [128, KT, SEQ])
        o_tm = sb("o_tm", [128, QT, D])
        big = sb("big", [128, 6144])
        scr = sb("scr", [128, 3, 1536])
        pe_rope = sb("pe_rope", [128, 6, SEQ])
        mod = sb("mod", [128, 6144])
        stage = sb("stage", [128, 2, 1024])
        rows_g = sb("rows_g", [128, 1024])
        rows_b = sb("rows_b", [128, 1024])
        vec_rows = sb("vec_rows", [128, 128])
        vec = sb("vec", [128, 128])
        modc = sb("modc", [128, 4, 8])
        relb = sb("relb", [33, 16])
        bias_rows = sb("bias_rows", [16, 512])
        onehot = scr[0:33, 0, 0:512]
        lam_rows = sb("lam_rows", [128, 256])
        lam_t = sb("lam_t", [128, 2, 64])
        lam_s = sb("lam_s", [128, 4])
        act_c = sb("act_c", [128, 8])
        brow = sb("brow", [1, 64])
        w_rt = sb("w_rt", [128, KT, 36])
        st6 = sb("st6", [128, 8, 2, 6])
        mv = sb("mv", [128, 8, 2])
        sv = sb("sv", [128, 8])
        sr = sb("sr", [128, 8])
        rstd = sb("rstd", [128, 8])
        nmax = sb("nmax", [128, 2, 4])
        esum = sb("esum", [128, 2, 4])
        rsum = sb("rsum", [128, 2, 4])

        def con(name, rows=128):
            a, b = CONST_AT[name]
            return consts[0:rows, a:b]

        ident = con("ident")
        bias = big[:, :].rearrange("p (h k) -> p h k", h=16)
        prob = scr[:, 0, :].rearrange("p (b m k) -> p b m k", b=2, m=2)
        prob_t = scr[:, 1, :].rearrange("p (b m k) -> p b m k", b=2, m=2)
        relu = scr[:, 0, :].rearrange("p (b n) -> p b n", b=3)
        hid = scr[:, 1, :].rearrange("p (b f n) -> p b f n", b=3, f=2)
        qn_t = big[:, 0:2048].rearrange("p (h t) -> p h t", h=8)
        kn_t = big[:, 2048:4096].rearrange("p (h t) -> p h t", h=8)
        v_mla = big[:, 4096:6144].rearrange("p (q n) -> p q n", q=2)
        rg = big[:, 0:2048].rearrange("p (q n) -> p q n", q=2)
        gate = big[:, 2048:4096].rearrange("p (q n) -> p q n", q=2)
        merged = big[:, 4096:6144].rearrange("p (q n) -> p q n", q=2)
        scr_flat = scr[:, :, :].rearrange("p a b -> p (a b)")
        lat = scr_flat[:, 0:1792].rearrange("p (q n) -> p q n", q=2)
        lat_t = scr_flat[:, 1792:3072].rearrange("p (c t) -> p c t", c=5)
        st_ret = scr[:, 2, :].rearrange("p (h k) -> p h k", h=4)
        o_mla = k_t[:, :, :].rearrange("p (q a) t -> p q (a t)", q=2)

        xe = x_t[:, 0:4, :].rearrange("p a t -> p (a t)").rearrange("p (k s) -> p k s", k=8)
        ysb = x_t[:, 4:8, :].rearrange("p a t -> p (a t)")
        room = [0, 0]

        def carve(part, *dims):
            size = math.prod(dims)
            at = room[part]
            room[part] += size
            assert room[part] <= 1536
            names = "abc"[:len(dims)]
            piece = scr[:, part, at:at + size]
            if len(dims) == 1:
                return piece
            pattern = f"p ({' '.join(names)}) -> p {' '.join(names)}"
            return piece.rearrange(pattern, **dict(zip(names[:-1], dims[:-1])))

        sel, gsel, gsel_t, silu_a = (carve(0, QT, 128) for _ in range(4))
        hid_x = carve(0, 2, 2, SLOTS)
        plan = carve(1, ROUNDS * STEPS + 1, 8)
        route = carve(1, QT, 64)
        router = carve(1, QT, 80)
        gates, picked, posn = (carve(1, QT, EXPERTS) for _ in range(3))
        now = sb("now", [128, 8])
        cnt = sb("cnt", [128, 8])
        trips = sb("trips", [128, 2], i32)

        moe = v_tm

        acc = ctx.enter_context(nc.psum_tensor("acc", [128, 4, 512], f32))
        pp = ctx.enter_context(nc.psum_tensor("pp", [128, 2, 512], f32))
        tp = ctx.enter_context(nc.psum_tensor("tp", [128, 2, 512], f32))

        up_bank = (pp[:, 0, :], acc[:, 2, :])

        def sem(name):
            return ctx.enter_context(nc.semaphore(name))

        w_full = [sem(f"w_full{i}") for i in range(RING)]
        ada_full = [sem(f"ada_full{i}") for i in range(2)]
        S = {n: sem(n) for n in """
            w_used consts_in x_in relb_in vec_in lam_in onehot_in rowsg_in rowsb_in small_in badd_in
            relb_set vecrow_set bias_mm bias_copied bias_dram bias_in vec_mm vec_done
            tp_ready tp_done x_ready v_done q_done k_done sc_ready nmax_ready exp_done attw_ready o_ready o_done
            osq_ready osq_rstd o_scaled ln_stat ln_rstd ln_out h_done up_ready relu_done hid_ready hid_used
            dve_chain act_chain pool_chain lam_ready lam_exp lam_done c_silu ada_done mod_mm mod_done modc_done acc_taken
            lat_copied lat_stat lat_rstd lat_done rq_done rk_done uqr_in kpe_done uq_ready uq_done pe_done vmla_done
            rv_done sret_ready st_ready y_ready y_done hn_stat hn_rstd rg_done gr_done yret_ready ret_merged gm_done
            mla_merged wo_done out_stored out_ready
            r_stat r_rstd r_out lg_ready lg_copied lg_max lg_exp lg_m2 lg_e2 mask_ready pos_ready trips_ready
            sel_ready xe_ready xe_done silu_e hid_e gt_ready gt_done y_half ysb_half cmb_ready cmb_done moe_g final_chain
            """.split()}
        block = ctx.enter_context(nc.Block())

        def w_row_tiles(w, kt, cols):
            return w[kt * 128:(kt + 2) * 128, cols].rearrange("(k p) n -> p k n", p=128)

        def w_cols(w, cols):
            return w[:, cols].rearrange("(k p) n -> p k n", p=128)

        def slot(b):
            return b % RING

        @block.sync
        def _(sp):
            def load(b, src, at=0):
                n = src.shape[1] * src.shape[2]
                if b >= RING:
                    sp.wait_ge(S["w_used"], b - RING + 1)
                dst = ring[:, slot(b), 0:n].rearrange("p (k n) -> p k n", k=src.shape[1])
                sp.dma_start(dst, src).then_inc(w_full[slot(b)], 16)

            def cols(a, n):
                return slice(a, a + n)

            sp.dma_start(consts[:, :], A["consts"]).then_inc(S["consts_in"], 16)
            sp.dma_start(h_tm[:, :, :], A["x"][0, :, :].rearrange("(q p) n -> p q n", p=128)).then_inc(S["x_in"], 16)
            for layer in range(2):
                b = B_ATT[layer]
                wv, cv = (A["w_in_a"][0, :, :], 2048) if layer == 0 else (A["w_kv_shared"], 1024)
                wq, cq = (A["w_in_a"][0, :, :], 0) if layer == 0 else (A["w_q_b"][0, :, :], 0)
                wk, ck = (A["w_in_a"][0, :, :], 1024) if layer == 0 else (A["w_kv_shared"], 0)
                wo = A["w_out_a"][0, :, :] if layer == 0 else A["w_out_b"][0, :, :]
                for i in range(4):
                    load(b + i, w_row_tiles(wv, 2 * i, cols(cv, D)))
                for i in range(4):
                    load(b + 4 + 2 * i, w_cols(wq, cols(cq + 256 * i, 256)))
                    load(b + 5 + 2 * i, w_cols(wk, cols(ck + 256 * i, 256)))
                for i in range(4):
                    load(b + 12 + i, w_row_tiles(wo, 2 * i, cols(0, D)))
                b = B_MLP[layer]
                up = A["w_up"][layer, :, :].rearrange("(k p) n -> p k n", p=128)
                down = A["w_down"][layer, :, :]
                load(b, up[:, :, 0:256])
                with sp.Fori(0, (PAIRS - 1) // 3) as t:
                    for u in range(3):
                        for part in range(2):
                            o = 1 + 2 * u + part
                            sp.wait_ge(S["w_used"], t * 6 + (b + o - RING + 1))
                            s = slot(b + o)
                            if part == 0:
                                src = up[:, :, bass.ds(t * 768 + (u + 1) * 256, 256)]
                                dst = ring[:, s, :].rearrange("p (k n) -> p k n", k=8)
                            else:
                                src = down[bass.ds(t * 768 + u * 256, 256), :].rearrange("(k p) n -> p k n", p=128)
                                dst = ring[:, s, :].rearrange("p (k n) -> p k n", k=2)
                            sp.dma_start(dst, src).then_inc(w_full[s], 16)
                load(b + 31, down[15 * 256:16 * 256, :].rearrange("(k p) n -> p k n", p=128))
            w_in = A["w_in_2"][0, :, :]
            for i in range(4):
                load(B_C + i, w_row_tiles(w_in, 2 * i, cols(4096, 704)))
            for h in range(4):
                load(B_RQK + 2 * h, w_cols(w_in, cols(256 * h, 256)))
                load(B_RQK + 2 * h + 1, w_cols(w_in, cols(1024 + 256 * h, 256)))
            for i in range(3):
                w = A["w_uq_2"][0, i * 128:(i + 1) * 128, :].rearrange("p (h c) -> p h c", c=192)
                load(B_UQ + i, w[:, :, 0:128])
                for x in range(2):
                    sp.dma_start(ring[:, slot(B_UQ + i), 1024 + 256 * x:1280 + 256 * x]
                                 .rearrange("p (h c) -> p h c", h=8),
                                 w[:, :, 128 + 32 * x:160 + 32 * x]).then_inc(S["uqr_in"], 16)
            for i in range(2):
                load(B_UKV + i, A["w_ukv_2"][0, i * 128:(i + 1) * 128, :].rearrange("(k p) n -> p k n", k=1))
            for b, w, c in ((B_RV, w_in, 2048), (B_RG, w_in, 3072), (B_GR, w_in, 4800), (B_RO, A["w_ret_o_2"][0, :, :], 0),
                            (B_GM, w_in, 5824), (B_MO, A["w_mla_o_2"][0, :, :], 0), (B_WO, A["w_out_2"][0, :, :], 0)):
                for i in range(4):
                    load(b + i, w_row_tiles(w, 2 * i, cols(c, D)))
            w1 = A["w1_2"][0, :, :, :, :].rearrange("g e (k p) f -> (g e) p k f", p=128)
            w3 = A["w3_2"][0, :, :, :, :].rearrange("g e (k p) f -> (g e) p k f", p=128)
            w2 = A["w2_2"][0, :, :, :, :].rearrange("g e (k p) n -> (g e) p k n", p=128)
            parts = ((w1, 0), (w3, 0), (w1, 1), (w3, 1), (w2, 0), (w2, 1))
            for o, (w, e) in enumerate(parts):
                load(B_MOE + o, w[e, :, :, :])
            sp.wait_ge(S["trips_ready"], 1)
            steps = sp.value_load(trips[0:1, 0:1], min_val=STEPS, max_val=ROUNDS * STEPS)
            with sp.Fori(1, steps) as i:
                for o, (w, e) in enumerate(parts):
                    sp.wait_ge(S["w_used"], i * 6 + (B_MOE + o - RING + 1))
                    s = slot(B_MOE + o)
                    sp.dma_start(ring[:, s, :].rearrange("p (k n) -> p k n", k=2 if w is w2 else 8),
                                 w[bass.ds((i % STEPS) * 2 + e, 1), :, :, :].rearrange("o p k n -> p (o k) n"))\
                        .then_inc(w_full[s], 16)
            for q in range(QT):
                sp.wait_ge(S["out_ready"], q + 1)
                sp.dma_start(A["out"][0, q * 128:(q + 1) * 128, :], h_tm[:, q, :]).then_inc(S["out_stored"], 16)
            sp.wait_ge(S["out_stored"], 16 * QT)

        @block.gpsimd
        def _(pool):
            n = [0]

            def link(ins):
                n[0] += 1
                ins.then_inc(S["pool_chain"], 1)
                pool.wait_ge(S["pool_chain"], n[0])

            pool.memset(relb[:, :], NEG).then_inc(S["relb_set"], 1)
            pool.wait_ge(S["relb_set"], 1)
            pool.dma_start(relb[0:32, :], A["rel_bias"]).then_inc(S["relb_in"], 16)
            pool.dma_start(onehot, A["onehot"]).then_inc(S["onehot_in"], 16)
            pool.memset(vec_rows[:, :], 0.0).then_inc(S["vecrow_set"], 1)
            pool.wait_ge(S["vecrow_set"], 1)
            for name, (at, rows) in VEC.items():
                flat = A[name].rearrange("a (r n) -> (a r) n", n=128)
                pool.dma_start(vec_rows[at:at + rows, :], flat).then_inc(S["vec_in"], 16)
            pool.dma_start(lam_rows[:, :], bass.AP(A["lam_a"].tensor, 0, [[0, 128], [1, 256]])).then_inc(S["lam_in"], 16)
            pool.dma_start(brow[0:1, 0:4], A["b_grp_2"]).then_inc(S["small_in"], 16)
            pool.dma_start(brow[0:1, 4:36], A["b_exp_2"]).then_inc(S["small_in"], 16)
            pool.dma_start(w_rt[:, :, 0:4], A["w_grp_2"][0, :, :].rearrange("(k p) n -> p k n", p=128))\
                .then_inc(S["small_in"], 16)
            pool.dma_start(w_rt[:, :, 4:36], A["w_exp_2"][0, :, :].rearrange("(k p) n -> p k n", p=128))\
                .then_inc(S["small_in"], 16)
            link(pool.memset(mod[:, :], 0.0))
            pool.dma_start(mod[0:1, :], A["b_ada_2"]).then_inc(S["badd_in"], 16)
            pool.wait_ge(S["bias_copied"], 1)
            pool.dma_start(A["bias_dram"], bias_rows[:, :].unsqueeze(1).to_broadcast([16, 128, 512]))\
                .then_inc(S["bias_dram"], 16)
            pool.wait_ge(S["bias_dram"], 16)
            t = A["bias_dram"].tensor
            pool.dma_start(bias[:, :, 0:128], bass.AP(t, 255, [[511, 128], [128 * 512, 16], [1, 128]]))\
                .then_inc(S["bias_in"], 16)
            pool.dma_start(bias[:, :, 128:384], bass.AP(t, 127, [[511, 128], [128 * 512, 16], [1, 256]]))\
                .then_inc(S["bias_in"], 16)

            pool.wait_ge(S["c_silu"], 1)
            pool.wait_ge(S["badd_in"], 16)

            def ada(k0, k1):
                for k in range(k0, k1):
                    for j in range(6):
                        i = 6 * k + j
                        s = i % 2
                        if i == 0:
                            fetch(0)
                        if i + 1 < 48:
                            fetch(i + 1)
                        pool.wait_ge(ada_full[s], 16 * (i // 2 + 1))
                        link(pool.tensor_scalar(stage[:, s, :], stage[:, s, :], act_c[:, k:k + 1], None, ALU.mult))
                        part = mod[:, j * 1024:(j + 1) * 1024]
                        last = pool.tensor_tensor(part, part, stage[:, s, :], ALU.add)
                        if i == 47:
                            last.then_inc(S["ada_done"], 1)
                        else:
                            link(last)

            def fetch(i):
                k, j = divmod(i, 6)
                pool.dma_start(stage[:, i % 2, :], A["w_ada_2"][0, k * 128:(k + 1) * 128, j * 1024:(j + 1) * 1024])\
                    .then_inc(ada_full[i % 2], 16)

            def rows(src_g, src_b, i, width=1024):
                pool.dma_start(rows_g[:, :], bass.AP(src_g.tensor, i * 1024, [[0, 128], [1, 1024]]))\
                    .then_inc(S["rowsg_in"], 16)
                pool.dma_start(rows_b[:, :], bass.AP(src_b.tensor, i * 1024, [[0, 128], [1, 1024]]))\
                    .then_inc(S["rowsb_in"], 16)

            def residual(i):
                pool.wait_ge(S["rowsg_in"], 16 * (i + 1))
                pool.wait_ge(S["rowsb_in"], 16 * (i + 1))
                for q in range(QT):
                    pool.wait_ge(S["ln_out"], QT * i + q + 1)
                    link(pool.tensor_tensor(h_tm[:, q, :], o_tm[:, q, :], rows_g[:, :], ALU.mult))
                    last = pool.tensor_tensor(h_tm[:, q, :], h_tm[:, q, :], rows_b[:, :], ALU.add)
                    if q == 0:
                        link(last)
                last.then_inc(S["h_done"], 1)
                pool.wait_ge(S["h_done"], i + 1)

            rows(A["ln1_g"], A["ln1_b"], 0)
            ada(0, 2)
            residual(0)
            rows(A["ln2_g"], A["ln2_b"], 0)
            ada(2, 5)
            residual(1)
            rows(A["ln1_g"], A["ln1_b"], 1)
            ada(5, 8)
            residual(2)
            rows(A["ln2_g"], A["ln2_b"], 1)
            pool.wait_ge(S["h_done"], 4)
            pool.dma_start(rows_g[:, :], bass.AP(A["norm2_2"].tensor, 0, [[0, 128], [1, 1024]]))\
                .then_inc(S["rowsg_in"], 16)
            pool.dma_start(rows_b[:, :], bass.AP(A["final_norm_2"].tensor, 0, [[0, 128], [1, 1024]]))\
                .then_inc(S["rowsb_in"], 16)

        @block.tensor
        def _(pe):
            groups = [0]

            def transposes(items):
                g = groups[0]
                groups[0] += 1
                if g >= 2:
                    pe.wait_ge(S["tp_done"], g - 1)
                for off, src in items:
                    last = pe.transpose(tp[:, g % 2, off:off + 128], src, ident)
                last.then_inc(S["tp_ready"], 1)

            def to_feature_major(src):
                for q in range(QT):
                    for half in range(2):
                        transposes([(128 * j, src[:, q, (4 * half + j) * 128:(4 * half + j + 1) * 128])
                                    for j in range(4)])

            def transposed():
                pe.wait_ge(S["tp_done"], groups[0])

            def arrive(b):
                pe.wait_ge(w_full[slot(b)], 16 * (b // RING + 1))

            def tokens_out(b, lhs):
                for i in range(4):
                    arrive(b + i)
                    for k in range(2):
                        kt = 2 * i + k
                        for q in range(QT):
                            for half in range(2):
                                at = 1024 * k + 512 * half
                                last = pe.matmul(acc[:, 2 * q + half, :], lhs[:, kt, q * 128:(q + 1) * 128],
                                                 ring[:, slot(b + i), at:at + 512], start=(kt == 0), stop=(kt == 7))
                    last.then_inc(S["w_used"], 1)

            def features_out(b, bank):
                arrive(b)
                for c in range(2):
                    for kt in range(KT):
                        at = 256 * kt + 128 * c
                        last = pe.matmul(bank[:, 256 * c:256 * c + 256], ring[:, slot(b), at:at + 128],
                                         x_t[:, kt, :], start=(kt == 0), stop=(kt == KT - 1))
                last.then_inc(S["w_used"], 1)

            def scores(n, c):
                pe.wait_ge(S["q_done"], n // 2 + 1)
                pe.wait_ge(S["k_done"], n // 2 + 1)
                if n % 8 >= 2:
                    pe.wait_ge(S["o_done"], n - 1)
                for m in range(2):
                    p = slice(64 * m, 64 * m + 64)
                    bank = acc[:, 2 * (c % 2) + m, :]
                    pe.matmul(bank[:, 0:128], q_t[p, c, 0:128], k_t[p, c, 0:128], start=True, stop=True)
                    last = pe.matmul(bank[:, 128:384], q_t[p, c, 128:256], k_t[p, c, :], start=True, stop=True)
                last.then_inc(S["sc_ready"], 1)

            def att_out(layer, n, c):
                pe.wait_ge(S["attw_ready"], n + 1)
                maps = (0,) if layer == 0 else (0, 1)
                for m in maps:
                    transposes([(128 * j, prob[:, c % 2, m, 128 * j:128 * j + 128]) for j in range(3)])
                transposed()
                pe.wait_ge(S["v_done"], layer + 1)
                for m in maps:
                    w = 128 if layer == 0 else 64
                    cols = slice(128 * c + w * m, 128 * c + w * m + w)
                    for q in range(QT):
                        out = acc[:, 2 * (c % 2) + q, 384 + w * m:384 + w * m + w]
                        for kb in range(q + 1):
                            j = 0 if q == 0 else 1 + kb
                            last = pe.matmul(out, prob_t[:, c % 2, m, 128 * j:128 * j + 128], v_tm[:, kb, cols],
                                             start=(kb == 0), stop=(kb == q))
                last.then_inc(S["o_ready"], 1)

            def attention(layer):
                b = B_ATT[layer]
                tokens_out(b, x_t)
                pe.wait_ge(S["v_done"], layer + 1)

                def queries(i):
                    if layer + i:
                        pe.wait_ge(S["q_done"], 4 * layer + i)
                    features_out(b + 4 + 2 * i, pp[:, 0, :])

                def keys(i):
                    if layer + i:
                        pe.wait_ge(S["k_done"], 4 * layer + i)
                    features_out(b + 5 + 2 * i, pp[:, 1, :])

                n = 8 * layer
                queries(0)
                keys(0)
                for i in range(1, 4):
                    queries(i)
                    scores(n + 2 * i - 2, 2 * i - 2)
                    if i >= 2:
                        att_out(layer, n + 2 * i - 3, 2 * i - 3)
                    scores(n + 2 * i - 1, 2 * i - 1)
                    keys(i)
                    att_out(layer, n + 2 * i - 2, 2 * i - 2)
                scores(n + 6, 6)
                att_out(layer, n + 5, 5)
                scores(n + 7, 7)
                att_out(layer, n + 6, 6)
                att_out(layer, n + 7, 7)
                if layer == 0:
                    for q in range(QT):
                        pe.wait_ge(S["o_scaled"], q + 1)
                        for half in range(2):
                            transposes([(128 * j, o_tm[:, q, (4 * half + j) * 128:(4 * half + j + 1) * 128])
                                        for j in range(4)])
                else:
                    pe.wait_ge(S["o_done"], 16)
                    to_feature_major(o_tm)
                transposed()
                tokens_out(b + 12, q_t)

            def norm_transposes(i):
                for q in range(QT):
                    pe.wait_ge(S["ln_out"], QT * i + q + 1)
                    for half in range(2):
                        transposes([(128 * j, o_tm[:, q, (4 * half + j) * 128:(4 * half + j + 1) * 128])
                                    for j in range(4)])
                transposed()

            def mlp(layer):
                b = B_MLP[layer]
                banks = (pp[:, 0, :], pp[:, 1, :], tp[:, 0, :])

                def up(o, v, t=None):
                    s = slot(b + o)
                    full, j = 16 * ((b + o) // RING + 1), PAIRS * layer + v
                    pe.wait_ge(w_full[s], full if t is None else t * 16 + full)
                    if v >= 3 or t is not None:
                        pe.wait_ge(S["relu_done"], j - 2 if t is None else t * 3 + (j - 2))
                    for c in range(2):
                        for kt in range(KT):
                            at = 256 * kt + 128 * c
                            last = pe.matmul(banks[v % 3][:, 256 * c:256 * c + 256], ring[:, s, at:at + 128],
                                             x_t[:, kt, :], start=(kt == 0), stop=(kt == KT - 1))
                    last.then_inc(S["w_used"], 1)

                def down(o, v, t=None, first=False, final=False):
                    s = slot(b + o)
                    full, j = 16 * ((b + o) // RING + 1), PAIRS * layer + v
                    pe.wait_ge(w_full[s], full if t is None else t * 16 + full)
                    pe.wait_ge(S["hid_ready"], j + 1 if t is None else t * 3 + (j + 1))
                    for f in range(2):
                        for q in range(QT):
                            for half in range(2):
                                at = 1024 * f + 512 * half
                                last = pe.matmul(acc[:, 2 * q + half, :], hid[:, v % 3, f, q * 128:(q + 1) * 128],
                                                 ring[:, s, at:at + 512], start=(first and f == 0),
                                                 stop=(final and f == 1))
                    last.then_inc(S["w_used"], 1)

                up(0, 0)
                up(1, 1)
                pe.wait_ge(S["acc_taken"], 2 * layer + 1)
                down(2, 0, first=True)
                up(3, 2)
                down(4, 1)
                up(5, 3)
                down(6, 2)
                with pe.Fori(0, 4) as t:
                    for u in range(3):
                        up(7 + 2 * u, 4 + u, t)
                        down(8 + 2 * u, 3 + u, t, final=False)
                down(31, 15, final=True)

            pe.wait_ge(S["consts_in"], 16)
            pe.wait_ge(S["relb_in"], 16)
            pe.wait_ge(S["onehot_in"], 16)
            pe.matmul(pp[0:16, 0, :], relb[:, :], onehot, start=True, stop=True).then_inc(S["bias_mm"], 1)
            pe.wait_ge(S["vec_in"], 16 * len(VEC))
            pe.transpose(pp[:, 1, 0:128], vec_rows[:, :], ident).then_inc(S["vec_mm"], 1)
            pe.wait_ge(S["x_in"], 16)
            to_feature_major(h_tm)
            transposed()
            pe.wait_ge(S["vec_done"], 1)
            pe.wait_ge(S["bias_copied"], 1)

            for layer in range(2):
                attention(layer)
                norm_transposes(2 * layer)
                mlp(layer)
                if layer == 0:
                    norm_transposes(1)

            pe.wait_ge(S["ada_done"], 1)
            pe.wait_ge(S["relu_done"], 2 * PAIRS)
            for i, part in enumerate((0, 1, 3, 4)):
                for j in range(8):
                    at = 1024 * part + 128 * j
                    last = pe.matmul(pp[:, 0, 8 * i + j:8 * i + j + 1], mod[:, at:at + 128],
                                     con("ones")[:, 0:1], start=True, stop=True)
            last.then_inc(S["mod_mm"], 1)
            for i in range(8):
                part, half = divmod(i, 2)
                at = 1024 * (2, 3, 4, 5)[part] + 512 * half
                if i >= 1:
                    pe.wait_ge(S["mod_done"], i)
                pe.matmul(pp[:, 1, :], con("ones"), mod[:, at:at + 512], start=True, stop=True)\
                    .then_inc(S["mod_mm"], 1)
            pe.wait_ge(S["mod_done"], 8)

            for q in range(QT):
                pe.wait_ge(S["r_out"], q + 1)
                for half in range(2):
                    transposes([(128 * j, o_tm[:, q, (4 * half + j) * 128:(4 * half + j + 1) * 128])
                                for j in range(4)])
            transposed()
            for i in range(4):
                arrive(B_C + i)
                for k in range(2):
                    kt = 2 * i + k
                    w = ring[:, slot(B_C + i), 704 * k:704 * k + 704]
                    for q in range(QT):
                        lhs = x_t[:, kt, q * 128:(q + 1) * 128]
                        pe.matmul(acc[:, 2 * q, 0:384], lhs, w[:, 0:384], start=(kt == 0), stop=(kt == 7))
                        last = pe.matmul(acc[:, 2 * q + 1, 0:320], lhs, w[:, 384:704], start=(kt == 0), stop=(kt == 7))
                last.then_inc(S["w_used"], 1)
            for h in range(4):
                if h:
                    pe.wait_ge(S["rq_done"], h)
                features_out(B_RQK + 2 * h, pp[:, 0, :])
                if h:
                    pe.wait_ge(S["rk_done"], h)
                features_out(B_RQK + 2 * h + 1, pp[:, 1, :])
            for q in range(QT):
                pe.wait_ge(S["lat_done"], q + 1)
                transposes([(128 * j, lat[:, q, 128 * j:128 * j + 128]) for j in range(3)])
                transposes([(128 * j, lat[:, q, 384 + 128 * j:512 + 128 * j]) for j in range(4)])
            transposed()
            pe.wait_ge(S["rq_done"], 4)
            pe.wait_ge(S["rk_done"], 4)
            for i in range(3):
                arrive(B_UQ + i)
            pe.wait_ge(S["uqr_in"], 16 * 6)
            n = 0

            def uq_bank():
                if n >= 2:
                    pe.wait_ge(S["uq_done"], n - 1)
                return pp[:, n % 2, :]

            for pair in range(6):
                bank = uq_bank()
                for c in range(2):
                    for kt in range(3):
                        at = 128 * (2 * pair + c) if pair < 4 else 1024 + 256 * c + 128 * (pair - 4)
                        lhs = ring[:, slot(B_UQ + kt), at:at + 128]
                        last = pe.matmul(bank[:, 256 * c:256 * c + 256], lhs, lat_t[:, kt, :],
                                         start=(kt == 0), stop=(kt == 2))
                last.then_inc(S["uq_ready"], 1)
                n += 1
            arrive(B_UKV)
            arrive(B_UKV + 1)
            for pair in range(4):
                bank = uq_bank()
                for c in range(2):
                    for kt in range(2):
                        at = 256 * (2 * pair + c)
                        last = pe.matmul(bank[:, 256 * c:256 * c + 256], ring[:, slot(B_UKV + kt), at:at + 128],
                                         lat_t[:, 3 + kt, :], start=(kt == 0), stop=(kt == 1))
                    if pair == 0 and c == 0:
                        last.then_inc(S["w_used"], 3)
                last.then_inc(S["uq_ready"], 1)
                n += 1
            for kt in range(2):
                w = ring[:, slot(B_UKV + kt), :].rearrange("p (h c) -> p h c", c=256)
                for q in range(QT):
                    for half in range(2):
                        last = pe.matmul(acc[:, 2 * q + half, :], lat_t[:, 3 + kt, q * 128:(q + 1) * 128],
                                         w[:, 4 * half:4 * half + 4, 128:256], start=(kt == 0), stop=(kt == 1))
            last.then_inc(S["w_used"], 2)
            pe.wait_ge(S["vmla_done"], 1)
            tokens_out(B_RV, x_t)
            pe.wait_ge(S["rv_done"], 1)
            for h in range(4):
                bank = acc[:, h, :]
                for c in range(2):
                    pe.matmul(bank[:, 0:256], k_t[:, 2 * h + c, 0:128], q_t[:, 2 * h + c, :],
                              start=(c == 0), stop=(c == 1))
                for c in range(2):
                    last = pe.matmul(bank[:, 256:384], k_t[:, 2 * h + c, 128:256], q_t[:, 2 * h + c, 128:256],
                                     start=(c == 0), stop=(c == 1))
                last.then_inc(S["sret_ready"], 1)
            for h in range(4):
                pe.wait_ge(S["st_ready"], h + 1)
                cols = slice(256 * h, 256 * h + 256)
                pe.matmul(acc[:, h, 0:256], st_ret[:, h, 0:128], v_tm[:, 0, cols], start=True, stop=True)
                pe.matmul(acc[:, h, 256:512], st_ret[:, h, 128:256], v_tm[:, 0, cols], start=True, stop=False)
                pe.matmul(acc[:, h, 256:512], st_ret[:, h, 256:384], v_tm[:, 1, cols], start=False, stop=True)\
                    .then_inc(S["y_ready"], 1)
            pe.wait_ge(S["y_done"], 4)
            pe.wait_ge(S["uq_done"], 10)

            def mla_scores(c):
                if c >= 2:
                    pe.wait_ge(S["attw_ready"], 16 + c - 1)
                for m in range(2):
                    hd = 2 * c + m
                    a, p = hd // 4, slice(32 * (hd % 4), 32 * (hd % 4) + 32)
                    bank = acc[:, 2 * (c % 2) + m, :]
                    for q in range(QT):
                        out = bank[:, 0:128] if q == 0 else bank[:, 128:384]
                        keys = slice(0, 128 * (q + 1))
                        tok = slice(128 * q, 128 * q + 128)
                        pe.matmul(out, qn_t[:, hd, tok], kn_t[:, hd, keys], start=True, stop=False)
                        pe.matmul(out, pe_rope[p, 2 * a, tok], pe_rope[p, 4, keys], start=False, stop=False)
                        last = pe.matmul(out, pe_rope[p, 2 * a + 1, tok], pe_rope[p, 5, keys],
                                         start=False, stop=True)
                last.then_inc(S["sc_ready"], 1)

            def mla_out(c):
                pe.wait_ge(S["attw_ready"], 16 + c + 1)
                for m in range(2):
                    transposes([(128 * j, prob[:, c % 2, m, 128 * j:128 * j + 128]) for j in range(3)])
                transposed()
                if c >= 2:
                    pe.wait_ge(S["o_done"], 16 + c - 1)
                for q in range(QT):
                    for m in range(2):
                        hd = 2 * c + m
                        out = pp[:, c % 2, 256 * q + 128 * m:256 * q + 128 * m + 128]
                        for kb in range(q + 1):
                            j = 0 if q == 0 else 1 + kb
                            last = pe.matmul(out, prob_t[:, c % 2, m, 128 * j:128 * j + 128],
                                             v_mla[:, kb, 128 * hd:128 * hd + 128], start=(kb == 0), stop=(kb == q))
                last.then_inc(S["o_ready"], 1)

            mla_scores(0)
            mla_scores(1)
            mla_out(0)
            mla_scores(2)
            mla_out(1)
            mla_scores(3)
            mla_out(2)
            mla_out(3)
            tokens_out(B_RG, x_t)
            pe.wait_ge(S["rg_done"], 1)
            tokens_out(B_GR, x_t)
            pe.wait_ge(S["yret_ready"], 1)
            to_feature_major(o_tm)
            transposed()
            pe.wait_ge(S["gr_done"], 1)
            tokens_out(B_RO, q_t)
            pe.wait_ge(S["o_done"], 20)
            to_feature_major(o_mla)
            transposed()
            pe.wait_ge(S["ret_merged"], 1)
            tokens_out(B_GM, x_t)
            pe.wait_ge(S["gm_done"], 1)
            tokens_out(B_MO, q_t)
            pe.wait_ge(S["mla_merged"], 1)
            to_feature_major(merged)
            transposed()
            tokens_out(B_WO, q_t)

            for q in range(QT):
                pe.wait_ge(S["r_out"], 2 + q + 1)
                for half in range(2):
                    transposes([(128 * j, o_tm[:, q, (4 * half + j) * 128:(4 * half + j + 1) * 128])
                                for j in range(4)])
            transposed()
            pe.wait_ge(S["small_in"], 64)
            for q in range(QT):
                for kt in range(KT):
                    pe.matmul(pp[:, q, 0:36], q_t[:, kt, q * 128:(q + 1) * 128], w_rt[:, kt, :],
                              start=(kt == 0), stop=False)
                last = pe.matmul(pp[:, q, 0:36], con("ones", 1), brow[0:1, 0:36], start=False, stop=True)
            last.then_inc(S["lg_ready"], 1)
            pe.wait_ge(S["mask_ready"], 1)
            pe.matmul(pp[:, 0, 0:32], con("tri"), picked[:, 0, :], start=True, stop=True)
            pe.matmul(pp[:, 0, 32:64], con("ones"), picked[:, 0, :], start=True, stop=False)
            pe.matmul(pp[:, 0, 32:64], con("tri"), picked[:, 1, :], start=False, stop=True)
            pe.matmul(pp[:, 0, 64:96], con("ones"), picked[:, 0, :], start=True, stop=False)
            pe.matmul(pp[:, 0, 64:96], con("ones"), picked[:, 1, :], start=False, stop=True).then_inc(S["pos_ready"], 1)

            def gather():
                for g in range(2):
                    for j in range(4):
                        f = 4 * g + j
                        for q in range(QT):
                            last = pe.matmul(tp[:, g, 128 * j:128 * j + 128], o_tm[:, q, 128 * f:128 * f + 128],
                                             sel[:, q, :], start=(q == 0), stop=(q == 1))
                last.then_inc(S["xe_ready"], 1)

            pe.wait_ge(S["sel_ready"], 1)
            gather()
            pe.wait_ge(S["trips_ready"], 1)
            steps = pe.value_load(trips[0:1, 0:1], min_val=STEPS, max_val=ROUNDS * STEPS)
            s0 = [slot(B_MOE + o) for o in range(6)]
            full0 = [16 * ((B_MOE + o) // RING + 1) for o in range(6)]
            with pe.Fori(0, steps) as i:
                for e in range(2):
                    for w in range(2):
                        o = 2 * e + w
                        pe.wait_ge(w_full[s0[o]], i * 16 + full0[o])
                        if e == 0 and w == 0:
                            pe.wait_ge(S["xe_done"], i + 1)
                        for f in range(2):
                            out = up_bank[e][:, 128 * w + 64 * f:128 * w + 64 * f + 64]
                            for kt in range(KT):
                                at = 256 * kt + 128 * f
                                last = pe.matmul(out, ring[:, s0[o], at:at + 128], xe[:, kt, 64 * e:64 * e + 64],
                                                 start=(kt == 0), stop=(kt == KT - 1))
                        last.then_inc(S["w_used"], 1)
                pe.wait_ge(S["sel_ready"], i + 2)
                gather()
                pe.wait_ge(S["cmb_done"], i * 4 + 4)
                pe.wait_ge(S["hid_e"], i * 2 + 2)
                for q in range(QT):
                    last = pe.transpose(acc[:, 2, 128 * q:128 * q + 128], gsel[:, q, :], ident)
                last.then_inc(S["gt_ready"], 1)
                for half in range(2):
                    for e in range(2):
                        if half == 0:
                            pe.wait_ge(w_full[s0[4 + e]], i * 16 + full0[4 + e])
                            pe.wait_ge(S["hid_e"], i * 2 + (e + 1))
                        for f in range(2):
                            out = (pp[:, 1, :], acc[:, 3, :])[half]
                            at = 1024 * f + 512 * half
                            last = pe.matmul(out[64 * e:64 * e + 64, :], hid_x[:, e, f, :],
                                             ring[:, s0[4 + e], at:at + 512], start=(f == 0), stop=(f == 1))
                        if half == 1:
                            last.then_inc(S["w_used"], 1)
                    if half == 0:
                        last.then_inc(S["y_half"], 1)
                pe.wait_ge(S["gt_done"], i + 1)
                for half in range(2):
                    pe.wait_ge(S["ysb_half"], i * 2 + (half + 1))
                    for q in range(QT):
                        if half == 1:
                            pe.wait_ge(S["cmb_done"], i * 4 + (4 + q + 1))
                        pe.matmul(acc[:, q, :], gsel_t[:, q, :], ysb[:, 512 * half:512 * half + 512],
                                  start=True, stop=True).then_inc(S["cmb_ready"], 1)

        @block.scalar
        def _(act):
            groups = [0]

            def copied(dsts, scales=None, shifts=None):
                g = groups[0]
                groups[0] += 1
                act.wait_ge(S["tp_ready"], g + 1)
                off = 0
                for i, dst in enumerate(dsts):
                    n = dst.shape[1] if len(dst.shape) == 2 else dst.shape[1] * dst.shape[2]
                    src = tp[:, g % 2, off:off + n]
                    if len(dst.shape) == 3:
                        src = src.rearrange("p (a b) -> p a b", a=dst.shape[1])
                    if scales is None:
                        last = act.activation(dst, src, ACT.Copy)
                    elif shifts is None:
                        last = act.activation(dst, src, ACT.Identity, scale=scales[i])
                    else:
                        last = act.activation(dst, src, ACT.Identity, scale=scales[i], bias=shifts[i])
                    off += n
                last.then_inc(S["tp_done"], 1)

            def to_feature_major(dst, scale=None, shift=None, fast=True):
                for q in range(QT):
                    for half in range(2):
                        fs = range(4 * half, 4 * half + 4)
                        if scale is None:
                            copied([dst[:, 4 * half:4 * half + 4, q * 128:(q + 1) * 128]])
                        else:
                            copied([dst[:, f, q * 128:(q + 1) * 128] for f in fs], [scale(f) for f in fs],
                                   None if shift is None else [shift(f) for f in fs])

            def column(name, i=0):
                at = VEC[name][0] + i
                return vec[:, at:at + 1]

            def used(b):
                act.wait_ge(S["w_used"], b + 1)

            act.wait_ge(S["bias_mm"], 1)
            act.activation(bias_rows[:, :], pp[0:16, 0, :], ACT.Copy).then_inc(S["bias_copied"], 1)
            act.wait_ge(S["vec_mm"], 1)
            act.activation(vec[:, :], pp[:, 1, 0:128], ACT.Copy).then_inc(S["vec_done"], 1)
            to_feature_major(x_t)
            act.wait_ge(S["vec_done"], 1)
            at = VEC["c_2"][0]
            act.activation(act_c[:, :], vec[:, at:at + 8], ACT.Silu).then_inc(S["c_silu"], 1)
            act.wait_ge(S["lam_ready"], 1)
            act.activation(lam_s[:, 2:4], lam_s[:, 0:2], ACT.Exp).then_inc(S["lam_exp"], 1)

            def exps(n, b):
                act.wait_ge(S["nmax_ready"], n + 1)
                for m in range(2):
                    for q in range(QT):
                        cols = slice(0, 128) if q == 0 else slice(128, 384)
                        last = act.activation(prob[:, b, m, cols], prob[:, b, m, cols], ACT.Exp,
                                              bias=nmax[:, b, 2 * q + m:2 * q + m + 1],
                                              accum_out=esum[:, b, 2 * q + m:2 * q + m + 1])
                last.then_inc(S["exp_done"], 1)

            def attention(layer):
                b = B_ATT[layer]
                used(b + 3)
                act.activation(v_tm[:, 0, :], acc[:, 0:2, :].rearrange("p a b -> p (a b)"), ACT.Copy)
                act.activation(v_tm[:, 1, :], acc[:, 2:4, :].rearrange("p a b -> p (a b)"), ACT.Copy)\
                    .then_inc(S["v_done"], 1)

                def queries(i):
                    used(b + 4 + 2 * i)
                    act.activation(q_t[:, 2 * i:2 * i + 2, :].rearrange("p a b -> p (a b)"), pp[:, 0, :], ACT.Copy)\
                        .then_inc(S["q_done"], 1)

                def out(c):
                    for m in range(1 if layer == 0 else 2):
                        copied([prob_t[:, c % 2, m, :]])
                    if layer == 0:
                        act.wait_ge(S["o_ready"], c + 1)
                        act.activation(o_tm[:, :, 128 * c:128 * c + 128],
                                       acc[:, 2 * (c % 2):2 * (c % 2) + 2, 384:512], ACT.Copy).then_inc(S["o_done"], 1)

                n = 8 * layer
                queries(0)
                for i in range(1, 4):
                    queries(i)
                    exps(n + 2 * i - 2, 0)
                    if i >= 2:
                        out(2 * i - 3)
                    exps(n + 2 * i - 1, 1)
                    out(2 * i - 2)
                exps(n + 6, 0)
                out(5)
                exps(n + 7, 1)
                out(6)
                out(7)
                if layer == 0:
                    for q in range(QT):
                        act.wait_ge(S["osq_ready"], q + 1)
                        act.activation(rstd[:, :], sr[:, :], ACT.Sqrt).then_inc(S["osq_rstd"], 1)
                    to_feature_major(q_t, scale=lambda f: lam_s[:, 1:2])
                else:
                    to_feature_major(q_t)

            def norm_root(i):
                for q in range(QT):
                    act.wait_ge(S["ln_stat"], QT * i + q + 1)
                    act.activation(rstd[:, q:q + 1], sr[:, q:q + 1], ACT.Sqrt).then_inc(S["ln_rstd"], 1)

            def mlp(layer):
                banks = (pp[:, 0, :], pp[:, 1, :], tp[:, 0, :])
                b = B_MLP[layer]

                def step(o, v, t=None):
                    j = PAIRS * layer + v
                    act.wait_ge(S["w_used"], b + o + 1 if t is None else t * 6 + (b + o + 1))
                    if v >= 3 or layer:
                        act.wait_ge(S["hid_ready"], j - 2 if t is None else t * 3 + (j - 2))
                    act.activation(relu[:, v % 3, :], banks[v % 3], ACT.Relu).then_inc(S["relu_done"], 1)

                step(0, 0)
                step(1, 1)
                step(3, 2)
                step(5, 3)
                with act.Fori(0, 4) as t:
                    for u in range(3):
                        step(7 + 2 * u, 4 + u, t)

            for layer in range(2):
                attention(layer)
                norm_root(2 * layer)
                to_feature_major(x_t, lambda f: column("ln1_g", 8 * layer + f), lambda f: column("ln1_b", 8 * layer + f))
                mlp(layer)
                norm_root(2 * layer + 1)
                if layer == 0:
                    to_feature_major(x_t, lambda f: column("ln2_g", f), lambda f: column("ln2_b", f))

            for i in range(8):
                part, half = divmod(i, 2)
                at = 1024 * (2, 3, 4, 5)[part] + 512 * half
                act.wait_ge(S["mod_mm"], i + 2)
                act.activation(mod[:, at:at + 512], pp[:, 1, :], ACT.Copy).then_inc(S["mod_done"], 1)
            for q in range(QT):
                act.wait_ge(S["r_stat"], q + 1)
                act.activation(rstd[:, q:q + 1], sr[:, q:q + 1], ACT.Sqrt).then_inc(S["r_rstd"], 1)
            act.wait_ge(S["modc_done"], 1)
            to_feature_major(x_t, lambda f: modc[:, 1, f:f + 1], lambda f: modc[:, 0, f:f + 1])
            used(B_C + 3)
            for q in range(QT):
                act.activation(lat[:, q, 0:384], acc[:, 2 * q, 0:384], ACT.Copy)
                act.activation(lat[:, q, 384:640], acc[:, 2 * q + 1, 0:256], ACT.Copy)
                for x in range(2):
                    last = act.activation(lat[:, q, 640 + 128 * x:768 + 128 * x].rearrange("p (r c) -> p r c", r=4),
                                          acc[:, 2 * q + 1, 256 + 32 * x:288 + 32 * x].unsqueeze(1)
                                          .to_broadcast([128, 4, 32]), ACT.Copy)
            last.then_inc(S["lat_copied"], 1)
            act.wait_ge(S["lat_stat"], 1)
            act.activation(rstd[:, 0:4], sr[:, 0:4], ACT.Sqrt).then_inc(S["lat_rstd"], 1)
            for q in range(QT):
                tok = slice(q * 128, (q + 1) * 128)
                copied([lat_t[:, j, tok] for j in range(3)], [column("q_norm_2", j) for j in range(3)])
                copied([lat_t[:, 3 + j, tok] for j in range(2)] + [pe_rope[:, 4 + x, tok] for x in range(2)],
                       [column("kv_norm_2", j) for j in range(2)] + [1.0, 1.0])
            assert groups[0] == TP_LATENTS
            for pair in range(4):
                act.wait_ge(S["uq_ready"], pair + 1)
                act.activation(qn_t[:, 2 * pair:2 * pair + 2, :].rearrange("p a b -> p (a b)"), pp[:, pair % 2, :],
                               ACT.Copy).then_inc(S["uq_done"], 1)
            act.wait_ge(S["uq_done"], 6)
            for pair in range(4):
                act.wait_ge(S["uq_ready"], 6 + pair + 1)
                act.activation(kn_t[:, 2 * pair:2 * pair + 2, :].rearrange("p a b -> p (a b)"), pp[:, pair % 2, :],
                               ACT.Copy).then_inc(S["uq_done"], 1)
            used(B_UKV + 1)
            act.activation(v_mla[:, :, :].rearrange("p a b -> p (a b)"), acc[:, :, :].rearrange("p a b -> p (a b)"),
                           ACT.Copy).then_inc(S["vmla_done"], 1)
            used(B_RV + 3)
            act.activation(v_tm[:, :, :].rearrange("p a b -> p (a b)"), acc[:, :, :].rearrange("p a b -> p (a b)"),
                           ACT.Copy).then_inc(S["rv_done"], 1)
            for h in range(4):
                act.wait_ge(S["y_ready"], h + 1)
                act.activation(o_tm[:, :, 256 * h:256 * h + 256], acc[:, h, :].rearrange("p (a b) -> p a b", a=2),
                               ACT.Copy).then_inc(S["y_done"], 1)
            exps(16, 0)
            exps(17, 1)

            def mla_out(c):
                copied([prob_t[:, c % 2, 0, :]])
                copied([prob_t[:, c % 2, 1, :]])

            mla_out(0)
            exps(18, 0)
            mla_out(1)
            exps(19, 1)
            mla_out(2)
            mla_out(3)
            act.wait_ge(S["hn_stat"], 1)
            act.activation(rstd[:, :], sr[:, :], ACT.Sqrt).then_inc(S["hn_rstd"], 1)
            flat = acc[:, :, :].rearrange("p a b -> p (a b)")
            used(B_RG + 3)
            act.activation(rg[:, :, :].rearrange("p a b -> p (a b)"), flat, ACT.Silu).then_inc(S["rg_done"], 1)
            used(B_GR + 3)
            act.activation(gate[:, :, :].rearrange("p a b -> p (a b)"), flat, ACT.Sigmoid).then_inc(S["gr_done"], 1)
            to_feature_major(q_t)
            used(B_RO + 3)
            to_feature_major(q_t)
            used(B_GM + 3)
            act.activation(gate[:, :, :].rearrange("p a b -> p (a b)"), flat, ACT.Sigmoid).then_inc(S["gm_done"], 1)
            used(B_MO + 3)
            to_feature_major(q_t)
            for q in range(QT):
                act.wait_ge(S["r_stat"], 2 + q + 1)
                act.activation(rstd[:, q:q + 1], sr[:, q:q + 1], ACT.Sqrt).then_inc(S["r_rstd"], 1)
            to_feature_major(q_t)
            act.wait_ge(S["lg_max"], 1)
            for q in range(QT):
                last = act.activation(route[:, q, 40:44], route[:, q, 0:4], ACT.Exp, bias=route[:, q, 36:37],
                                      accum_out=route[:, q, 37:38])
            last.then_inc(S["lg_exp"], 1)
            act.wait_ge(S["lg_m2"], 1)
            for q in range(QT):
                last = act.activation(route[:, q, 39:40], route[:, q, 38:39], ACT.Exp)
            last.then_inc(S["lg_e2"], 1)
            act.wait_ge(S["trips_ready"], 1)
            steps = act.value_load(trips[0:1, 0:1], min_val=STEPS, max_val=ROUNDS * STEPS)

            def take_gathered():
                for g in range(2):
                    last = act.activation(xe[:, 4 * g:4 * g + 4, :].rearrange("p a b -> p (a b)"), tp[:, g, :],
                                          ACT.Copy)
                last.then_inc(S["xe_done"], 1)

            act.wait_ge(S["xe_ready"], 1)
            take_gathered()
            with act.Fori(0, steps) as i:
                for e in range(2):
                    act.wait_ge(S["w_used"], i * 6 + (B_MOE + 2 * e + 2))
                    act.activation(silu_a[:, e, :], up_bank[e][:, 0:128], ACT.Silu).then_inc(S["silu_e"], 1)
                act.wait_ge(S["xe_ready"], i + 2)
                take_gathered()
                act.wait_ge(S["gt_ready"], i + 1)
                act.activation(gsel_t[:, :, :].rearrange("p a b -> p (a b)"), acc[:, 2, 0:256], ACT.Copy)\
                    .then_inc(S["gt_done"], 1)
                act.wait_ge(S["y_half"], i + 1)
                act.activation(ysb[:, 0:512], pp[:, 1, :], ACT.Copy).then_inc(S["ysb_half"], 1)
                act.wait_ge(S["w_used"], i * 6 + (B_MOE + 6))
                act.activation(ysb[:, 512:1024], acc[:, 3, :], ACT.Copy).then_inc(S["ysb_half"], 1)
            for q in range(QT):
                act.wait_ge(S["r_stat"], 4 + q + 1)
                act.activation(rstd[:, q:q + 1], sr[:, q:q + 1], ACT.Sqrt).then_inc(S["r_rstd"], 1)

        @block.vector
        def _(dve):
            n = [0]

            def link(ins):
                n[0] += 1
                ins.then_inc(S["dve_chain"], 1)
                dve.wait_ge(S["dve_chain"], n[0])

            def column(name, i=0):
                at = VEC[name][0] + i
                return vec[:, at:at + 1]

            def used(b):
                dve.wait_ge(S["w_used"], b + 1)

            dve.wait_ge(S["lam_in"], 16)
            rows = lam_rows[:, :].rearrange("p (a b d) -> p a b d", a=2, b=2)
            link(dve.tensor_tensor(lam_t[:, :, :], rows[:, :, 0, :], rows[:, :, 1, :], ALU.mult))
            dve.tensor_reduce(lam_s[:, 0:2], lam_t[:, :, :], AX.X, ALU.add).then_inc(S["lam_ready"], 1)
            dve.wait_ge(S["lam_exp"], 1)
            link(dve.tensor_tensor(lam_s[:, 0:1], lam_s[:, 3:4], lam_s[:, 2:3], ALU.subtract))
            lam_init = 0.8 - 0.6 * math.exp(-0.3 * 0)
            link(dve.tensor_scalar(lam_s[:, 0:1], lam_s[:, 0:1], -lam_init, None, ALU.add))
            dve.wait_ge(S["vec_done"], 1)
            link(dve.tensor_scalar(lam_s[:, 1:2], column("subln_a"), 1.0 - lam_init, None, ALU.mult))

            def soft_first(k, b, bias_of, scale):
                dve.wait_ge(S["sc_ready"], k + 1)
                if k >= 2:
                    dve.wait_ge(S["o_ready"], k - 1)
                for m in range(2):
                    last = dve.scalar_tensor_tensor(prob[:, b, m, :], acc[:, 2 * b + m, 0:384], scale, bias_of(m),
                                                    ALU.mult, ALU.add)
                link(last)
                dve.tensor_reduce(nmax[:, b, 0:2], prob[:, b, :, 0:128], AX.X, ALU.max)
                link(dve.tensor_reduce(nmax[:, b, 2:4], prob[:, b, :, 128:384], AX.X, ALU.max))
                dve.tensor_scalar(nmax[:, b, :], nmax[:, b, :], -1.0, None, ALU.mult).then_inc(S["nmax_ready"], 1)

            def attention(layer):
                bl = B_ATT[layer]

                def keys(i):
                    used(bl + 5 + 2 * i)
                    dve.tensor_copy(k_t[:, 2 * i:2 * i + 2, :].rearrange("p a b -> p (a b)"), pp[:, 1, :])\
                        .then_inc(S["k_done"], 1)

                def first(c):
                    soft_first(8 * layer + c, c % 2, lambda m: bias[:, 2 * c + m, :], 0.125)

                def second(c):
                    b = c % 2
                    dve.wait_ge(S["exp_done"], 8 * layer + c + 1)
                    if layer == 1:
                        dve.reciprocal(rsum[:, b, :], esum[:, b, :]).then_inc(S["attw_ready"], 1)
                        return
                    link(dve.reciprocal(rsum[:, b, :], esum[:, b, :]))
                    for q in range(QT):
                        r1 = rsum[:, b, 2 * q + 1:2 * q + 2]
                        last = dve.tensor_tensor(r1, r1, lam_s[:, 0:1], ALU.mult)
                    link(last)
                    for q in range(QT):
                        cols = slice(0, 128) if q == 0 else slice(128, 384)
                        last = dve.tensor_scalar(prob[:, b, 0, cols], prob[:, b, 0, cols],
                                                 rsum[:, b, 2 * q:2 * q + 1], None, ALU.mult)
                    link(last)
                    for q in range(QT):
                        cols = slice(0, 128) if q == 0 else slice(128, 384)
                        last = dve.scalar_tensor_tensor(prob[:, b, 0, cols], prob[:, b, 1, cols],
                                                        rsum[:, b, 2 * q + 1:2 * q + 2], prob[:, b, 0, cols],
                                                        ALU.mult, ALU.add)
                    last.then_inc(S["attw_ready"], 1)

                def out(c):
                    if layer == 0:
                        return
                    b = c % 2
                    dve.wait_ge(S["h_done"], 2)
                    dve.wait_ge(S["o_ready"], 8 + c + 1)
                    for q in range(QT):
                        for m in range(2):
                            at = 128 * c + 64 * m
                            last = dve.tensor_scalar(o_tm[:, q, at:at + 64],
                                                     acc[:, 2 * b + q, 384 + 64 * m:448 + 64 * m],
                                                     rsum[:, b, 2 * q + m:2 * q + m + 1], None, ALU.mult)
                    last.then_inc(S["o_done"], 1)

                keys(0)
                for i in range(1, 4):
                    if layer == 0 and i == 1:
                        dve.wait_ge(S["bias_in"], 32)
                    first(2 * i - 2)
                    if i >= 2:
                        out(2 * i - 3)
                    second(2 * i - 2)
                    first(2 * i - 1)
                    second(2 * i - 1)
                    keys(i)
                    out(2 * i - 2)
                first(6)
                out(5)
                second(6)
                first(7)
                second(7)
                out(6)
                out(7)
                if layer == 0:
                    dve.wait_ge(S["o_done"], 8)
                    for q in range(QT):
                        o3 = o_tm[:, q, :].rearrange("p (h d) -> p h d", h=8)
                        if q:
                            dve.wait_ge(S["osq_rstd"], q)
                        link(dve.tensor_tensor(stage_sq, o_tm[:, q, :], o_tm[:, q, :], ALU.mult))
                        link(dve.tensor_reduce(sv[:, :], stage_sq.rearrange("p (h d) -> p h d", h=8), AX.X, ALU.add))
                        link(dve.tensor_scalar(sv[:, :], sv[:, :], 1.0 / 128, LN_EPS, ALU.mult, ALU.add))
                        dve.reciprocal(sr[:, :], sv[:, :]).then_inc(S["osq_ready"], 1)
                        dve.wait_ge(S["osq_rstd"], q + 1)
                        dve.tensor_tensor(o3, o3, rstd[:, :].unsqueeze(2).to_broadcast([128, 8, 128]), ALU.mult)\
                            .then_inc(S["o_scaled"], 1)

            stage_sq = scr[:, 2, 0:1024]

            def row_stats(q, src, eps, done, rms=False):
                for a in range(2):
                    last = dve.bn_stats(st6[:, q, a, :], src[:, 512 * a:512 * a + 512])
                link(last)
                link(dve.bn_aggr(mv[:, q, :], st6[:, q, :, :].rearrange("p a b -> p (a b)")))
                if rms:
                    link(dve.scalar_tensor_tensor(sv[:, q:q + 1], mv[:, q, 0:1], mv[:, q, 0:1], mv[:, q, 1:2],
                                                  ALU.mult, ALU.add))
                    link(dve.tensor_scalar(sv[:, q:q + 1], sv[:, q:q + 1], eps, None, ALU.add))
                else:
                    link(dve.tensor_scalar(sv[:, q:q + 1], mv[:, q, 1:2], eps, None, ALU.add))
                dve.reciprocal(sr[:, q:q + 1], sv[:, q:q + 1]).then_inc(done, 1)

            def layer_norm(i, b):
                used(b)
                if i:
                    dve.wait_ge(S["h_done"], i)
                for q in range(QT):
                    bank = acc[:, 2 * q:2 * q + 2, :].rearrange("p a b -> p (a b)")
                    last = dve.scalar_tensor_tensor(o_tm[:, q, :], h_tm[:, q, :], ALPHA, bank, ALU.mult, ALU.add)
                    if q == 0:
                        link(last)
                    else:
                        last.then_inc(S["acc_taken"], 1)
                dve.wait_ge(S["acc_taken"], i + 1)
                for q in range(QT):
                    row_stats(q, o_tm[:, q, :], LN_EPS, S["ln_stat"])
                for q in range(QT):
                    dve.wait_ge(S["ln_rstd"], QT * i + q + 1)
                    dve.tensor_scalar(o_tm[:, q, :], o_tm[:, q, :], mv[:, q, 0:1], rstd[:, q:q + 1],
                                      ALU.subtract, ALU.mult).then_inc(S["ln_out"], 1)

            def mlp(layer):
                def step(v, t=None):
                    j = PAIRS * layer + v
                    dve.wait_ge(S["relu_done"], j + 1 if t is None else t * 3 + (j + 1))
                    if v >= 3:
                        b = B_MLP[layer] + 2 * (v - 3) + 3
                        dve.wait_ge(S["w_used"], b if t is None else t * 6 + b)
                    dve.tensor_tensor(hid[:, v % 3, :, :].rearrange("p a b -> p (a b)"), relu[:, v % 3, :],
                                      relu[:, v % 3, :], ALU.mult).then_inc(S["hid_ready"], 1)

                for v in range(4):
                    step(v)
                with dve.Fori(0, 4) as t:
                    for u in range(3):
                        step(4 + u, t)

            for layer in range(2):
                attention(layer)
                layer_norm(2 * layer, B_ATT[layer] + 15)
                mlp(layer)
                layer_norm(2 * layer + 1, B_MLP[layer] + 31)

            dve.wait_ge(S["rowsg_in"], 64)
            dve.wait_ge(S["rowsb_in"], 64)
            dve.wait_ge(S["ln_out"], 8)
            for q in range(QT):
                link(dve.tensor_tensor(h_tm[:, q, :], o_tm[:, q, :], rows_g[:, :], ALU.mult))
                last = dve.tensor_tensor(h_tm[:, q, :], h_tm[:, q, :], rows_b[:, :], ALU.add)
                if q == 0:
                    link(last)
            last.then_inc(S["h_done"], 1)
            dve.wait_ge(S["h_done"], 4)
            for q in range(QT):
                row_stats(q, h_tm[:, q, :], EPS, S["r_stat"], rms=True)
            for q in range(QT):
                dve.wait_ge(S["r_rstd"], q + 1)
                dve.tensor_scalar(o_tm[:, q, :], h_tm[:, q, :], rstd[:, q:q + 1], None, ALU.mult)\
                    .then_inc(S["r_out"], 1)
            dve.wait_ge(S["mod_mm"], 1)
            link(dve.tensor_copy(modc[:, :, :].rearrange("p a b -> p (a b)"), pp[:, 0, 0:32]))
            at = VEC["norm1_2"][0]
            dve.scalar_tensor_tensor(modc[:, 1, :], modc[:, 1, :], 1.0, vec[:, at:at + 8], ALU.add, ALU.mult)\
                .then_inc(S["modc_done"], 1)

            def rotate(out1, out2, bank, cos, sin, done, count, tmp):
                x = bank.rearrange("p (a b) -> p a b", a=2)
                a = tmp[:, 0, :].rearrange("p (a b) -> p a b", a=2)
                b = tmp[:, 1, :].rearrange("p (a b) -> p a b", a=2)
                dve.tensor_tensor(a, x, cos.unsqueeze(1).to_broadcast([128, 2, 256]), ALU.mult)
                link(dve.tensor_tensor(b, x, sin.unsqueeze(1).to_broadcast([128, 2, 256]), ALU.mult))
                dve.tensor_tensor(out1, a[:, 0, :], b[:, 1, :], ALU.subtract)
                dve.tensor_tensor(out2, a[:, 1, :], b[:, 0, :], ALU.add).then_inc(done, 1)
                dve.wait_ge(done, count)

            tmp = scr[:, 2, 0:1024].rearrange("p (a b) -> p a b", a=2)
            dve.wait_ge(S["lat_copied"], 1)
            for q in range(QT):
                dve.bn_stats(st6[:, q, 0, :], lat[:, q, 0:384])
                last = dve.bn_stats(st6[:, q, 1, :], lat[:, q, 384:640])
            link(last)
            for q in range(QT):
                for a in range(2):
                    last = dve.bn_aggr(mv[:, 2 * q + a, :], st6[:, q, a, :])
            link(last)
            link(dve.tensor_tensor(sv[:, 0:4], mv[:, 0:4, 0], mv[:, 0:4, 0], ALU.mult))
            link(dve.scalar_tensor_tensor(sv[:, 0:4], sv[:, 0:4], EPS, mv[:, 0:4, 1], ALU.add, ALU.add))
            dve.reciprocal(sr[:, 0:4], sv[:, 0:4]).then_inc(S["lat_stat"], 1)
            dve.wait_ge(S["lat_rstd"], 1)
            for q in range(QT):
                dve.tensor_scalar(lat[:, q, 0:384], lat[:, q, 0:384], rstd[:, 2 * q:2 * q + 1], None, ALU.mult)
                dve.tensor_scalar(lat[:, q, 384:640], lat[:, q, 384:640], rstd[:, 2 * q + 1:2 * q + 2], None,
                                  ALU.mult).then_inc(S["lat_done"], 1)
            for h in range(4):
                used(B_RQK + 2 * h)
                rotate(q_t[:, 2 * h, :], q_t[:, 2 * h + 1, :], pp[:, 0, :], con("cos_ret"), con("sin_ret"),
                       S["rq_done"], h + 1, tmp)
                used(B_RQK + 2 * h + 1)
                rotate(k_t[:, 2 * h, :], k_t[:, 2 * h + 1, :], pp[:, 1, :], con("cos_ret"), con("sin_ret"),
                       S["rk_done"], h + 1, tmp)
            dve.wait_ge(S["tp_done"], TP_LATENTS)
            rotate(pe_rope[:, 4, :], pe_rope[:, 5, :], pe_rope[:, 4:6, :].rearrange("p a b -> p (a b)"),
                   con("cos_mla"), con("sin_mla"), S["kpe_done"], 1, tmp)
            for a in range(2):
                dve.wait_ge(S["uq_ready"], 4 + a + 1)
                dve.wait_ge(S["uq_done"], 4 + a)
                rotate(pe_rope[:, 2 * a, :], pe_rope[:, 2 * a + 1, :], pp[:, a, :], con("cos_mla"), con("sin_mla"),
                       S["uq_done"], 5 + a, tmp)
            for h in range(4):
                dve.wait_ge(S["sret_ready"], h + 1)
                decay = con("decay")[:, 256 * h:256 * h + 256]
                link(dve.tensor_tensor(st_ret[:, h, 0:256], acc[:, h, 0:256], decay, ALU.mult))
                dve.tensor_tensor(st_ret[:, h, 256:384], acc[:, h, 256:384], decay[:, 0:128], ALU.mult)\
                    .then_inc(S["st_ready"], 1)

            def second(c):
                dve.wait_ge(S["exp_done"], 16 + c + 1)
                dve.reciprocal(rsum[:, c % 2, :], esum[:, c % 2, :]).then_inc(S["attw_ready"], 1)

            def out(c):
                dve.wait_ge(S["o_ready"], 16 + c + 1)
                for q in range(QT):
                    for m in range(2):
                        at = 256 * c + 128 * m
                        last = dve.tensor_scalar(o_mla[:, q, at:at + 128],
                                                 pp[:, c % 2, 256 * q + 128 * m:256 * q + 128 * m + 128],
                                                 rsum[:, c % 2, 2 * q + m:2 * q + m + 1], None, ALU.mult)
                last.then_inc(S["o_done"], 1)

            def first(c):
                soft_first(16 + c, c % 2, lambda m: con("mask"), MLA_SCALE)

            first(0)
            first(1)
            second(0)
            second(1)
            out(0)
            first(2)
            second(2)
            out(1)
            first(3)
            second(3)
            out(2)
            out(3)
            dve.wait_ge(S["y_done"], 4)
            for q in range(QT):
                for h in range(4):
                    last = dve.bn_stats(st6[:, 4 * q + h, 0, :], o_tm[:, q, 256 * h:256 * h + 256])
            link(last)
            for j in range(8):
                last = dve.bn_aggr(mv[:, j, :], st6[:, j, 0, :])
            link(last)
            link(dve.tensor_scalar(sv[:, :], mv[:, :, 1], EPS, None, ALU.add))
            dve.reciprocal(sr[:, :], sv[:, :]).then_inc(S["hn_stat"], 1)
            dve.wait_ge(S["hn_rstd"], 1)
            for q in range(QT):
                for h in range(4):
                    j = 4 * q + h
                    cols = slice(256 * h, 256 * h + 256)
                    last = dve.tensor_scalar(o_tm[:, q, cols], o_tm[:, q, cols], mv[:, j, 0:1], rstd[:, j:j + 1],
                                             ALU.subtract, ALU.mult)
            link(last)
            dve.wait_ge(S["rg_done"], 1)
            flat = acc[:, :, :].rearrange("p a b -> p (a b)")

            def whole(x):
                return x[:, :, :].rearrange("p a b -> p (a b)")

            dve.tensor_tensor(whole(o_tm), whole(o_tm), whole(rg), ALU.mult).then_inc(S["yret_ready"], 1)
            used(B_RO + 3)
            dve.wait_ge(S["gr_done"], 1)
            dve.tensor_tensor(whole(merged), flat, whole(gate), ALU.mult).then_inc(S["ret_merged"], 1)
            used(B_MO + 3)
            dve.wait_ge(S["gm_done"], 1)
            link(dve.tensor_tensor(whole(gate), flat, whole(gate), ALU.mult))
            dve.wait_ge(S["ret_merged"], 1)
            dve.tensor_tensor(whole(merged), whole(merged), whole(gate), ALU.add).then_inc(S["mla_merged"], 1)
            used(B_WO + 3)
            dve.wait_ge(S["mod_done"], 8)
            for q in range(QT):
                bank = acc[:, 2 * q:2 * q + 2, :].rearrange("p a b -> p (a b)")
                link(dve.tensor_tensor(o_tm[:, q, :], bank, mod[:, 2048:3072], ALU.mult))
                link(dve.tensor_tensor(h_tm[:, q, :], h_tm[:, q, :], o_tm[:, q, :], ALU.add))
            dve.wait_ge(S["rowsg_in"], 80)
            link(dve.scalar_tensor_tensor(mod[:, 4096:5120], mod[:, 4096:5120], 1.0, rows_g[:, :],
                                          ALU.add, ALU.mult))
            for q in range(QT):
                row_stats(q, h_tm[:, q, :], EPS, S["r_stat"], rms=True)
            for q in range(QT):
                dve.wait_ge(S["r_rstd"], 2 + q + 1)
                link(dve.scalar_tensor_tensor(o_tm[:, q, :], h_tm[:, q, :], rstd[:, q:q + 1], mod[:, 4096:5120],
                                              ALU.mult, ALU.mult))
                dve.tensor_tensor(o_tm[:, q, :], o_tm[:, q, :], mod[:, 3072:4096], ALU.add).then_inc(S["r_out"], 1)

            dve.wait_ge(S["lg_ready"], 1)
            link(dve.tensor_copy(route[:, :, 0:36], pp[:, :, 0:36]))
            link(dve.tensor_reduce(route[:, :, 36:37], route[:, :, 0:4], AX.X, ALU.max))
            dve.tensor_scalar(route[:, :, 36:37], route[:, :, 36:37], -1.0, None, ALU.mult).then_inc(S["lg_max"], 1)
            dve.wait_ge(S["lg_max"], 1)
            dve.wait_ge(S["lg_exp"], 1)

            def first_max(out, src, width, q, top, scratch):
                order = con("order")[:, 0:width]
                link(dve.tensor_reduce(top, src, AX.X, ALU.max))
                link(dve.scalar_tensor_tensor(out, src, top, order, ALU.is_equal, ALU.mult))
                link(dve.tensor_reduce(scratch, out, AX.X, ALU.max))
                link(dve.tensor_scalar(out, out, scratch, None, ALU.is_equal))

            big_s = router
            for q in range(QT):
                r = route[:, q, :]
                w = big_s[:, q, :]
                first_max(w[:, 0:4], r[:, 0:4], 4, q, w[:, 32:33], w[:, 34:35])
                picks = w[:, 0:4].unsqueeze(2).to_broadcast([128, 4, 8])
                prods = w[:, 48:80].rearrange("p (g e) -> p g e", g=4)
                link(dve.tensor_tensor(prods, r[:, 4:36].rearrange("p (g e) -> p g e", g=4), picks, ALU.mult))
                link(dve.tensor_reduce(w[:, 8:16], prods.rearrange("p g e -> p e g"), AX.X, ALU.add))
                first_max(w[:, 16:24], w[:, 8:16], 8, q, w[:, 32:33], w[:, 34:35])
                link(dve.scalar_tensor_tensor(w[:, 40:48], w[:, 16:24], NEG, w[:, 8:16], ALU.mult, ALU.add))
                first_max(w[:, 24:32], w[:, 40:48], 8, q, w[:, 33:34], w[:, 34:35])
                last = dve.tensor_tensor(r[:, 38:39], w[:, 33:34], w[:, 32:33], ALU.subtract)
                if q == 0:
                    link(last)
            last.then_inc(S["lg_m2"], 1)
            dve.wait_ge(S["lg_e2"], 1)
            for q in range(QT):
                r = route[:, q, :]
                w = big_s[:, q, :]
                link(dve.reciprocal(w[:, 35:36], r[:, 37:38]))
                link(dve.tensor_scalar(w[:, 36:37], r[:, 39:40], 1.0, None, ALU.add))
                link(dve.reciprocal(w[:, 36:37], w[:, 36:37]))
                link(dve.tensor_tensor(w[:, 36:37], w[:, 36:37], w[:, 35:36], ALU.mult))
                link(dve.tensor_tensor(w[:, 37:38], w[:, 36:37], r[:, 39:40], ALU.mult))
                link(dve.tensor_scalar(w[:, 40:48], w[:, 24:32], w[:, 37:38], None, ALU.mult))
                link(dve.scalar_tensor_tensor(w[:, 40:48], w[:, 16:24], w[:, 36:37], w[:, 40:48],
                                              ALU.mult, ALU.add))
                link(dve.tensor_tensor(w[:, 16:24], w[:, 16:24], w[:, 24:32], ALU.add))
                picks = w[:, 0:4].unsqueeze(2).to_broadcast([128, 4, 8])
                g3 = gates[:, q, :].rearrange("p (g e) -> p g e", g=4)
                m3 = picked[:, q, :].rearrange("p (g e) -> p g e", g=4)
                link(dve.tensor_tensor(g3, picks, w[:, 40:48].unsqueeze(1).to_broadcast([128, 4, 8]), ALU.mult))
                last = dve.tensor_tensor(m3, picks, w[:, 16:24].unsqueeze(1).to_broadcast([128, 4, 8]), ALU.mult)
                if q == 0:
                    link(last)
            last.then_inc(S["mask_ready"], 1)
            dve.wait_ge(S["pos_ready"], 1)
            pos = pp[:, 0, 0:64].rearrange("p (q e) -> p q e", q=2)
            link(dve.scalar_tensor_tensor(posn[:, :, :], pos, 1.0, picked[:, :, :], ALU.add, ALU.mult))
            link(dve.tensor_scalar(posn[:, :, :], posn[:, :, :], -1.0, None, ALU.add))
            link(dve.tensor_reduce(cnt[:, 0:1], pp[:, 0, 64:96], AX.X, ALU.max))
            for r in range(1, ROUNDS):
                link(dve.tensor_scalar(cnt[:, r:r + 1], cnt[:, 0:1], float(SLOTS * r), None, ALU.is_gt))
            link(dve.tensor_reduce(cnt[:, 4:5], cnt[:, 1:4], AX.X, ALU.add))
            link(dve.tensor_scalar(cnt[:, 4:5], cnt[:, 4:5], 1.0, None, ALU.add))
            link(dve.tensor_scalar(cnt[:, 5:6], cnt[:, 4:5], float(STEPS), None, ALU.mult))
            link(dve.tensor_copy(trips[:, 1:2], cnt[:, 4:5]))
            dve.tensor_copy(trips[:, 0:1], cnt[:, 5:6]).then_inc(S["trips_ready"], 1)
            dve.wait_ge(S["trips_ready"], 1)
            link(dve.memset(plan[:, ROUNDS * STEPS, :], -1.0))
            for r in range(ROUNDS):
                part = plan[:, r * STEPS:(r + 1) * STEPS, :].rearrange("p s (w q e) -> p s w q e", w=2, q=2)
                for q in range(QT):
                    src = posn[:, q, :].rearrange("p (s e) -> p s e", e=2)
                    dve.tensor_scalar(part[:, :, 0, q, :], src, float(-SLOTS * r), None, ALU.add)
                    last = dve.tensor_copy(part[:, :, 1, q, :], gates[:, q, :].rearrange("p (s e) -> p s e", e=2))
                link(last)
            steps = dve.value_load(trips[0:1, 0:1], min_val=STEPS, max_val=ROUNDS * STEPS)
            iota = con("iota")

            def select(next_pair):
                for q in range(QT):
                    for e in range(2):
                        last = dve.tensor_scalar(sel[:, q, 64 * e:64 * e + 64], iota,
                                                 now[:, 2 * q + e:2 * q + e + 1], None, ALU.is_equal)
                last.then_inc(S["sel_ready"], 1)

            link(dve.tensor_copy(now[:, :], plan[:, 0, :]))
            select(0)
            dve.memset(moe[:, :, :], 0.0).then_inc(S["cmb_done"], 4)
            base = n[0]
            with dve.Fori(0, steps) as i:
                for q in range(QT):
                    for e in range(2):
                        last = dve.tensor_scalar(gsel[:, q, 64 * e:64 * e + 64], iota,
                                                 now[:, 2 * q + e:2 * q + e + 1], now[:, 4 + 2 * q + e:5 + 2 * q + e],
                                                 ALU.is_equal, ALU.mult)
                last.then_inc(S["dve_chain"], 1)
                dve.wait_ge(S["dve_chain"], i * 2 + (base + 1))
                dve.tensor_copy(now[:, :], plan[:, bass.ds(i + 1, 1), :].rearrange("p a b -> p (a b)"))\
                    .then_inc(S["dve_chain"], 1)
                dve.wait_ge(S["dve_chain"], i * 2 + (base + 2))
                dve.wait_ge(S["xe_ready"], i + 1)
                select(1)
                for e in range(2):
                    dve.wait_ge(S["silu_e"], i * 2 + (e + 1))
                    dve.tensor_tensor(hid_x[:, e, :, :].rearrange("p a b -> p (a b)"), silu_a[:, e, :],
                                      up_bank[e][:, 128:256], ALU.mult).then_inc(S["hid_e"], 1)
                for half in range(2):
                    for q in range(QT):
                        dve.wait_ge(S["cmb_ready"], i * 4 + (2 * half + q + 1))
                        part = moe[:, q, 512 * half:512 * half + 512]
                        dve.tensor_tensor(part, acc[:, q, :], part, ALU.add).then_inc(S["cmb_done"], 1)
            dve.wait_ge(S["rowsb_in"], 80)
            dve.wait_ge(S["cmb_done"], steps * 4 + 4)
            for q in range(QT):
                dve.tensor_tensor(moe[:, q, :], moe[:, q, :], mod[:, 5120:6144], ALU.mult).then_inc(S["moe_g"], 1)
                dve.wait_ge(S["moe_g"], 2 * q + 1)
                dve.tensor_tensor(h_tm[:, q, :], h_tm[:, q, :], moe[:, q, :], ALU.add).then_inc(S["moe_g"], 1)
                dve.wait_ge(S["moe_g"], 2 * q + 2)
            fin = [0]

            def flink(ins):
                fin[0] += 1
                ins.then_inc(S["final_chain"], 1)
                dve.wait_ge(S["final_chain"], fin[0])

            for q in range(QT):
                for a in range(2):
                    last = dve.bn_stats(st6[:, q, a, :], h_tm[:, q, 512 * a:512 * a + 512])
                flink(last)
                flink(dve.bn_aggr(mv[:, q, :], st6[:, q, :, :].rearrange("p a b -> p (a b)")))
                flink(dve.scalar_tensor_tensor(sv[:, q:q + 1], mv[:, q, 0:1], mv[:, q, 0:1], mv[:, q, 1:2],
                                               ALU.mult, ALU.add))
                flink(dve.tensor_scalar(sv[:, q:q + 1], sv[:, q:q + 1], EPS, None, ALU.add))
                dve.reciprocal(sr[:, q:q + 1], sv[:, q:q + 1]).then_inc(S["r_stat"], 1)
            for q in range(QT):
                dve.wait_ge(S["r_rstd"], 4 + q + 1)
                dve.scalar_tensor_tensor(h_tm[:, q, :], h_tm[:, q, :], rstd[:, q:q + 1], rows_b[:, :],
                                         ALU.mult, ALU.mult).then_inc(S["out_ready"], 1)


def constant_tables():
    f = np.float32
    t = {"ident": np.eye(128, dtype=f)}
    pos = np.arange(SEQ, dtype=f)

    def rope(dim, copies):
        inv = (f(10000.0) ** (-np.arange(0, dim, 2, dtype=f) / f(dim))).astype(f)
        angle = pos[None, :] * inv[:, None]
        return [np.tile(fn(angle.astype(f)).astype(f), (copies, 1)) for fn in (np.cos, np.sin)]

    t["cos_ret"], t["sin_ret"] = rope(256, 1)
    t["cos_mla"], t["sin_mla"] = rope(64, 4)
    log_gamma = np.log1p(-np.exp2(-5.0 - np.arange(4, dtype=f))).astype(f)
    rel = np.arange(SEQ, dtype=f)[None, :] - np.arange(128, dtype=f)[:, None]
    decay = [np.where(rel >= 0, np.exp(g * np.maximum(rel, 0)), 0) * 256 ** -0.5 for g in log_gamma]
    t["decay"] = np.concatenate(decay, axis=1)
    i = np.arange(128)
    t["tri"] = (i[:, None] < i[None, :]).astype(f)
    t["ones"] = np.ones((128, 128), f)
    t["iota"] = np.tile(np.arange(64, dtype=f), (128, 1))
    k = np.arange(SEQ)
    t["mask"] = np.concatenate([np.where(k[None, :128] > i[:, None], NEG, 0),
                                np.where(k[None, :] > 128 + i[:, None], NEG, 0)], axis=1)
    t["order"] = np.tile(100.0 - np.arange(8), (128, 1))
    table = np.concatenate([t[name].astype(f) for name, _ in CONST_WIDTHS], axis=1)
    n = 255 - np.arange(512)
    nf = np.maximum(n, 16).astype(f)
    large = 16 + (np.log(nf / f(16)) / f(math.log(128 / 16)) * f(16)).astype(np.int32)
    bucket = np.where(n < 0, 32, np.where(n < 16, n, np.minimum(large, 31)))
    onehot = (np.arange(33)[:, None] == bucket[None, :]).astype(f)
    return np.ascontiguousarray(table), onehot


_INS = ["x", "w_in_a", "lam_a", "subln_a", "w_out_a", "w_kv_shared", "w_q_b", "w_out_b", "rel_bias", "ln1_g", "ln1_b",
        "ln2_g", "ln2_b", "w_up", "w_down", "c_2", "w_ada_2", "b_ada_2", "norm1_2", "norm2_2", "w_in_2", "w_ret_o_2",
        "q_norm_2", "kv_norm_2", "w_uq_2", "w_ukv_2", "w_mla_o_2", "w_out_2", "w_grp_2", "b_grp_2", "w_exp_2",
        "b_exp_2", "w1_2", "w3_2", "w2_2", "final_norm_2"]


def kernel(**inputs):
    import concourse.bacc as _bacc
    from concourse.bass_utils import run_bass_kernel_spmd as _run

    nc = _bacc.Bacc("TRN2", target_bir_lowering=False, num_devices=1)
    arrays, aps = {}, {}
    given = {name: np.ascontiguousarray(inputs[name]) for name in _INS}
    given["consts"], given["onehot"] = constant_tables()
    for name, a in given.items():
        arrays[f"in_{name}_dram"] = a
        aps[name] = nc.dram_tensor(f"in_{name}_dram", a.shape, mybir.dt.from_np(a.dtype), kind="ExternalInput").ap()
    aps["bias_dram"] = nc.dram_tensor("bias_dram", (16, 128, 512), mybir.dt.float32, kind="Internal").ap()
    aps["out"] = nc.dram_tensor("out_dram", (1, SEQ, D), mybir.dt.float32, kind="ExternalOutput").ap()
    program(nc, aps)
    r = _run(nc, [arrays], core_ids=[0])
    return r.results[0]["out_dram"]
```

```python
import math
from contextlib import ExitStack

import numpy as np

import concourse.bass as bass
from concourse import mybir

D = 1024
KT = D // 128
SEQ = 256
QT = SEQ // 128
D_FF = 4096
PAIRS = D_FF // 256
RING = 4
CHUNK = 512
PARTS = 4
EXPERTS = 32
SLOTS = 64
ROUNDS = SEQ // SLOTS
STEPS = EXPERTS // 4
ALPHA = (2 * 2) ** 0.25
NEG = -1e30
LN_EPS = 1e-5
EPS = 1e-6
MLA_SCALE = (128 + 64) ** -0.5

CONST_WIDTHS = [("ident", 128), ("tri", 128), ("ones", 128), ("iota", 64), ("mask", 384), ("order", 8)]
LATE_WIDTHS = [("cos_ret", 256), ("sin_ret", 256), ("cos_mla", 256), ("sin_mla", 256), ("decay", 1024)]
CONST_AT = {}
_at = 0
for _name, _w in CONST_WIDTHS:
    CONST_AT[_name] = (_at, _at + _w)
    _at += _w
CONST_COLS = _at
LATE_AT = {}
_at = 0
for _name, _w in LATE_WIDTHS:
    LATE_AT[_name] = (_at, _at + _w)
    _at += _w

VEC = {}
_at = 0
for _name, _rows in [("ln1_g", 16), ("ln1_b", 16), ("ln2_g", 16), ("ln2_b", 16), ("norm1_2", 8), ("norm2_2", 8),
                     ("q_norm_2", 3), ("kv_norm_2", 2), ("subln_a", 1), ("c_2", 8)]:
    VEC[_name] = (_at, _rows)
    _at += _rows
VEC_ROWS = _at

B_ATT = [0, 48]
B_MLP = [16, 64]
B_C = 96
B_RQK = 100
B_UQ = 108
B_UKV = 111
B_RV = 113
B_RG = 117
B_GR = 121
B_GM = 125
B_RO = 129
B_MO = 133
B_WO = 137
B_MOE = 141
INPUT_AT = [0, 12, 16, 20, 40, 44, 48, 64, 68, 72]
TP_LATENTS = 56


def is_split(b):
    return b < B_UQ or B_RV <= b < B_MOE


def slot_of(b):
    return b % RING


def split_index(b):
    return b if b < B_UQ else b - (B_RV - B_UQ)


def whole_index(b):
    return b - B_UQ


def low_by_vector(b):
    return b < B_ATT[0] + 4 or any(a <= b < a + 32 for a in B_MLP)


def low_index(b):
    n = sum(low_by_vector(x) for x in range(b))
    return n if low_by_vector(b) else split_index(b) - n


def program(nc, A):
    f32, i32, f32r = mybir.dt.float32, mybir.dt.int32, mybir.dt.float32r
    ALU, ACT, AX = mybir.AluOpType, mybir.ActivationFunctionType, mybir.AxisListType
    ctx = ExitStack()
    with ctx:
        def sb(name, shape, dt=f32):
            return ctx.enter_context(nc.sbuf_tensor(name, shape, dt))

        consts = sb("consts", [128, CONST_COLS])
        ring = sb("ring", [128, RING, 2048])
        h_tm = sb("h_tm", [128, QT, D])
        x_hi = sb("x_hi", [128, KT, SEQ], f32r)
        x_lo = sb("x_lo", [128, KT, SEQ], f32r)
        w_hi = sb("w_hi", [128, PARTS, CHUNK], f32r)
        w_lo = sb("w_lo", [128, PARTS, CHUNK], f32r)
        hid_hi = sb("hid_hi", [128, 2, 2, SEQ], f32r)
        hid_lo = sb("hid_lo", [128, 2, 2, SEQ], f32r)
        v_tm = sb("v_tm", [128, QT, D])
        q_t = sb("q_t", [128, KT, SEQ])
        k_t = sb("k_t", [128, KT, SEQ])
        o_tm = sb("o_tm", [128, QT, D])
        big = sb("big", [128, 6144])
        scr = sb("scr", [128, 2, 1536])
        mod = sb("mod", [128, 6144])
        stage = sb("stage", [128, 2, 1024])
        rows = sb("rows", [128, 2, 1024])
        rows_g, rows_b = rows[:, 0, :], rows[:, 1, :]
        pe_rope = rows[:, :, :].rearrange("p a b -> p (a b)")[:, 0:1536].rearrange("p (a t) -> p a t", a=6)
        vec_rows = sb("vec_rows", [128, 128])
        vec = sb("vec", [128, 128])
        modc = sb("modc", [128, 2, 8])
        relb = sb("relb", [33, 16])
        bias_rows = stage[0:16, 0, 0:512]
        onehot = stage[0:33, 1, 0:512]
        lam_rows = sb("lam_rows", [128, 256])
        lam_t = sb("lam_t", [128, 2, 64])
        lam_s = sb("lam_s", [128, 4])
        act_c = sb("act_c", [128, 8])
        brow = sb("brow", [1, 64])
        w_rt = sb("w_rt", [128, KT, 36])
        st6 = sb("st6", [128, 8, 2, 6])
        mv = sb("mv", [128, 8, 2])
        sv = sb("sv", [128, 8])
        sr = sb("sr", [128, 8])
        rstd = sb("rstd", [128, 8])
        nmax = sb("nmax", [128, 2, 4])
        esum = sb("esum", [128, 2, 4])
        rsum = sb("rsum", [128, 2, 4])

        def con(name, rows=128):
            if name in LATE_AT:
                a, b = LATE_AT[name]
                return stage[:, :, :].rearrange("p a b -> p (a b)")[:, a:b]
            a, b = CONST_AT[name]
            return consts[0:rows, a:b]

        ident = con("ident")
        bias = big[:, :].rearrange("p (h k) -> p h k", h=16)
        prob = scr[:, 0, :].rearrange("p (b m k) -> p b m k", b=2, m=2)
        prob_t = scr[:, 1, :].rearrange("p (b m k) -> p b m k", b=2, m=2)
        relu = scr[:, 0, 0:1024].rearrange("p (b n) -> p b n", b=2)
        x_f = scr[:, 1, 0:1024].rearrange("p (b c n) -> p b c n", b=2, c=4)
        qn_t = big[:, 0:2048].rearrange("p (h t) -> p h t", h=8)
        kn_t = big[:, 2048:4096].rearrange("p (h t) -> p h t", h=8)
        v_mla = big[:, 4096:6144].rearrange("p (q n) -> p q n", q=2)
        rg = big[:, 0:2048].rearrange("p (q n) -> p q n", q=2)
        gate_r = big[:, 2048:4096].rearrange("p (q n) -> p q n", q=2)
        gate_m = big[:, 4096:6144].rearrange("p (q n) -> p q n", q=2)
        merged = q_t[:, :, :].rearrange("p (q a) t -> p q (a t)", q=2)
        lat = o_tm[:, :, 0:896]
        lat_t = scr[:, 1, 0:1280].rearrange("p (c t) -> p c t", c=5)
        st_ret = scr[:, 0, :].rearrange("p (h k) -> p h k", h=4)
        o_mla = k_t[:, :, :].rearrange("p (q a) t -> p q (a t)", q=2)

        xe = k_t
        ysb = big[:, 0:1024]
        u_hi = x_hi[:, :, :].rearrange("p (q a) t -> p q (a t)", q=2)
        u_lo = x_lo[:, :, :].rearrange("p (q a) t -> p q (a t)", q=2)
        sel = sb("sel", [128, QT, 4 * SLOTS], f32r)
        room = [0, 0]

        def carve(part, *dims):
            size = math.prod(dims)
            at = room[part]
            room[part] += size
            assert room[part] <= 1536
            names = "abc"[:len(dims)]
            piece = scr[:, part, at:at + size]
            if len(dims) == 1:
                return piece
            pattern = f"p ({' '.join(names)}) -> p {' '.join(names)}"
            return piece.rearrange(pattern, **dict(zip(names[:-1], dims[:-1])))

        gsel = carve(0, 2, QT, 128)
        hid_e = carve(0, 256)
        silu_e = carve(0, 256)
        turned = carve(0, 512)
        e_ring = [big[:, 2048:4096], big[:, 4096:6144]] + [ring[:, slot_of(B_WO + i), :] for i in range(4)]
        plan = carve(1, ROUNDS * STEPS + 1, 16)
        route = carve(1, QT, 64)
        router = carve(1, QT, 80)
        gates, picked, posn = (carve(1, QT, EXPERTS) for _ in range(3))
        now = sb("now", [128, 16])
        cnt = sb("cnt", [128, 8])
        trips = sb("trips", [128, 2], i32)

        moe = v_tm

        acc = ctx.enter_context(nc.psum_tensor("acc", [128, 4, 512], f32))
        pp = ctx.enter_context(nc.psum_tensor("pp", [128, 2, 512], f32))
        tp = ctx.enter_context(nc.psum_tensor("tp", [128, 2, 512], f32))

        up_bank, turn_bank, y_bank = pp[:, 0, :], pp[:, 1, :], (tp[:, 0, :], tp[:, 1, :])
        gather_bank = (turn_bank, y_bank[0], y_bank[1], turn_bank)

        def sem(name):
            return ctx.enter_context(nc.semaphore(name))

        w_full = [sem(f"w_full{i}") for i in range(RING)]
        e_full = [sem(f"e_full{i}") for i in range(6)]
        ada_full = [sem(f"ada_full{i}") for i in range(2)]
        S = {n: sem(n) for n in """
            w_used chunk_used hi_ready lo_pool lo_dve xf_ready x_split tile_ready sq_done u_split late_in consts_in x_in relb_in vec_in lam_in onehot_in rowsg_in rowsb_in small_in badd_in
            relb_set vecrow_set bias_mm bias_copied bias_dram bias_in vec_mm vec_done
            tp_ready tp_done x_ready v_done q_done k_done sc_ready nmax_ready exp_done attw_ready o_ready o_done
            osq_ready osq_rstd o_scaled ln_stat ln_rstd ln_out h_done up_ready relu_done hid_ready hid_used
            dve_chain act_chain pool_chain lam_ready lam_exp lam_done c_silu ada_done mod_mm mod_done modc_done acc_taken
            lat_copied lat_stat lat_rstd lat_done rq_done rk_done uqr_in kpe_done uq_ready uq_done pe_done vmla_done
            rv_done sret_ready st_ready y_ready y_done hn_stat hn_rstd rg_done gr_done yret_ready ret_merged gm_done
            mla_merged wo_done out_stored out_ready
            r_stat r_rstd r_out lg_ready lg_copied lg_max lg_exp lg_m2 lg_e2 mask_ready pos_ready trips_ready
            sel_ready gsel_ready xe_ready xe_done e_used silu_done hid_done turn_ready turned_done y0_ready y0_done y1_done
            sums_ready moe_g final_chain
            """.split()}
        block = ctx.enter_context(nc.Block())

        def w_row_tiles(w, kt, cols):
            return w[kt * 128:(kt + 2) * 128, cols].rearrange("(k p) n -> p k n", p=128)

        def w_cols(w, cols):
            return w[:, cols].rearrange("(k p) n -> p k n", p=128)

        def chunk(b, j):
            s = ring[:, slot_of(b), :]
            if b >= B_C and b < B_RQK:
                k, half = divmod(j, 2)
                return s[:, 704 * k + 384 * half:704 * k + (704 if half else 384)]
            if is_cols(b):
                c, k = divmod(j, 2)
                return s.rearrange("p (k n) -> p k n", k=8)[:, 4 * k:4 * k + 4, 128 * c:128 * c + 128]
            return s[:, CHUNK * j:CHUNK * j + CHUNK]

        def is_cols(b):
            for a in B_ATT:
                if a + 4 <= b < a + 12:
                    return True
            for a in B_MLP:
                if b == a or (a < b < a + 31 and (b - a) % 2 == 1):
                    return True
            return B_RQK <= b < B_RQK + 8

        def split_view(w, j, part):
            if len(part.shape) == 3:
                return w[:, j, :].rearrange("p (k n) -> p k n", k=part.shape[1])
            return w[:, j, 0:part.shape[1]]

        @block.sync
        def _(sp):
            def load(b, src, at=0):
                n = src.shape[1] * src.shape[2]
                if b >= RING:
                    old = b - RING
                    if is_split(old):
                        sp.wait_ge(S["lo_dve"] if low_by_vector(old) else S["lo_pool"], PARTS * (low_index(old) + 1))
                    else:
                        sp.wait_ge(S["w_used"], whole_index(old) + 1)
                dst = ring[:, slot_of(b), 0:n].rearrange("p (k n) -> p k n", k=src.shape[1])
                sp.dma_start(dst, src).then_inc(w_full[slot_of(b)], 16)

            def cols(a, n):
                return slice(a, a + n)

            sp.dma_start(consts[:, :], A["consts"]).then_inc(S["consts_in"], 16)
            sp.dma_start(h_tm[:, :, :], A["x"][0, :, :].rearrange("(q p) n -> p q n", p=128)).then_inc(S["x_in"], 16)
            for layer in range(2):
                b = B_ATT[layer]
                wv, cv = (A["w_in_a"][0, :, :], 2048) if layer == 0 else (A["w_kv_shared"], 1024)
                wq, cq = (A["w_in_a"][0, :, :], 0) if layer == 0 else (A["w_q_b"][0, :, :], 0)
                wk, ck = (A["w_in_a"][0, :, :], 1024) if layer == 0 else (A["w_kv_shared"], 0)
                wo = A["w_out_a"][0, :, :] if layer == 0 else A["w_out_b"][0, :, :]
                for i in range(4):
                    load(b + i, w_row_tiles(wv, 2 * i, cols(cv, D)))
                for i in range(4):
                    load(b + 4 + 2 * i, w_cols(wq, cols(cq + 256 * i, 256)))
                    load(b + 5 + 2 * i, w_cols(wk, cols(ck + 256 * i, 256)))
                for i in range(4):
                    load(b + 12 + i, w_row_tiles(wo, 2 * i, cols(0, D)))
                b = B_MLP[layer]
                up = A["w_up"][layer, :, :].rearrange("(k p) n -> p k n", p=128)
                down = A["w_down"][layer, :, :]

                def up_cols(j):
                    load(b + max(2 * j - 1, 0), up[:, :, 256 * j:256 * j + 256])

                def down_rows(j):
                    load(b + min(2 * j + 2, 31), down[j * 256:(j + 1) * 256, :].rearrange("(k p) n -> p k n", p=128))

                up_cols(0)
                for j in range(3):
                    up_cols(j + 1)
                    down_rows(j)
                with sp.Fori(0, 6) as t:
                    for u in range(2):
                        for part in range(2):
                            o = 7 + 2 * u + part
                            low = PARTS * (low_index(b + o - RING) + 1)
                            sp.wait_ge(S["lo_dve"], t * (4 * PARTS) + low)
                            s = slot_of(b + o)
                            if part == 0:
                                src = up[:, :, bass.ds(t * 512 + (u + 4) * 256, 256)]
                                dst = ring[:, s, :].rearrange("p (k n) -> p k n", k=8)
                            else:
                                src = down[bass.ds(t * 512 + (u + 3) * 256, 256), :]\
                                    .rearrange("(k p) n -> p k n", p=128)
                                dst = ring[:, s, :].rearrange("p (k n) -> p k n", k=2)
                            sp.dma_start(dst, src).then_inc(w_full[s], 16)
                down_rows(15)
            w_in = A["w_in_2"][0, :, :]
            for i in range(4):
                load(B_C + i, w_row_tiles(w_in, 2 * i, cols(4096, 704)))
            for h in range(4):
                load(B_RQK + 2 * h, w_cols(w_in, cols(256 * h, 256)))
                load(B_RQK + 2 * h + 1, w_cols(w_in, cols(1024 + 256 * h, 256)))
            for i in range(3):
                w = A["w_uq_2"][0, i * 128:(i + 1) * 128, :].rearrange("p (h c) -> p h c", c=192)
                load(B_UQ + i, w[:, :, 0:128])
                for x in range(2):
                    sp.dma_start(ring[:, slot_of(B_UQ + i), 1024 + 256 * x:1280 + 256 * x]
                                 .rearrange("p (h c) -> p h c", h=8),
                                 w[:, :, 128 + 32 * x:160 + 32 * x]).then_inc(S["uqr_in"], 16)
            for i in range(2):
                load(B_UKV + i, A["w_ukv_2"][0, i * 128:(i + 1) * 128, :].rearrange("(k p) n -> p k n", k=1))
            for b, w, c in ((B_RV, w_in, 2048), (B_RG, w_in, 3072), (B_GR, w_in, 4800), (B_GM, w_in, 5824),
                            (B_RO, A["w_ret_o_2"][0, :, :], 0), (B_MO, A["w_mla_o_2"][0, :, :], 0), (B_WO, A["w_out_2"][0, :, :], 0)):
                for i in range(4):
                    load(b + i, w_row_tiles(w, 2 * i, cols(c, D)))
            w1 = A["w1_2"][0, :, :, :, :].rearrange("g e (k p) f -> (g e) p k f", p=128)
            w3 = A["w3_2"][0, :, :, :, :].rearrange("g e (k p) f -> (g e) p k f", p=128)
            w2 = A["w2_2"][0, :, :, :, :].rearrange("g e (k p) n -> (g e) p k n", p=128)
            parts = [(w, 2 * pair + e) for pair in range(2) for w in (w1, w3, w2) for e in range(2)]
            for o, (w, e) in enumerate(parts):
                if o < 2:
                    sp.wait_ge(S["mla_merged"], QT)
                elif o < 6:
                    sp.wait_ge(S["lo_pool"], PARTS * (low_index(B_WO + o - 2) + 1))
                else:
                    sp.wait_ge(S["e_used"], o - 5)
                sp.dma_start(e_ring[o % 6].rearrange("p (k n) -> p k n", k=2 if w is w2 else 8), w[e, :, :, :])\
                    .then_inc(e_full[o % 6], 16)
            sp.wait_ge(S["trips_ready"], 1)
            steps = sp.value_load(trips[0:1, 0:1], min_val=STEPS, max_val=ROUNDS * STEPS)
            with sp.Fori(1, steps) as i:
                for o, (w, e) in enumerate(parts):
                    sp.wait_ge(S["e_used"], i * 12 + (o - 5))
                    sp.dma_start(e_ring[o % 6].rearrange("p (k n) -> p k n", k=2 if w is w2 else 8),
                                 w[bass.ds((i % STEPS) * 4 + e, 1), :, :, :].rearrange("o p k n -> p (o k) n"))\
                        .then_inc(e_full[o % 6], 16)
            for q in range(QT):
                sp.wait_ge(S["out_ready"], q + 1)
                sp.dma_start(A["out"][0, q * 128:(q + 1) * 128, :], h_tm[:, q, :]).then_inc(S["out_stored"], 16)
            sp.wait_ge(S["out_stored"], 16 * QT)

        @block.gpsimd
        def _(pool):
            n = [0]

            def link(ins):
                n[0] += 1
                ins.then_inc(S["pool_chain"], 1)
                pool.wait_ge(S["pool_chain"], n[0])

            pool.memset(relb[:, :], NEG).then_inc(S["relb_set"], 1)
            pool.wait_ge(S["relb_set"], 1)
            pool.dma_start(relb[0:32, :], A["rel_bias"]).then_inc(S["relb_in"], 16)
            pool.dma_start(onehot, A["onehot"]).then_inc(S["onehot_in"], 16)
            pool.memset(vec_rows[:, :], 0.0).then_inc(S["vecrow_set"], 1)
            pool.wait_ge(S["vecrow_set"], 1)
            for name, (at, rows) in VEC.items():
                flat = A[name].rearrange("a (r n) -> (a r) n", n=128)
                pool.dma_start(vec_rows[at:at + rows, :], flat).then_inc(S["vec_in"], 16)
            pool.dma_start(lam_rows[:, :], bass.AP(A["lam_a"].tensor, 0, [[0, 128], [1, 256]])).then_inc(S["lam_in"], 16)
            pool.wait_ge(S["bias_copied"], 1)
            pool.dma_start(A["bias_dram"], bias_rows.unsqueeze(1).to_broadcast([16, 128, 512]))\
                .then_inc(S["bias_dram"], 16)
            pool.dma_start(brow[0:1, 0:4], A["b_grp_2"]).then_inc(S["small_in"], 16)
            pool.dma_start(brow[0:1, 4:36], A["b_exp_2"]).then_inc(S["small_in"], 16)
            pool.dma_start(w_rt[:, :, 0:4], A["w_grp_2"][0, :, :].rearrange("(k p) n -> p k n", p=128))\
                .then_inc(S["small_in"], 16)
            pool.dma_start(w_rt[:, :, 4:36], A["w_exp_2"][0, :, :].rearrange("(k p) n -> p k n", p=128))\
                .then_inc(S["small_in"], 16)
            link(pool.memset(mod[:, :], 0.0))
            pool.dma_start(mod[0:1, :], A["b_ada_2"]).then_inc(S["badd_in"], 16)
            pool.wait_ge(S["bias_dram"], 16)
            t = A["bias_dram"].tensor
            pool.dma_start(bias[:, :, 0:128], bass.AP(t, 255, [[511, 128], [128 * 512, 16], [1, 128]]))\
                .then_inc(S["bias_in"], 16)
            pool.dma_start(bias[:, :, 128:384], bass.AP(t, 127, [[511, 128], [128 * 512, 16], [1, 256]]))\
                .then_inc(S["bias_in"], 16)

            def ada(k0, k1):
                for k in range(k0, k1):
                    for j in range(6):
                        i = 6 * k + j
                        s = i % 2
                        if i == 0:
                            fetch(0)
                        if i + 1 < 48:
                            fetch(i + 1)
                        pool.wait_ge(ada_full[s], 16 * (i // 2 + 1))
                        link(pool.tensor_scalar(stage[:, s, :], stage[:, s, :], act_c[:, k:k + 1], None, ALU.mult))
                        part = mod[:, j * 1024:(j + 1) * 1024]
                        last = pool.tensor_tensor(part, part, stage[:, s, :], ALU.add)
                        if i == 47:
                            last.then_inc(S["ada_done"], 1)
                        else:
                            link(last)

            def fetch(i):
                k, j = divmod(i, 6)
                pool.dma_start(stage[:, i % 2, :], A["w_ada_2"][0, k * 128:(k + 1) * 128, j * 1024:(j + 1) * 1024])\
                    .then_inc(ada_full[i % 2], 16)

            done = [0]

            def low(b, n=1):
                for bb in range(b, b + n):
                    for j in range(PARTS):
                        pool.wait_ge(S["hi_ready"], PARTS * split_index(bb) + j + 1)
                        part = chunk(bb, j)
                        pool.tensor_tensor(split_view(w_lo, j, part), part, split_view(w_hi, j, part),
                                           ALU.subtract).then_inc(S["lo_pool"], 1)

            def rows(src_g, src_b, i):
                pool.dma_start(rows_g, bass.AP(src_g.tensor, i * 1024, [[0, 128], [1, 1024]]))\
                    .then_inc(S["rowsg_in"], 16)
                pool.dma_start(rows_b, bass.AP(src_b.tensor, i * 1024, [[0, 128], [1, 1024]]))\
                    .then_inc(S["rowsb_in"], 16)

            def residual(i):
                pool.wait_ge(S["rowsg_in"], 16 * (i + 1))
                pool.wait_ge(S["rowsb_in"], 16 * (i + 1))
                for q in range(QT):
                    pool.wait_ge(S["ln_out"], QT * i + q + 1)
                    link(pool.tensor_tensor(h_tm[:, q, :], o_tm[:, q, :], rows_g, ALU.mult))
                    last = pool.tensor_tensor(h_tm[:, q, :], h_tm[:, q, :], rows_b, ALU.add)
                    if q == 0:
                        link(last)
                last.then_inc(S["h_done"], 1)
                pool.wait_ge(S["h_done"], i + 1)

            rows(A["ln1_g"], A["ln1_b"], 0)
            low(B_ATT[0] + 4, 12)
            pool.wait_ge(S["c_silu"], 1)
            pool.wait_ge(S["badd_in"], 16)
            ada(0, 1)
            residual(0)
            rows(A["ln2_g"], A["ln2_b"], 0)
            ada(1, 4)
            low(B_ATT[1], 1)
            pool.wait_ge(S["h_done"], 2)
            rows(A["ln1_g"], A["ln1_b"], 1)
            low(B_ATT[1] + 1, 15)
            residual(2)
            rows(A["ln2_g"], A["ln2_b"], 1)
            ada(4, 8)
            pool.wait_ge(S["ada_done"], 1)
            pool.dma_start(stage[:, :, :].rearrange("p a b -> p (a b)"), A["late"]).then_inc(S["late_in"], 16)
            low(B_C, 12)
            low(B_RV, 16)
            pool.wait_ge(S["o_done"], 20)
            pool.dma_start(rows_g, bass.AP(A["norm2_2"].tensor, 0, [[0, 128], [1, 1024]]))\
                .then_inc(S["rowsg_in"], 16)
            pool.dma_start(rows_b, bass.AP(A["final_norm_2"].tensor, 0, [[0, 128], [1, 1024]]))\
                .then_inc(S["rowsb_in"], 16)
            low(B_RO, 12)
            pool.wait_ge(S["mla_merged"], QT)
            pool.memset(ysb[:, 0:512], 0.0).then_inc(S["y0_done"], 1)
            pool.memset(ysb[:, 512:1024], 0.0).then_inc(S["y1_done"], 1)
            pool.memset(turned, 0.0).then_inc(S["turned_done"], 1)

        @block.tensor
        def _(pe):
            groups = [0]

            def transposes(items):
                g = groups[0]
                groups[0] += 1
                if g >= 2:
                    pe.wait_ge(S["tp_done"], g - 1)
                for off, src in items:
                    last = pe.transpose(tp[:, g % 2, off:off + 128], src, ident)
                last.then_inc(S["tp_ready"], 1)

            def tile_to_feature_major(src, q):
                for half in range(2):
                    transposes([(128 * j, src[:, q, (4 * half + j) * 128:(4 * half + j + 1) * 128])
                                for j in range(4)])

            def to_feature_major(src):
                for q in range(QT):
                    tile_to_feature_major(src, q)

            def transposed():
                pe.wait_ge(S["tp_done"], groups[0])

            inputs = [0]

            def input_split():
                inputs[0] += 4
                pe.wait_ge(S["x_split"], inputs[0])

            def product(out, lhs, rhs, start, stop):
                pe.matmul(out, lhs[0], rhs[0], start=start, stop=False)
                pe.matmul(out, lhs[0], rhs[1], start=False, stop=False)
                return pe.matmul(out, lhs[1], rhs[0], start=False, stop=stop)

            def chunk_ready(b, j, t=None, per=0):
                sem_ = S["lo_dve"] if low_by_vector(b) else S["lo_pool"]
                n = PARTS * low_index(b) + j + 1
                pe.wait_ge(sem_, n if t is None else t * per + n)

            def x_parts(kt, cols=slice(0, SEQ)):
                return x_hi[:, kt, cols], x_lo[:, kt, cols]

            def w_parts(j, cols=slice(0, CHUNK)):
                return w_hi[:, j, cols], w_lo[:, j, cols]

            def arrive(b):
                pe.wait_ge(w_full[slot_of(b)], 16 * (b // RING + 1))

            def tokens_out(b, freed=None, by_tile=False):

                def part(i, j, q):
                    k, half = divmod(j, 2)
                    kt = 2 * i + k
                    return product(acc[:, 2 * q + half, :], x_parts(kt, slice(q * 128, (q + 1) * 128)),
                                   w_parts(j), start=(kt == 0), stop=(kt == 7))

                for i in range(3 if by_tile else 4):
                    for j in range(PARTS):
                        chunk_ready(b + i, j)
                        if freed and i == 0 and j < 2:
                            pe.wait_ge(S[freed], 2 * (j + 1))
                        for q in range(QT):
                            last = part(i, j, q)
                        last.then_inc(S["chunk_used"], 1)
                if by_tile:
                    for j in range(PARTS):
                        chunk_ready(b + 3, j)
                        last = part(3, j, 0)
                    last.then_inc(S["tile_ready"], 1)
                    for j in range(PARTS):
                        part(3, j, 1).then_inc(S["chunk_used"], 1)

            def features_out(b, bank, t=None):
                for j in range(PARTS):
                    c, k = divmod(j, 2)
                    chunk_ready(b, j, t, 4 * PARTS)
                    for i in range(4):
                        kt = 4 * k + i
                        last = product(bank[:, 256 * c:256 * c + 256], w_parts(j, slice(128 * i, 128 * i + 128)),
                                       x_parts(kt), start=(kt == 0), stop=(kt == KT - 1))
                    last.then_inc(S["chunk_used"], 1)

            def scores(n, c):
                pe.wait_ge(S["q_done"], n // 2 + 1)
                pe.wait_ge(S["k_done"], n // 2 + 1)
                if n % 8 >= 2:
                    pe.wait_ge(S["o_done"], n - 1)
                for m in range(2):
                    p = slice(64 * m, 64 * m + 64)
                    bank = acc[:, 2 * (c % 2) + m, :]
                    pe.matmul(bank[:, 0:128], q_t[p, c, 0:128], k_t[p, c, 0:128], start=True, stop=True)
                    last = pe.matmul(bank[:, 128:384], q_t[p, c, 128:256], k_t[p, c, :], start=True, stop=True)
                last.then_inc(S["sc_ready"], 1)

            def att_out(layer, n, c):
                pe.wait_ge(S["attw_ready"], n + 1)
                maps = (0,) if layer == 0 else (0, 1)
                for m in maps:
                    transposes([(128 * j, prob[:, c % 2, m, 128 * j:128 * j + 128]) for j in range(3)])
                transposed()
                pe.wait_ge(S["v_done"], layer + 1)
                for m in maps:
                    w = 128 if layer == 0 else 64
                    cols = slice(128 * c + w * m, 128 * c + w * m + w)
                    for q in range(QT):
                        out = acc[:, 2 * (c % 2) + q, 384 + w * m:384 + w * m + w]
                        for kb in range(q + 1):
                            j = 0 if q == 0 else 1 + kb
                            last = pe.matmul(out, prob_t[:, c % 2, m, 128 * j:128 * j + 128], v_tm[:, kb, cols],
                                             start=(kb == 0), stop=(kb == q))
                last.then_inc(S["o_ready"], 1)

            def attention(layer):
                b = B_ATT[layer]
                tokens_out(b)
                if layer == 0:
                    pe.wait_ge(S["vec_in"], 16 * len(VEC))
                    pe.transpose(pp[:, 1, 0:128], vec_rows[:, :], ident).then_inc(S["vec_mm"], 1)
                    pe.wait_ge(S["bias_copied"], 1)
                    pe.wait_ge(S["vec_done"], 1)
                pe.wait_ge(S["v_done"], layer + 1)

                def queries(i):
                    if layer + i:
                        pe.wait_ge(S["q_done"], 4 * layer + i)
                    features_out(b + 4 + 2 * i, pp[:, 0, :])

                def keys(i):
                    if layer + i:
                        pe.wait_ge(S["k_done"], 4 * layer + i)
                    features_out(b + 5 + 2 * i, pp[:, 1, :])

                n = 8 * layer
                queries(0)
                keys(0)
                for i in range(1, 4):
                    queries(i)
                    scores(n + 2 * i - 2, 2 * i - 2)
                    if i >= 2:
                        att_out(layer, n + 2 * i - 3, 2 * i - 3)
                    scores(n + 2 * i - 1, 2 * i - 1)
                    keys(i)
                    att_out(layer, n + 2 * i - 2, 2 * i - 2)
                scores(n + 6, 6)
                att_out(layer, n + 5, 5)
                scores(n + 7, 7)
                att_out(layer, n + 6, 6)
                att_out(layer, n + 7, 7)
                if layer == 0:
                    for q in range(QT):
                        pe.wait_ge(S["o_scaled"], q + 1)
                        for half in range(2):
                            transposes([(128 * j, o_tm[:, q, (4 * half + j) * 128:(4 * half + j + 1) * 128])
                                        for j in range(4)])
                else:
                    pe.wait_ge(S["o_done"], 16)
                    to_feature_major(o_tm)
                input_split()
                tokens_out(b + 12, by_tile=True)

            def norm_transposes(i):
                for q in range(QT):
                    pe.wait_ge(S["ln_out"], QT * i + q + 1)
                    for half in range(2):
                        transposes([(128 * j, o_tm[:, q, (4 * half + j) * 128:(4 * half + j + 1) * 128])
                                    for j in range(4)])
                input_split()

            def mlp(layer):
                b = B_MLP[layer]

                def up(o, v, t=None):
                    j = PAIRS * layer + v
                    if v >= 2 or t is not None:
                        pe.wait_ge(S["relu_done"], j - 1 if t is None else t * 2 + (j - 1))
                    features_out(b + o, pp[:, v % 2, :], t)

                def down_part(c, v, q, first=False, final=False):
                    f, half = divmod(c, 2)
                    tok = slice(q * 128, (q + 1) * 128)
                    return product(acc[:, 2 * q + half, :], (hid_hi[:, v % 2, f, tok], hid_lo[:, v % 2, f, tok]),
                                   w_parts(c), start=(first and f == 0), stop=(final and f == 1))

                def down(o, v, t=None, first=False):
                    j = PAIRS * layer + v
                    pe.wait_ge(S["hid_ready"], j + 1 if t is None else t * 2 + (j + 1))
                    for c in range(PARTS):
                        chunk_ready(b + o, c, t, 4 * PARTS)
                        for q in range(QT):
                            last = down_part(c, v, q, first)
                        last.then_inc(S["chunk_used"], 1)

                up(0, 0)
                for v in range(3):
                    up(2 * v + 1, v + 1)
                    if v == 0:
                        pe.wait_ge(S["acc_taken"], 2 * layer + 1)
                    down(2 * v + 2, v, first=(v == 0))
                with pe.Fori(0, 6) as t:
                    for u in range(2):
                        up(7 + 2 * u, 4 + u, t)
                        down(8 + 2 * u, 3 + u, t)
                pe.wait_ge(S["hid_ready"], PAIRS * (layer + 1))
                for c in range(PARTS):
                    chunk_ready(b + 31, c)
                    last = down_part(c, 15, 0, final=True)
                last.then_inc(S["tile_ready"], 1)
                for c in range(PARTS):
                    down_part(c, 15, 1, final=True).then_inc(S["chunk_used"], 1)

            pe.wait_ge(S["consts_in"], 16)
            pe.wait_ge(S["x_in"], 16)
            to_feature_major(h_tm)
            pe.wait_ge(S["relb_in"], 16)
            pe.wait_ge(S["onehot_in"], 16)
            pe.matmul(pp[0:16, 0, :], relb[:, :], onehot, start=True, stop=True).then_inc(S["bias_mm"], 1)
            input_split()

            for layer in range(2):
                attention(layer)
                norm_transposes(2 * layer)
                mlp(layer)
                if layer == 0:
                    norm_transposes(1)

            pe.wait_ge(S["ada_done"], 1)
            pe.wait_ge(S["relu_done"], 2 * PAIRS)
            for part in range(2):
                for j in range(8):
                    at = 1024 * part + 128 * j
                    last = pe.matmul(pp[:, 0, 8 * part + j:8 * part + j + 1], mod[:, at:at + 128],
                                     con("ones")[:, 0:1], start=True, stop=True)
            last.then_inc(S["mod_mm"], 1)

            def mod_rows(part):
                if part:
                    pe.wait_ge(S["mod_done"], 2 * part)
                for half in range(2):
                    at = 2048 + 1024 * part + 512 * half
                    pe.matmul(pp[:, half, :], con("ones"), mod[:, at:at + 512], start=True, stop=True)\
                        .then_inc(S["mod_mm"], 1)

            for q in range(QT):
                pe.wait_ge(S["r_out"], q + 1)
                for half in range(2):
                    transposes([(128 * j, o_tm[:, q, (4 * half + j) * 128:(4 * half + j + 1) * 128])
                                for j in range(4)])
            input_split()
            for i in range(4):
                for j in range(PARTS):
                    k, part = divmod(j, 2)
                    kt = 2 * i + k
                    n = 320 if part else 384
                    chunk_ready(B_C + i, j)
                    for q in range(QT):
                        last = product(acc[:, 2 * q + part, 0:n], x_parts(kt, slice(q * 128, (q + 1) * 128)),
                                       w_parts(j, slice(0, n)), start=(kt == 0), stop=(kt == 7))
                    last.then_inc(S["chunk_used"], 1)
            for h in range(4):
                if h:
                    pe.wait_ge(S["rq_done"], h)
                features_out(B_RQK + 2 * h, pp[:, 0, :])
                if h:
                    pe.wait_ge(S["rk_done"], h)
                features_out(B_RQK + 2 * h + 1, pp[:, 1, :])
            for q in range(QT):
                pe.wait_ge(S["lat_done"], q + 1)
                transposes([(128 * j, lat[:, q, 128 * j:128 * j + 128]) for j in range(3)])
                transposes([(128 * j, lat[:, q, 384 + 128 * j:512 + 128 * j]) for j in range(4)])
            transposed()
            pe.wait_ge(S["rq_done"], 4)
            pe.wait_ge(S["rk_done"], 4)
            for i in range(3):
                arrive(B_UQ + i)
            pe.wait_ge(S["uqr_in"], 16 * 6)
            n = 0

            def uq_bank():
                if n >= 2:
                    pe.wait_ge(S["uq_done"], n - 1)
                return pp[:, n % 2, :]

            for pair in range(6):
                bank = uq_bank()
                for c in range(2):
                    for kt in range(3):
                        at = 128 * (2 * pair + c) if pair < 4 else 1024 + 256 * c + 128 * (pair - 4)
                        lhs = ring[:, slot_of(B_UQ + kt), at:at + 128]
                        last = pe.matmul(bank[:, 256 * c:256 * c + 256], lhs, lat_t[:, kt, :],
                                         start=(kt == 0), stop=(kt == 2))
                last.then_inc(S["uq_ready"], 1)
                n += 1
            arrive(B_UKV)
            for pair in range(4):
                bank = uq_bank()
                for c in range(2):
                    for kt in range(2):
                        if pair == 0 and c == 0 and kt == 1:
                            last.then_inc(S["w_used"], 3)
                            arrive(B_UKV + 1)
                        at = 256 * (2 * pair + c)
                        last = pe.matmul(bank[:, 256 * c:256 * c + 256], ring[:, slot_of(B_UKV + kt), at:at + 128],
                                         lat_t[:, 3 + kt, :], start=(kt == 0), stop=(kt == 1))
                last.then_inc(S["uq_ready"], 1)
                n += 1
            for kt in range(2):
                w = ring[:, slot_of(B_UKV + kt), :].rearrange("p (h c) -> p h c", c=256)
                for q in range(QT):
                    for half in range(2):
                        last = pe.matmul(acc[:, 2 * q + half, :], lat_t[:, 3 + kt, q * 128:(q + 1) * 128],
                                         w[:, 4 * half:4 * half + 4, 128:256], start=(kt == 0), stop=(kt == 1))
            last.then_inc(S["w_used"], 2)
            tokens_out(B_RV, freed="vmla_done")
            pe.wait_ge(S["rv_done"], 1)
            for h in range(4):
                bank = acc[:, h, :]
                for c in range(2):
                    pe.matmul(bank[:, 0:256], k_t[:, 2 * h + c, 0:128], q_t[:, 2 * h + c, :],
                              start=(c == 0), stop=(c == 1))
                for c in range(2):
                    last = pe.matmul(bank[:, 256:384], k_t[:, 2 * h + c, 128:256], q_t[:, 2 * h + c, 128:256],
                                     start=(c == 0), stop=(c == 1))
                last.then_inc(S["sret_ready"], 1)
            for h in range(4):
                pe.wait_ge(S["st_ready"], h + 1)
                cols = slice(256 * h, 256 * h + 256)
                pe.matmul(acc[:, h, 0:256], st_ret[:, h, 0:128], v_tm[:, 0, cols], start=True, stop=True)
                pe.matmul(acc[:, h, 256:512], st_ret[:, h, 128:256], v_tm[:, 0, cols], start=True, stop=False)
                pe.matmul(acc[:, h, 256:512], st_ret[:, h, 256:384], v_tm[:, 1, cols], start=False, stop=True)\
                    .then_inc(S["y_ready"], 1)
            pe.wait_ge(S["y_done"], 4)
            pe.wait_ge(S["uq_done"], 10)

            def mla_scores(c):
                if c >= 2:
                    pe.wait_ge(S["attw_ready"], 16 + c - 1)
                for m in range(2):
                    hd = 2 * c + m
                    a, p = hd // 4, slice(32 * (hd % 4), 32 * (hd % 4) + 32)
                    bank = acc[:, 2 * (c % 2) + m, :]
                    for q in range(QT):
                        out = bank[:, 0:128] if q == 0 else bank[:, 128:384]
                        keys = slice(0, 128 * (q + 1))
                        tok = slice(128 * q, 128 * q + 128)
                        pe.matmul(out, qn_t[:, hd, tok], kn_t[:, hd, keys], start=True, stop=False)
                        pe.matmul(out, pe_rope[p, 2 * a, tok], pe_rope[p, 4, keys], start=False, stop=False)
                        last = pe.matmul(out, pe_rope[p, 2 * a + 1, tok], pe_rope[p, 5, keys],
                                         start=False, stop=True)
                last.then_inc(S["sc_ready"], 1)

            def mla_out(c):
                pe.wait_ge(S["attw_ready"], 16 + c + 1)
                for m in range(2):
                    transposes([(128 * j, prob[:, c % 2, m, 128 * j:128 * j + 128]) for j in range(3)])
                transposed()
                if c >= 2:
                    pe.wait_ge(S["o_done"], 16 + c - 1)
                for q in range(QT):
                    for m in range(2):
                        hd = 2 * c + m
                        out = pp[:, c % 2, 256 * q + 128 * m:256 * q + 128 * m + 128]
                        for kb in range(q + 1):
                            j = 0 if q == 0 else 1 + kb
                            last = pe.matmul(out, prob_t[:, c % 2, m, 128 * j:128 * j + 128],
                                             v_mla[:, kb, 128 * hd:128 * hd + 128], start=(kb == 0), stop=(kb == q))
                last.then_inc(S["o_ready"], 1)

            mla_scores(0)
            mla_scores(1)
            mla_out(0)
            mla_scores(2)
            mla_out(1)
            mla_scores(3)
            mla_out(2)
            mla_out(3)
            tokens_out(B_RG)
            pe.wait_ge(S["o_done"], 20)
            mod_rows(0)
            tokens_out(B_GR, freed="rg_done")
            mod_rows(1)
            tokens_out(B_GM, freed="gr_done")
            mod_rows(2)
            for q in range(QT):
                pe.wait_ge(S["yret_ready"], q + 1)
                tile_to_feature_major(o_tm, q)
            input_split()
            tokens_out(B_RO, freed="gm_done")
            mod_rows(3)
            to_feature_major(o_mla)
            input_split()
            tokens_out(B_MO, freed="ret_merged")
            for q in range(QT):
                pe.wait_ge(S["mla_merged"], q + 1)
                tile_to_feature_major(merged, q)
            input_split()
            tokens_out(B_WO, by_tile=True)

            pe.wait_ge(S["small_in"], 64)
            for q in range(QT):
                pe.wait_ge(S["r_out"], 2 + q + 1)
                tile_to_feature_major(o_tm, q)
                transposed()
                for kt in range(KT):
                    pe.matmul(pp[:, q, 0:36], q_t[:, kt, q * 128:(q + 1) * 128], w_rt[:, kt, :],
                              start=(kt == 0), stop=False)
                last = pe.matmul(pp[:, q, 0:36], con("ones", 1), brow[0:1, 0:36], start=False, stop=True)
            last.then_inc(S["lg_ready"], 1)
            pe.wait_ge(S["y0_done"], 1)
            pe.wait_ge(S["y1_done"], 1)
            pe.wait_ge(S["turned_done"], 1)
            for i in range(2 * QT):
                pe.matmul(acc[:, i, :], turned[:, 0:128], ysb[:, 0:512], start=True, stop=False)
            pe.wait_ge(S["mask_ready"], 1)
            pe.matmul(pp[:, 0, 0:32], con("tri"), picked[:, 0, :], start=True, stop=True)
            pe.matmul(pp[:, 0, 32:64], con("ones"), picked[:, 0, :], start=True, stop=False)
            pe.matmul(pp[:, 0, 32:64], con("tri"), picked[:, 1, :], start=False, stop=True)
            pe.matmul(pp[:, 0, 64:96], con("ones"), picked[:, 0, :], start=True, stop=False)
            pe.matmul(pp[:, 0, 64:96], con("ones"), picked[:, 1, :], start=False, stop=True).then_inc(S["pos_ready"], 1)

            def gather(g):
                for c in range(2):
                    f = slice(256 * g + 128 * c, 256 * g + 128 * c + 128)
                    out = gather_bank[g][:, 256 * c:256 * c + 256]
                    for q in range(QT):
                        pe.matmul(out, u_hi[:, q, f], sel[:, q, :], start=(q == 0), stop=False)
                        last = pe.matmul(out, u_lo[:, q, f], sel[:, q, :], start=False, stop=(q == 1))
                last.then_inc(S["xe_ready"], 1)

            pe.wait_ge(S["u_split"], QT)
            pe.wait_ge(S["sel_ready"], 1)
            for g in range(4):
                if g == 3:
                    pe.wait_ge(S["xe_done"], 1)
                gather(g)
            pe.wait_ge(S["trips_ready"], 1)
            steps = pe.value_load(trips[0:1, 0:1], min_val=STEPS, max_val=ROUNDS * STEPS)

            def combine(half, stop=False):
                for q in range(QT):
                    last = pe.matmul(acc[:, 2 * q + half, :], turned[:, 256 + 128 * q:384 + 128 * q],
                                     ysb[:, 512 * half:512 * half + 512], start=False, stop=stop)
                return last

            with pe.Fori(0, steps) as i:
                for pair in range(2):
                    for w in range(2):
                        for e in range(2):
                            o = 6 * pair + 2 * w + e
                            pe.wait_ge(e_full[o % 6], i * 32 + 16 * (o // 6 + 1))
                            if o == 0:
                                pe.wait_ge(S["xe_done"], i * 4 + 4)
                        for kt in range(KT):
                            for e in range(2):
                                x = slice(128 * pair + 64 * e, 128 * pair + 64 * e + 64)
                                last = pe.matmul(up_bank[64 * e:64 * e + 64, 256 * w:256 * w + 256], xe[:, kt, x],
                                                 e_ring[(6 * pair + 2 * w + e) % 6][:, 256 * kt:256 * kt + 256],
                                                 start=(kt == 0), stop=(kt == KT - 1))
                        last.then_inc(S["e_used"], 2)
                    if pair == 1:
                        pe.wait_ge(S["sel_ready"], i + 2)
                        gather(0)
                    pe.wait_ge(S["y0_done"], i * 2 + (pair + 1))
                    combine(0)
                    if pair == 1:
                        gather(1)
                    pe.wait_ge(S["y1_done"], i * 2 + (pair + 1))
                    combine(1)
                    pe.wait_ge(S["gsel_ready"], i + 1)
                    pe.wait_ge(S["hid_done"], i * 2 + (pair + 1))
                    if pair == 1:
                        pe.wait_ge(S["xe_done"], i * 4 + 5)
                    for f in range(2):
                        pe.transpose(turn_bank[:, 128 * f:128 * f + 128], hid_e[:, 128 * f:128 * f + 128], ident)
                    for q in range(QT):
                        last = pe.transpose(turn_bank[:, 256 + 128 * q:384 + 128 * q], gsel[:, pair, q, :], ident)
                    last.then_inc(S["turn_ready"], 1)
                    if pair == 1:
                        gather(2)
                    pe.wait_ge(S["turned_done"], i * 2 + (pair + 2))
                    for half in range(2):
                        if pair == 1:
                            pe.wait_ge(S["xe_done"], i * 4 + (6 + half))
                        for f in range(2):
                            for e in range(2):
                                o = 6 * pair + 4 + e
                                if half == 0 and f == 0:
                                    pe.wait_ge(e_full[o % 6], i * 32 + 16 * (o // 6 + 1))
                                at = 1024 * f + 512 * half
                                last = pe.matmul(y_bank[half][64 * e:64 * e + 64, :],
                                                 turned[:, 128 * f + 64 * e:128 * f + 64 * e + 64],
                                                 e_ring[o % 6][:, at:at + 512], start=(f == 0), stop=(f == 1))
                        if half == 0:
                            last.then_inc(S["y0_ready"], 1)
                            if pair == 1:
                                gather(3)
                        else:
                            last.then_inc(S["e_used"], 2)
            pe.wait_ge(S["y0_done"], steps * 2 + 1)
            combine(0, stop=True)
            pe.wait_ge(S["y1_done"], steps * 2 + 1)
            combine(1, stop=True).then_inc(S["sums_ready"], 1)

        @block.scalar
        def _(act):
            groups = [0]

            def copied(dsts, scales=None, shifts=None):
                g = groups[0]
                groups[0] += 1
                act.wait_ge(S["tp_ready"], g + 1)
                off = 0
                for i, dst in enumerate(dsts):
                    n = dst.shape[1] if len(dst.shape) == 2 else dst.shape[1] * dst.shape[2]
                    src = tp[:, g % 2, off:off + n]
                    if len(dst.shape) == 3:
                        src = src.rearrange("p (a b) -> p a b", a=dst.shape[1])
                    if scales is None:
                        last = act.activation(dst, src, ACT.Copy)
                    elif shifts is None:
                        last = act.activation(dst, src, ACT.Identity, scale=scales[i])
                    else:
                        last = act.activation(dst, src, ACT.Identity, scale=scales[i], bias=shifts[i])
                    off += n
                last.then_inc(S["tp_done"], 1)

            def to_feature_major(dst, scale=None, shift=None, fast=True):
                for q in range(QT):
                    for half in range(2):
                        fs = range(4 * half, 4 * half + 4)
                        if scale is None:
                            copied([dst[:, 4 * half:4 * half + 4, q * 128:(q + 1) * 128]])
                        else:
                            copied([dst[:, f, q * 128:(q + 1) * 128] for f in fs], [scale(f) for f in fs],
                                   None if shift is None else [shift(f) for f in fs])

            inputs = [0]

            def to_input(scale=None, shift=None):
                for q in range(QT):
                    for half in range(2):
                        n = inputs[0]
                        inputs[0] += 1
                        assert groups[0] == INPUT_AT[n // 4] + n % 4
                        if n >= 2:
                            act.wait_ge(S["x_split"], n - 1)
                        fs = range(4 * half, 4 * half + 4)
                        if scale is None:
                            copied([x_f[:, n % 2, :, :]])
                        else:
                            copied([x_f[:, n % 2, f % 4, :] for f in fs], [scale(f) for f in fs],
                                   None if shift is None else [shift(f) for f in fs])

            def high(b, t=None, n=1):
                for bb in range(b, b + n):
                    full = 16 * (bb // RING + 1)
                    act.wait_ge(w_full[slot_of(bb)], full if t is None else t * 16 + full)
                    for j in range(PARTS):
                        c = PARTS * split_index(bb) + j
                        if c >= PARTS:
                            at = c - PARTS + 1
                            act.wait_ge(S["chunk_used"], at if t is None else t * (4 * PARTS) + at)
                        part = chunk(bb, j)
                        act.activation(split_view(w_hi, j, part), part, ACT.Copy).then_inc(S["hi_ready"], 1)

            def column(name, i=0):
                at = VEC[name][0] + i
                return vec[:, at:at + 1]

            def used(b):
                if is_split(b):
                    act.wait_ge(S["chunk_used"], PARTS * (split_index(b) + 1))
                else:
                    act.wait_ge(S["w_used"], whole_index(b) + 1)

            high(B_ATT[0])
            to_input()
            act.wait_ge(S["bias_mm"], 1)
            act.activation(bias_rows, pp[0:16, 0, :], ACT.Copy).then_inc(S["bias_copied"], 1)

            def exps(n, b):
                act.wait_ge(S["nmax_ready"], n + 1)
                for m in range(2):
                    for q in range(QT):
                        cols = slice(0, 128) if q == 0 else slice(128, 384)
                        last = act.activation(prob[:, b, m, cols], prob[:, b, m, cols], ACT.Exp,
                                              bias=nmax[:, b, 2 * q + m:2 * q + m + 1],
                                              accum_out=esum[:, b, 2 * q + m:2 * q + m + 1])
                last.then_inc(S["exp_done"], 1)

            def attention(layer):
                b = B_ATT[layer]
                high(b + 1, n=4)
                used(b + 3)
                act.activation(v_tm[:, 0, :], acc[:, 0:2, :].rearrange("p a b -> p (a b)"), ACT.Copy)
                act.activation(v_tm[:, 1, :], acc[:, 2:4, :].rearrange("p a b -> p (a b)"), ACT.Copy)\
                    .then_inc(S["v_done"], 1)
                if layer == 0:
                    act.wait_ge(S["vec_mm"], 1)
                    act.activation(vec[:, :], pp[:, 1, 0:128], ACT.Copy).then_inc(S["vec_done"], 1)
                    act.wait_ge(S["vec_done"], 1)
                    at = VEC["c_2"][0]
                    act.activation(act_c[:, :], vec[:, at:at + 8], ACT.Silu).then_inc(S["c_silu"], 1)
                    act.wait_ge(S["lam_ready"], 1)
                    act.activation(lam_s[:, 2:4], lam_s[:, 0:2], ACT.Exp).then_inc(S["lam_exp"], 1)

                def queries(i):
                    used(b + 4 + 2 * i)
                    act.activation(q_t[:, 2 * i:2 * i + 2, :].rearrange("p a b -> p (a b)"), pp[:, 0, :], ACT.Copy)\
                        .then_inc(S["q_done"], 1)

                def out(c):
                    for m in range(1 if layer == 0 else 2):
                        copied([prob_t[:, c % 2, m, :]])
                    if layer == 0:
                        act.wait_ge(S["o_ready"], c + 1)
                        act.activation(o_tm[:, :, 128 * c:128 * c + 128],
                                       acc[:, 2 * (c % 2):2 * (c % 2) + 2, 384:512], ACT.Copy).then_inc(S["o_done"], 1)

                n = 8 * layer
                high(b + 5)
                queries(0)
                high(b + 6)
                for i in range(1, 4):
                    high(b + 5 + 2 * i)
                    queries(i)
                    if i >= 2:
                        out(2 * i - 3)
                    exps(n + 2 * i - 2, 0)
                    exps(n + 2 * i - 1, 1)
                    high(b + 6 + 2 * i)
                    out(2 * i - 2)
                out(5)
                exps(n + 6, 0)
                out(6)
                exps(n + 7, 1)
                out(7)
                if layer == 0:
                    for q in range(QT):
                        act.wait_ge(S["osq_ready"], q + 1)
                        act.activation(rstd[:, :], sr[:, :], ACT.Sqrt).then_inc(S["osq_rstd"], 1)
                    to_input(scale=lambda f: lam_s[:, 1:2])
                else:
                    to_input()
                high(b + 13, n=3)
                high(B_MLP[layer])

            def norm_root(i):
                for q in range(QT):
                    act.wait_ge(S["ln_stat"], QT * i + q + 1)
                    act.activation(rstd[:, q:q + 1], sr[:, q:q + 1], ACT.Sqrt).then_inc(S["ln_rstd"], 1)

            def mlp(layer):
                b = B_MLP[layer]

                def relus(o, v, t=None):
                    j = PAIRS * layer + v
                    at = PARTS * (split_index(b + o) + 1)
                    act.wait_ge(S["chunk_used"], at if t is None else t * (4 * PARTS) + at)
                    if v >= 2 or layer:
                        act.wait_ge(S["hid_ready"], j - 1 if t is None else t * 2 + (j - 1))
                    act.activation(relu[:, v % 2, :], pp[:, v % 2, :], ACT.Relu).then_inc(S["relu_done"], 1)

                high(b + 1)
                relus(0, 0)
                high(b + 2)
                for v in range(1, 3):
                    relus(2 * v - 1, v)
                    high(b + 2 * v + 1)
                    high(b + 2 * v + 2)
                with act.Fori(0, 6) as t:
                    for u in range(2):
                        relus(5 + 2 * u, 3 + u, t)
                        high(b + 7 + 2 * u, t)
                        high(b + 8 + 2 * u, t)
                relus(29, 15)
                high(b + 31)
                high(B_ATT[1] if layer == 0 else B_C)

            def banks_out(dst, function, done):
                for half in range(2):
                    for q in range(QT):
                        act.activation(dst[:, q, 512 * half:512 * half + 512], acc[:, 2 * q + half, :], function)\
                            .then_inc(done, 1)

            def mod_rows(part):
                for half in range(2):
                    at = 2048 + 1024 * part + 512 * half
                    act.wait_ge(S["mod_mm"], 2 * part + half + 2)
                    act.activation(mod[:, at:at + 512], pp[:, half, :], ACT.Copy).then_inc(S["mod_done"], 1)

            for layer in range(2):
                attention(layer)
                norm_root(2 * layer)
                to_input(lambda f: column("ln1_g", 8 * layer + f), lambda f: column("ln1_b", 8 * layer + f))
                mlp(layer)
                norm_root(2 * layer + 1)
                if layer == 0:
                    to_input(lambda f: column("ln2_g", f), lambda f: column("ln2_b", f))

            for q in range(QT):
                act.wait_ge(S["r_stat"], q + 1)
                act.activation(rstd[:, q:q + 1], sr[:, q:q + 1], ACT.Sqrt).then_inc(S["r_rstd"], 1)
            act.wait_ge(S["modc_done"], 1)
            to_input(lambda f: modc[:, 1, f:f + 1], lambda f: modc[:, 0, f:f + 1])
            high(B_C + 1, n=4)
            used(B_C + 3)
            for q in range(QT):
                act.activation(lat[:, q, 0:384], acc[:, 2 * q, 0:384], ACT.Copy)
                act.activation(lat[:, q, 384:640], acc[:, 2 * q + 1, 0:256], ACT.Copy)
                for x in range(2):
                    last = act.activation(lat[:, q, 640 + 128 * x:768 + 128 * x].rearrange("p (r c) -> p r c", r=4),
                                          acc[:, 2 * q + 1, 256 + 32 * x:288 + 32 * x].unsqueeze(1)
                                          .to_broadcast([128, 4, 32]), ACT.Copy)
            last.then_inc(S["lat_copied"], 1)
            act.wait_ge(S["lat_stat"], 1)
            act.activation(rstd[:, 0:4], sr[:, 0:4], ACT.Sqrt).then_inc(S["lat_rstd"], 1)
            high(B_RQK + 1, n=7)
            for q in range(QT):
                tok = slice(q * 128, (q + 1) * 128)
                copied([lat_t[:, j, tok] for j in range(3)], [column("q_norm_2", j) for j in range(3)])
                copied([lat_t[:, 3 + j, tok] for j in range(2)] + [pe_rope[:, 4 + x, tok] for x in range(2)],
                       [column("kv_norm_2", j) for j in range(2)] + [1.0, 1.0])
            assert groups[0] == TP_LATENTS
            for pair in range(4):
                act.wait_ge(S["uq_ready"], pair + 1)
                act.activation(qn_t[:, 2 * pair:2 * pair + 2, :].rearrange("p a b -> p (a b)"), pp[:, pair % 2, :],
                               ACT.Copy).then_inc(S["uq_done"], 1)
            act.wait_ge(S["uq_done"], 6)
            for pair in range(4):
                act.wait_ge(S["uq_ready"], 6 + pair + 1)
                act.activation(kn_t[:, 2 * pair:2 * pair + 2, :].rearrange("p a b -> p (a b)"), pp[:, pair % 2, :],
                               ACT.Copy).then_inc(S["uq_done"], 1)
            used(B_UKV + 1)
            banks_out(v_mla, ACT.Copy, S["vmla_done"])
            high(B_RV, n=5)
            used(B_RV + 3)
            act.activation(v_tm[:, :, :].rearrange("p a b -> p (a b)"), acc[:, :, :].rearrange("p a b -> p (a b)"),
                           ACT.Copy).then_inc(S["rv_done"], 1)
            for h in range(4):
                act.wait_ge(S["y_ready"], h + 1)
                act.activation(o_tm[:, :, 256 * h:256 * h + 256], acc[:, h, :].rearrange("p (a b) -> p a b", a=2),
                               ACT.Copy).then_inc(S["y_done"], 1)
            exps(16, 0)
            exps(17, 1)

            def mla_out(c):
                copied([prob_t[:, c % 2, 0, :]])
                copied([prob_t[:, c % 2, 1, :]])

            mla_out(0)
            exps(18, 0)
            mla_out(1)
            exps(19, 1)
            mla_out(2)
            mla_out(3)
            act.wait_ge(S["hn_stat"], 1)
            act.activation(rstd[:, :], sr[:, :], ACT.Sqrt).then_inc(S["hn_rstd"], 1)
            high(B_RG + 1, n=4)
            used(B_RG + 3)
            banks_out(rg, ACT.Silu, S["rg_done"])
            mod_rows(0)
            high(B_GR + 1, n=4)
            used(B_GR + 3)
            banks_out(gate_r, ACT.Sigmoid, S["gr_done"])
            mod_rows(1)
            high(B_GM + 1, n=4)
            used(B_GM + 3)
            banks_out(gate_m, ACT.Sigmoid, S["gm_done"])
            mod_rows(2)
            to_input()
            high(B_RO + 1, n=4)
            mod_rows(3)
            to_input()
            high(B_MO + 1, n=4)
            to_input()
            high(B_WO + 1, n=3)
            for q in range(QT):
                act.wait_ge(S["r_stat"], 2 + q + 1)
                act.activation(rstd[:, q:q + 1], sr[:, q:q + 1], ACT.Sqrt).then_inc(S["r_rstd"], 1)
            to_feature_major(q_t)
            act.wait_ge(S["lg_max"], 1)
            for q in range(QT):
                last = act.activation(route[:, q, 40:44], route[:, q, 0:4], ACT.Exp, bias=route[:, q, 36:37],
                                      accum_out=route[:, q, 37:38])
            last.then_inc(S["lg_exp"], 1)
            act.wait_ge(S["lg_m2"], 1)
            for q in range(QT):
                last = act.activation(route[:, q, 39:40], route[:, q, 38:39], ACT.Exp)
            last.then_inc(S["lg_e2"], 1)
            act.wait_ge(S["trips_ready"], 1)
            steps = act.value_load(trips[0:1, 0:1], min_val=STEPS, max_val=ROUNDS * STEPS)

            def take_gathered(g):
                act.activation(xe[:, 2 * g:2 * g + 2, :].rearrange("p a b -> p (a b)"), gather_bank[g],
                               ACT.Copy).then_inc(S["xe_done"], 1)

            for g in range(4):
                act.wait_ge(S["xe_ready"], g + 1)
                take_gathered(g)
            with act.Fori(0, steps) as i:
                for pair in range(2):
                    act.wait_ge(S["e_used"], i * 12 + (6 * pair + 4))
                    act.activation(silu_e, up_bank[:, 0:256], ACT.Silu).then_inc(S["silu_done"], 1)
                    if pair == 1:
                        for g in range(2):
                            act.wait_ge(S["xe_ready"], i * 4 + (5 + g))
                            take_gathered(g)
                    act.wait_ge(S["turn_ready"], i * 2 + (pair + 1))
                    act.activation(turned, turn_bank, ACT.Copy).then_inc(S["turned_done"], 1)
                    if pair == 1:
                        act.wait_ge(S["xe_ready"], i * 4 + 7)
                        take_gathered(2)
                    act.wait_ge(S["y0_ready"], i * 2 + (pair + 1))
                    act.activation(ysb[:, 0:512], y_bank[0], ACT.Copy).then_inc(S["y0_done"], 1)
                    if pair == 1:
                        act.wait_ge(S["xe_ready"], i * 4 + 8)
                        take_gathered(3)
            for q in range(QT):
                act.wait_ge(S["r_stat"], 4 + q + 1)
                act.activation(rstd[:, q:q + 1], sr[:, q:q + 1], ACT.Sqrt).then_inc(S["r_rstd"], 1)

        @block.vector
        def _(dve):
            n = [0]

            def link(ins):
                n[0] += 1
                ins.then_inc(S["dve_chain"], 1)
                dve.wait_ge(S["dve_chain"], n[0])

            def column(name, i=0):
                at = VEC[name][0] + i
                return vec[:, at:at + 1]

            def used(b):
                if is_split(b):
                    dve.wait_ge(S["chunk_used"], PARTS * (split_index(b) + 1))
                else:
                    dve.wait_ge(S["w_used"], whole_index(b) + 1)

            inputs = [0]

            input_groups = [g + i for g in INPUT_AT for i in range(4)]

            def split_input():
                for q in range(QT):
                    for half in range(2):
                        n, g = inputs[0], input_groups[inputs[0]]
                        inputs[0] += 1
                        dve.wait_ge(S["tp_done"], g + 1)
                        at = slice(4 * half, 4 * half + 4), slice(q * 128, (q + 1) * 128)
                        link(dve.tensor_copy(x_hi[:, at[0], at[1]], x_f[:, n % 2, :, :]))
                        dve.tensor_tensor(x_lo[:, at[0], at[1]], x_f[:, n % 2, :, :], x_hi[:, at[0], at[1]],
                                          ALU.subtract).then_inc(S["x_split"], 1)

            def low(b, t=None):
                for j in range(PARTS):
                    at = PARTS * split_index(b) + j + 1
                    dve.wait_ge(S["hi_ready"], at if t is None else t * (4 * PARTS) + at)
                    part = chunk(b, j)
                    dve.tensor_tensor(split_view(w_lo, j, part), part, split_view(w_hi, j, part),
                                      ALU.subtract).then_inc(S["lo_dve"], 1)

            low(B_ATT[0])
            split_input()
            for i in range(1, 4):
                low(B_ATT[0] + i)
            dve.wait_ge(S["lam_in"], 16)
            rows = lam_rows[:, :].rearrange("p (a b d) -> p a b d", a=2, b=2)
            link(dve.tensor_tensor(lam_t[:, :, :], rows[:, :, 0, :], rows[:, :, 1, :], ALU.mult))
            dve.tensor_reduce(lam_s[:, 0:2], lam_t[:, :, :], AX.X, ALU.add).then_inc(S["lam_ready"], 1)
            dve.wait_ge(S["lam_exp"], 1)
            link(dve.tensor_tensor(lam_s[:, 0:1], lam_s[:, 3:4], lam_s[:, 2:3], ALU.subtract))
            lam_init = 0.8 - 0.6 * math.exp(-0.3 * 0)
            link(dve.tensor_scalar(lam_s[:, 0:1], lam_s[:, 0:1], -lam_init, None, ALU.add))
            dve.wait_ge(S["vec_done"], 1)
            link(dve.tensor_scalar(lam_s[:, 1:2], column("subln_a"), 1.0 - lam_init, None, ALU.mult))

            def soft_first(k, b, bias_of, scale):
                dve.wait_ge(S["sc_ready"], k + 1)
                if k >= 2:
                    dve.wait_ge(S["o_ready"], k - 1)
                for m in range(2):
                    last = dve.scalar_tensor_tensor(prob[:, b, m, :], acc[:, 2 * b + m, 0:384], scale, bias_of(m),
                                                    ALU.mult, ALU.add)
                link(last)
                dve.tensor_reduce(nmax[:, b, 0:2], prob[:, b, :, 0:128], AX.X, ALU.max)
                link(dve.tensor_reduce(nmax[:, b, 2:4], prob[:, b, :, 128:384], AX.X, ALU.max))
                dve.tensor_scalar(nmax[:, b, :], nmax[:, b, :], -1.0, None, ALU.mult).then_inc(S["nmax_ready"], 1)

            def attention(layer):
                bl = B_ATT[layer]

                def keys(i):
                    used(bl + 5 + 2 * i)
                    dve.tensor_copy(k_t[:, 2 * i:2 * i + 2, :].rearrange("p a b -> p (a b)"), pp[:, 1, :])\
                        .then_inc(S["k_done"], 1)

                def first(c):
                    soft_first(8 * layer + c, c % 2, lambda m: bias[:, 2 * c + m, :], 0.125)

                def second(c):
                    b = c % 2
                    dve.wait_ge(S["exp_done"], 8 * layer + c + 1)
                    if layer == 1:
                        dve.reciprocal(rsum[:, b, :], esum[:, b, :]).then_inc(S["attw_ready"], 1)
                        return
                    link(dve.reciprocal(rsum[:, b, :], esum[:, b, :]))
                    for q in range(QT):
                        r1 = rsum[:, b, 2 * q + 1:2 * q + 2]
                        last = dve.tensor_tensor(r1, r1, lam_s[:, 0:1], ALU.mult)
                    link(last)
                    for q in range(QT):
                        cols = slice(0, 128) if q == 0 else slice(128, 384)
                        last = dve.tensor_scalar(prob[:, b, 0, cols], prob[:, b, 0, cols],
                                                 rsum[:, b, 2 * q:2 * q + 1], None, ALU.mult)
                    link(last)
                    for q in range(QT):
                        cols = slice(0, 128) if q == 0 else slice(128, 384)
                        last = dve.scalar_tensor_tensor(prob[:, b, 0, cols], prob[:, b, 1, cols],
                                                        rsum[:, b, 2 * q + 1:2 * q + 2], prob[:, b, 0, cols],
                                                        ALU.mult, ALU.add)
                    last.then_inc(S["attw_ready"], 1)

                def out(c):
                    if layer == 0:
                        return
                    b = c % 2
                    dve.wait_ge(S["o_ready"], 8 + c + 1)
                    for q in range(QT):
                        for m in range(2):
                            at = 128 * c + 64 * m
                            last = dve.tensor_scalar(o_tm[:, q, at:at + 64],
                                                     acc[:, 2 * b + q, 384 + 64 * m:448 + 64 * m],
                                                     rsum[:, b, 2 * q + m:2 * q + m + 1], None, ALU.mult)
                    last.then_inc(S["o_done"], 1)

                if layer == 1:
                    dve.wait_ge(S["rowsg_in"], 32)
                    dve.wait_ge(S["rowsb_in"], 32)
                    dve.wait_ge(S["ln_out"], 4)
                    gain_rows(2)
                keys(0)
                for i in range(1, 4):
                    if layer == 0 and i == 1:
                        dve.wait_ge(S["bias_in"], 32)
                    first(2 * i - 2)
                    if i >= 2:
                        out(2 * i - 3)
                    second(2 * i - 2)
                    first(2 * i - 1)
                    second(2 * i - 1)
                    keys(i)
                    out(2 * i - 2)
                first(6)
                out(5)
                second(6)
                first(7)
                second(7)
                out(6)
                out(7)
                if layer == 0:
                    dve.wait_ge(S["o_done"], 8)
                    for q in range(QT):
                        o3 = o_tm[:, q, :].rearrange("p (h d) -> p h d", h=8)
                        if q:
                            dve.wait_ge(S["osq_rstd"], q)
                        link(dve.tensor_tensor(stage_sq, o_tm[:, q, :], o_tm[:, q, :], ALU.mult))
                        link(dve.tensor_reduce(sv[:, :], stage_sq.rearrange("p (h d) -> p h d", h=8), AX.X, ALU.add))
                        link(dve.tensor_scalar(sv[:, :], sv[:, :], 1.0 / 128, LN_EPS, ALU.mult, ALU.add))
                        dve.reciprocal(sr[:, :], sv[:, :]).then_inc(S["osq_ready"], 1)
                        dve.wait_ge(S["osq_rstd"], q + 1)
                        dve.tensor_tensor(o3, o3, rstd[:, :].unsqueeze(2).to_broadcast([128, 8, 128]), ALU.mult)\
                            .then_inc(S["o_scaled"], 1)
                split_input()

            stage_sq = scr[:, 0, 0:1024]

            def gain_rows(count):
                for q in range(QT):
                    link(dve.tensor_tensor(h_tm[:, q, :], o_tm[:, q, :], rows_g, ALU.mult))
                    last = dve.tensor_tensor(h_tm[:, q, :], h_tm[:, q, :], rows_b, ALU.add)
                    if q == 0:
                        link(last)
                last.then_inc(S["h_done"], 1)
                dve.wait_ge(S["h_done"], count)

            def row_stats(q, src, eps, done, rms=False):
                for a in range(2):
                    last = dve.bn_stats(st6[:, q, a, :], src[:, 512 * a:512 * a + 512])
                link(last)
                link(dve.bn_aggr(mv[:, q, :], st6[:, q, :, :].rearrange("p a b -> p (a b)")))
                if rms:
                    link(dve.scalar_tensor_tensor(sv[:, q:q + 1], mv[:, q, 0:1], mv[:, q, 0:1], mv[:, q, 1:2],
                                                  ALU.mult, ALU.add))
                    link(dve.tensor_scalar(sv[:, q:q + 1], sv[:, q:q + 1], eps, None, ALU.add))
                else:
                    link(dve.tensor_scalar(sv[:, q:q + 1], mv[:, q, 1:2], eps, None, ALU.add))
                dve.reciprocal(sr[:, q:q + 1], sv[:, q:q + 1]).then_inc(done, 1)

            def layer_norm(i, b):
                if i:
                    dve.wait_ge(S["h_done"], i)

                def rows_sum(q):
                    bank = acc[:, 2 * q:2 * q + 2, :].rearrange("p a b -> p (a b)")
                    return dve.scalar_tensor_tensor(o_tm[:, q, :], h_tm[:, q, :], ALPHA, bank, ALU.mult, ALU.add)

                def normalise(q):
                    dve.wait_ge(S["ln_rstd"], QT * i + q + 1)
                    dve.tensor_scalar(o_tm[:, q, :], o_tm[:, q, :], mv[:, q, 0:1], rstd[:, q:q + 1],
                                      ALU.subtract, ALU.mult).then_inc(S["ln_out"], 1)

                dve.wait_ge(S["tile_ready"], i + 1)
                link(rows_sum(0))
                row_stats(0, o_tm[:, 0, :], LN_EPS, S["ln_stat"])
                used(b)
                rows_sum(1).then_inc(S["acc_taken"], 1)
                normalise(0)
                dve.wait_ge(S["acc_taken"], i + 1)
                row_stats(1, o_tm[:, 1, :], LN_EPS, S["ln_stat"])
                normalise(1)

            def mlp(layer):
                b = B_MLP[layer]

                def square(v, t=None):
                    j = PAIRS * layer + v
                    dve.wait_ge(S["relu_done"], j + 1 if t is None else t * 2 + (j + 1))
                    if v >= 2:
                        at = PARTS * (split_index(b + 2 * (v - 2) + 2) + 1)
                        dve.wait_ge(S["chunk_used"], at if t is None else t * (4 * PARTS) + at)
                    h = relu[:, v % 2, :]
                    hi = hid_hi[:, v % 2, :, :].rearrange("p a b -> p (a b)")
                    dve.tensor_tensor(h, h, h, ALU.mult).then_inc(S["sq_done"], 1)
                    dve.wait_ge(S["sq_done"], 2 * j + 1 if t is None else t * 4 + (2 * j + 1))
                    dve.tensor_copy(hi, h).then_inc(S["sq_done"], 1)
                    dve.wait_ge(S["sq_done"], 2 * j + 2 if t is None else t * 4 + (2 * j + 2))
                    dve.tensor_tensor(hid_lo[:, v % 2, :, :].rearrange("p a b -> p (a b)"), h, hi,
                                      ALU.subtract).then_inc(S["hid_ready"], 1)

                low(b)
                split_input()
                low(b + 1)
                square(0)
                low(b + 2)
                for v in range(1, 3):
                    square(v)
                    low(b + 2 * v + 1)
                    low(b + 2 * v + 2)
                with dve.Fori(0, 6) as t:
                    for u in range(2):
                        square(3 + u, t)
                        low(b + 7 + 2 * u, t)
                        low(b + 8 + 2 * u, t)
                square(15)
                low(b + 31)

            for layer in range(2):
                attention(layer)
                layer_norm(2 * layer, B_ATT[layer] + 15)
                mlp(layer)
                layer_norm(2 * layer + 1, B_MLP[layer] + 31)
                if layer == 0:
                    split_input()

            dve.wait_ge(S["rowsg_in"], 64)
            dve.wait_ge(S["rowsb_in"], 64)
            dve.wait_ge(S["ln_out"], 8)
            gain_rows(4)
            for q in range(QT):
                row_stats(q, h_tm[:, q, :], EPS, S["r_stat"], rms=True)
            for q in range(QT):
                dve.wait_ge(S["r_rstd"], q + 1)
                dve.tensor_scalar(o_tm[:, q, :], h_tm[:, q, :], rstd[:, q:q + 1], None, ALU.mult)\
                    .then_inc(S["r_out"], 1)
            dve.wait_ge(S["mod_mm"], 1)
            link(dve.tensor_copy(modc[:, :, :].rearrange("p a b -> p (a b)"), pp[:, 0, 0:16]))
            at = VEC["norm1_2"][0]
            dve.scalar_tensor_tensor(modc[:, 1, :], modc[:, 1, :], 1.0, vec[:, at:at + 8], ALU.add, ALU.mult)\
                .then_inc(S["modc_done"], 1)
            split_input()

            def rotate(out1, out2, bank, cos, sin, done, count, tmp):
                x = bank.rearrange("p (a b) -> p a b", a=2)
                a = tmp[:, 0, :].rearrange("p (a b) -> p a b", a=2)
                b = tmp[:, 1, :].rearrange("p (a b) -> p a b", a=2)
                dve.tensor_tensor(a, x, cos.unsqueeze(1).to_broadcast([128, 2, 256]), ALU.mult)
                link(dve.tensor_tensor(b, x, sin.unsqueeze(1).to_broadcast([128, 2, 256]), ALU.mult))
                dve.tensor_tensor(out1, a[:, 0, :], b[:, 1, :], ALU.subtract)
                dve.tensor_tensor(out2, a[:, 1, :], b[:, 0, :], ALU.add).then_inc(done, 1)
                dve.wait_ge(done, count)

            tmp = scr[:, 0, 0:1024].rearrange("p (a b) -> p a b", a=2)
            dve.wait_ge(S["late_in"], 16)
            dve.wait_ge(S["lat_copied"], 1)
            for q in range(QT):
                dve.bn_stats(st6[:, q, 0, :], lat[:, q, 0:384])
                last = dve.bn_stats(st6[:, q, 1, :], lat[:, q, 384:640])
            link(last)
            for q in range(QT):
                for a in range(2):
                    last = dve.bn_aggr(mv[:, 2 * q + a, :], st6[:, q, a, :])
            link(last)
            link(dve.tensor_tensor(sv[:, 0:4], mv[:, 0:4, 0], mv[:, 0:4, 0], ALU.mult))
            link(dve.scalar_tensor_tensor(sv[:, 0:4], sv[:, 0:4], EPS, mv[:, 0:4, 1], ALU.add, ALU.add))
            dve.reciprocal(sr[:, 0:4], sv[:, 0:4]).then_inc(S["lat_stat"], 1)
            dve.wait_ge(S["lat_rstd"], 1)
            for q in range(QT):
                dve.tensor_scalar(lat[:, q, 0:384], lat[:, q, 0:384], rstd[:, 2 * q:2 * q + 1], None, ALU.mult)
                dve.tensor_scalar(lat[:, q, 384:640], lat[:, q, 384:640], rstd[:, 2 * q + 1:2 * q + 2], None,
                                  ALU.mult).then_inc(S["lat_done"], 1)
            for h in range(4):
                used(B_RQK + 2 * h)
                rotate(q_t[:, 2 * h, :], q_t[:, 2 * h + 1, :], pp[:, 0, :], con("cos_ret"), con("sin_ret"),
                       S["rq_done"], h + 1, tmp)
                used(B_RQK + 2 * h + 1)
                rotate(k_t[:, 2 * h, :], k_t[:, 2 * h + 1, :], pp[:, 1, :], con("cos_ret"), con("sin_ret"),
                       S["rk_done"], h + 1, tmp)
            dve.wait_ge(S["tp_done"], TP_LATENTS)
            rotate(pe_rope[:, 4, :], pe_rope[:, 5, :], pe_rope[:, 4:6, :].rearrange("p a b -> p (a b)"),
                   con("cos_mla"), con("sin_mla"), S["kpe_done"], 1, tmp)
            for a in range(2):
                dve.wait_ge(S["uq_ready"], 4 + a + 1)
                dve.wait_ge(S["uq_done"], 4 + a)
                rotate(pe_rope[:, 2 * a, :], pe_rope[:, 2 * a + 1, :], pp[:, a, :], con("cos_mla"), con("sin_mla"),
                       S["uq_done"], 5 + a, tmp)
            for h in range(4):
                dve.wait_ge(S["sret_ready"], h + 1)
                decay = con("decay")[:, 256 * h:256 * h + 256]
                link(dve.tensor_tensor(st_ret[:, h, 0:256], acc[:, h, 0:256], decay, ALU.mult))
                dve.tensor_tensor(st_ret[:, h, 256:384], acc[:, h, 256:384], decay[:, 0:128], ALU.mult)\
                    .then_inc(S["st_ready"], 1)

            def second(c):
                dve.wait_ge(S["exp_done"], 16 + c + 1)
                dve.reciprocal(rsum[:, c % 2, :], esum[:, c % 2, :]).then_inc(S["attw_ready"], 1)

            def out(c):
                dve.wait_ge(S["o_ready"], 16 + c + 1)
                for q in range(QT):
                    for m in range(2):
                        at = 256 * c + 128 * m
                        last = dve.tensor_scalar(o_mla[:, q, at:at + 128],
                                                 pp[:, c % 2, 256 * q + 128 * m:256 * q + 128 * m + 128],
                                                 rsum[:, c % 2, 2 * q + m:2 * q + m + 1], None, ALU.mult)
                last.then_inc(S["o_done"], 1)

            def first(c):
                soft_first(16 + c, c % 2, lambda m: con("mask"), MLA_SCALE)

            first(0)
            first(1)
            second(0)
            second(1)
            out(0)
            first(2)
            second(2)
            out(1)
            first(3)
            second(3)
            out(2)
            out(3)
            dve.wait_ge(S["y_done"], 4)
            for q in range(QT):
                for h in range(4):
                    last = dve.bn_stats(st6[:, 4 * q + h, 0, :], o_tm[:, q, 256 * h:256 * h + 256])
            link(last)
            for j in range(8):
                last = dve.bn_aggr(mv[:, j, :], st6[:, j, 0, :])
            link(last)
            link(dve.tensor_scalar(sv[:, :], mv[:, :, 1], EPS, None, ALU.add))
            dve.reciprocal(sr[:, :], sv[:, :]).then_inc(S["hn_stat"], 1)
            dve.wait_ge(S["hn_rstd"], 1)
            for q in range(QT):
                for h in range(4):
                    j = 4 * q + h
                    cols = slice(256 * h, 256 * h + 256)
                    last = dve.tensor_scalar(o_tm[:, q, cols], o_tm[:, q, cols], mv[:, j, 0:1], rstd[:, j:j + 1],
                                             ALU.subtract, ALU.mult)
            link(last)
            dve.wait_ge(S["rg_done"], 4)
            for q in range(QT):
                dve.tensor_tensor(o_tm[:, q, :], o_tm[:, q, :], rg[:, q, :], ALU.mult).then_inc(S["yret_ready"], 1)
            split_input()
            used(B_RO + 3)
            dve.wait_ge(S["gr_done"], 4)
            for half in range(2):
                for q in range(QT):
                    cols = slice(512 * half, 512 * half + 512)
                    dve.tensor_tensor(merged[:, q, cols], acc[:, 2 * q + half, :], gate_r[:, q, cols], ALU.mult)\
                        .then_inc(S["ret_merged"], 1)
            split_input()
            dve.wait_ge(S["mod_done"], 8)
            dve.wait_ge(S["rowsg_in"], 80)
            link(dve.scalar_tensor_tensor(mod[:, 4096:5120], mod[:, 4096:5120], 1.0, rows_g, ALU.add, ALU.mult))
            used(B_MO + 3)
            dve.wait_ge(S["gm_done"], 4)
            dve.wait_ge(S["ret_merged"], 4)
            for q in range(QT):
                bank = acc[:, 2 * q:2 * q + 2, :].rearrange("p a b -> p (a b)")
                link(dve.tensor_tensor(gate_m[:, q, :], bank, gate_m[:, q, :], ALU.mult))
                dve.tensor_tensor(merged[:, q, :], merged[:, q, :], gate_m[:, q, :], ALU.add)\
                    .then_inc(S["mla_merged"], 1)
            split_input()

            def residual(q):
                bank = acc[:, 2 * q:2 * q + 2, :].rearrange("p a b -> p (a b)")
                link(dve.tensor_tensor(o_tm[:, q, :], bank, mod[:, 2048:3072], ALU.mult))
                link(dve.tensor_tensor(h_tm[:, q, :], h_tm[:, q, :], o_tm[:, q, :], ALU.add))

            def modulate(q):
                dve.wait_ge(S["r_rstd"], 2 + q + 1)
                link(dve.scalar_tensor_tensor(o_tm[:, q, :], h_tm[:, q, :], rstd[:, q:q + 1], mod[:, 4096:5120],
                                              ALU.mult, ALU.mult))
                dve.tensor_tensor(o_tm[:, q, :], o_tm[:, q, :], mod[:, 3072:4096], ALU.add).then_inc(S["r_out"], 1)

            dve.wait_ge(S["tile_ready"], 5)
            residual(0)
            row_stats(0, h_tm[:, 0, :], EPS, S["r_stat"], rms=True)
            used(B_WO + 3)
            residual(1)
            modulate(0)
            row_stats(1, h_tm[:, 1, :], EPS, S["r_stat"], rms=True)
            modulate(1)
            dve.wait_ge(S["r_out"], 4)
            for q in range(QT):
                link(dve.tensor_copy(u_hi[:, q, :], o_tm[:, q, :]))
                dve.tensor_tensor(u_lo[:, q, :], o_tm[:, q, :], u_hi[:, q, :], ALU.subtract).then_inc(S["u_split"], 1)

            dve.wait_ge(S["lg_ready"], 1)
            link(dve.tensor_copy(route[:, :, 0:36], pp[:, :, 0:36]))
            link(dve.tensor_reduce(route[:, :, 36:37], route[:, :, 0:4], AX.X, ALU.max))
            dve.tensor_scalar(route[:, :, 36:37], route[:, :, 36:37], -1.0, None, ALU.mult).then_inc(S["lg_max"], 1)
            dve.wait_ge(S["lg_max"], 1)
            dve.wait_ge(S["lg_exp"], 1)

            def both(step):
                for q in range(QT):
                    last = step(route[:, q, :], router[:, q, :], q)
                link(last)

            def first_max(out, src, width, top):
                order = con("order")[:, 0:width]

                def at(w):
                    return w[:, out:out + width]

                both(lambda r, w, q: dve.tensor_reduce(w[:, top:top + 1], src(r, w), AX.X, ALU.max))
                both(lambda r, w, q: dve.scalar_tensor_tensor(at(w), src(r, w), w[:, top:top + 1], order,
                                                              ALU.is_equal, ALU.mult))
                both(lambda r, w, q: dve.tensor_reduce(w[:, 34:35], at(w), AX.X, ALU.max))
                both(lambda r, w, q: dve.tensor_scalar(at(w), at(w), w[:, 34:35], None, ALU.is_equal))

            def picks(w):
                return w[:, 0:4].unsqueeze(2).to_broadcast([128, 4, 8])

            def prods(w):
                return w[:, 48:80].rearrange("p (g e) -> p g e", g=4)

            first_max(0, lambda r, w: r[:, 0:4], 4, 32)
            both(lambda r, w, q: dve.tensor_tensor(prods(w), r[:, 4:36].rearrange("p (g e) -> p g e", g=4), picks(w),
                                                   ALU.mult))
            both(lambda r, w, q: dve.tensor_reduce(w[:, 8:16], prods(w).rearrange("p g e -> p e g"), AX.X, ALU.add))
            first_max(16, lambda r, w: w[:, 8:16], 8, 32)
            both(lambda r, w, q: dve.scalar_tensor_tensor(w[:, 40:48], w[:, 16:24], NEG, w[:, 8:16],
                                                          ALU.mult, ALU.add))
            first_max(24, lambda r, w: w[:, 40:48], 8, 33)
            for q in range(QT):
                w = router[:, q, :]
                last = dve.tensor_tensor(route[:, q, 38:39], w[:, 33:34], w[:, 32:33], ALU.subtract)
            last.then_inc(S["lg_m2"], 1)
            both(lambda r, w, q: dve.tensor_tensor(w[:, 8:16], w[:, 16:24], w[:, 24:32], ALU.add))
            for q in range(QT):
                w = router[:, q, :]
                m3 = picked[:, q, :].rearrange("p (g e) -> p g e", g=4)
                last = dve.tensor_tensor(m3, picks(w), w[:, 8:16].unsqueeze(1).to_broadcast([128, 4, 8]), ALU.mult)
            last.then_inc(S["mask_ready"], 1)
            dve.wait_ge(S["lg_e2"], 1)
            both(lambda r, w, q: dve.reciprocal(w[:, 35:36], r[:, 37:38]))
            both(lambda r, w, q: dve.tensor_scalar(w[:, 36:37], r[:, 39:40], 1.0, None, ALU.add))
            both(lambda r, w, q: dve.reciprocal(w[:, 36:37], w[:, 36:37]))
            both(lambda r, w, q: dve.tensor_tensor(w[:, 36:37], w[:, 36:37], w[:, 35:36], ALU.mult))
            both(lambda r, w, q: dve.tensor_tensor(w[:, 37:38], w[:, 36:37], r[:, 39:40], ALU.mult))
            both(lambda r, w, q: dve.tensor_scalar(w[:, 40:48], w[:, 24:32], w[:, 37:38], None, ALU.mult))
            both(lambda r, w, q: dve.scalar_tensor_tensor(w[:, 40:48], w[:, 16:24], w[:, 36:37], w[:, 40:48],
                                                          ALU.mult, ALU.add))
            both(lambda r, w, q: dve.tensor_tensor(gates[:, q, :].rearrange("p (g e) -> p g e", g=4), picks(w),
                                                   w[:, 40:48].unsqueeze(1).to_broadcast([128, 4, 8]), ALU.mult))
            dve.wait_ge(S["pos_ready"], 1)
            pos = pp[:, 0, 0:64].rearrange("p (q e) -> p q e", q=2)
            link(dve.scalar_tensor_tensor(posn[:, :, :], pos, 1.0, picked[:, :, :], ALU.add, ALU.mult))
            link(dve.tensor_scalar(posn[:, :, :], posn[:, :, :], -1.0, None, ALU.add))
            link(dve.tensor_reduce(cnt[:, 0:1], pp[:, 0, 64:96], AX.X, ALU.max))
            for r in range(1, ROUNDS):
                link(dve.tensor_scalar(cnt[:, r:r + 1], cnt[:, 0:1], float(SLOTS * r), None, ALU.is_gt))
            link(dve.tensor_reduce(cnt[:, 4:5], cnt[:, 1:4], AX.X, ALU.add))
            link(dve.tensor_scalar(cnt[:, 4:5], cnt[:, 4:5], 1.0, None, ALU.add))
            link(dve.tensor_scalar(cnt[:, 5:6], cnt[:, 4:5], float(STEPS), None, ALU.mult))
            link(dve.tensor_copy(trips[:, 1:2], cnt[:, 4:5]))
            dve.tensor_copy(trips[:, 0:1], cnt[:, 5:6]).then_inc(S["trips_ready"], 1)
            dve.wait_ge(S["trips_ready"], 1)
            link(dve.memset(plan[:, ROUNDS * STEPS, :], -1.0))
            for r in range(ROUNDS):
                part = plan[:, r * STEPS:(r + 1) * STEPS, :].rearrange("p s (w q e) -> p s w q e", w=2, q=2)
                for q in range(QT):
                    src = posn[:, q, :].rearrange("p (s e) -> p s e", e=4)
                    dve.tensor_scalar(part[:, :, 0, q, :], src, float(-SLOTS * r), None, ALU.add)
                    last = dve.tensor_copy(part[:, :, 1, q, :], gates[:, q, :].rearrange("p (s e) -> p s e", e=4))
                link(last)
            steps = dve.value_load(trips[0:1, 0:1], min_val=STEPS, max_val=ROUNDS * STEPS)
            iota = con("iota")

            def select():
                for q in range(QT):
                    for e in range(4):
                        last = dve.tensor_scalar(sel[:, q, 64 * e:64 * e + 64], iota,
                                                 now[:, 4 * q + e:4 * q + e + 1], None, ALU.is_equal)
                last.then_inc(S["sel_ready"], 1)

            link(dve.tensor_copy(now[:, :], plan[:, 0, :]))
            select()
            base = n[0]
            with dve.Fori(0, steps) as i:
                for pair in range(2):
                    for q in range(QT):
                        for e in range(2):
                            at = 4 * q + 2 * pair + e
                            last = dve.tensor_scalar(gsel[:, pair, q, 64 * e:64 * e + 64], iota, now[:, at:at + 1],
                                                     now[:, 8 + at:9 + at], ALU.is_equal, ALU.mult)
                last.then_inc(S["gsel_ready"], 1)
                dve.wait_ge(S["gsel_ready"], i + 1)
                dve.tensor_copy(now[:, :], plan[:, bass.ds(i + 1, 1), :].rearrange("p a b -> p (a b)"))\
                    .then_inc(S["dve_chain"], 1)
                dve.wait_ge(S["dve_chain"], i + (base + 1))
                dve.wait_ge(S["xe_ready"], i * 4 + 4)
                select()
                for pair in range(2):
                    dve.wait_ge(S["silu_done"], i * 2 + (pair + 1))
                    dve.tensor_tensor(hid_e, silu_e, up_bank[:, 256:512], ALU.mult).then_inc(S["hid_done"], 1)
                    dve.wait_ge(S["e_used"], i * 12 + (6 * pair + 6))
                    dve.tensor_copy(ysb[:, 512:1024], y_bank[1]).then_inc(S["y1_done"], 1)
            dve.wait_ge(S["rowsb_in"], 80)
            dve.wait_ge(S["sums_ready"], 1)
            for q in range(QT):
                sums = acc[:, 2 * q:2 * q + 2, :].rearrange("p a b -> p (a b)")
                dve.tensor_tensor(moe[:, q, :], sums, mod[:, 5120:6144], ALU.mult).then_inc(S["moe_g"], 1)
                dve.wait_ge(S["moe_g"], 2 * q + 1)
                dve.tensor_tensor(h_tm[:, q, :], h_tm[:, q, :], moe[:, q, :], ALU.add).then_inc(S["moe_g"], 1)
                dve.wait_ge(S["moe_g"], 2 * q + 2)
            fin = [0]

            def flink(ins):
                fin[0] += 1
                ins.then_inc(S["final_chain"], 1)
                dve.wait_ge(S["final_chain"], fin[0])

            for q in range(QT):
                for a in range(2):
                    last = dve.bn_stats(st6[:, q, a, :], h_tm[:, q, 512 * a:512 * a + 512])
                flink(last)
                flink(dve.bn_aggr(mv[:, q, :], st6[:, q, :, :].rearrange("p a b -> p (a b)")))
                flink(dve.scalar_tensor_tensor(sv[:, q:q + 1], mv[:, q, 0:1], mv[:, q, 0:1], mv[:, q, 1:2],
                                               ALU.mult, ALU.add))
                flink(dve.tensor_scalar(sv[:, q:q + 1], sv[:, q:q + 1], EPS, None, ALU.add))
                dve.reciprocal(sr[:, q:q + 1], sv[:, q:q + 1]).then_inc(S["r_stat"], 1)
            for q in range(QT):
                dve.wait_ge(S["r_rstd"], 4 + q + 1)
                dve.scalar_tensor_tensor(h_tm[:, q, :], h_tm[:, q, :], rstd[:, q:q + 1], rows_b,
                                         ALU.mult, ALU.mult).then_inc(S["out_ready"], 1)


def constant_tables():
    f = np.float32
    t = {"ident": np.eye(128, dtype=f)}
    pos = np.arange(SEQ, dtype=f)

    def rope(dim, copies):
        inv = (f(10000.0) ** (-np.arange(0, dim, 2, dtype=f) / f(dim))).astype(f)
        angle = pos[None, :] * inv[:, None]
        return [np.tile(fn(angle.astype(f)).astype(f), (copies, 1)) for fn in (np.cos, np.sin)]

    t["cos_ret"], t["sin_ret"] = rope(256, 1)
    t["cos_mla"], t["sin_mla"] = rope(64, 4)
    log_gamma = np.log1p(-np.exp2(-5.0 - np.arange(4, dtype=f))).astype(f)
    rel = np.arange(SEQ, dtype=f)[None, :] - np.arange(128, dtype=f)[:, None]
    decay = [np.where(rel >= 0, np.exp(g * np.maximum(rel, 0)), 0) * 256 ** -0.5 for g in log_gamma]
    t["decay"] = np.concatenate(decay, axis=1)
    i = np.arange(128)
    t["tri"] = (i[:, None] < i[None, :]).astype(f)
    t["ones"] = np.ones((128, 128), f)
    t["iota"] = np.tile(np.arange(64, dtype=f), (128, 1))
    k = np.arange(SEQ)
    t["mask"] = np.concatenate([np.where(k[None, :128] > i[:, None], NEG, 0),
                                np.where(k[None, :] > 128 + i[:, None], NEG, 0)], axis=1)
    t["order"] = np.tile(100.0 - np.arange(8), (128, 1))
    table = np.concatenate([t[name].astype(f) for name, _ in CONST_WIDTHS], axis=1)
    late = np.ascontiguousarray(np.concatenate([t[name].astype(f) for name, _ in LATE_WIDTHS], axis=1))
    n = 255 - np.arange(512)
    nf = np.maximum(n, 16).astype(f)
    large = 16 + (np.log(nf / f(16)) / f(math.log(128 / 16)) * f(16)).astype(np.int32)
    bucket = np.where(n < 0, 32, np.where(n < 16, n, np.minimum(large, 31)))
    onehot = (np.arange(33)[:, None] == bucket[None, :]).astype(f)
    return np.ascontiguousarray(table), late, onehot


_INS = ["x", "w_in_a", "lam_a", "subln_a", "w_out_a", "w_kv_shared", "w_q_b", "w_out_b", "rel_bias", "ln1_g", "ln1_b",
        "ln2_g", "ln2_b", "w_up", "w_down", "c_2", "w_ada_2", "b_ada_2", "norm1_2", "norm2_2", "w_in_2", "w_ret_o_2",
        "q_norm_2", "kv_norm_2", "w_uq_2", "w_ukv_2", "w_mla_o_2", "w_out_2", "w_grp_2", "b_grp_2", "w_exp_2",
        "b_exp_2", "w1_2", "w3_2", "w2_2", "final_norm_2"]


def kernel(**inputs):
    import concourse.bacc as _bacc
    from concourse.bass_utils import run_bass_kernel_spmd as _run

    nc = _bacc.Bacc("TRN2", target_bir_lowering=False, num_devices=1)
    arrays, aps = {}, {}
    given = {name: np.ascontiguousarray(inputs[name]) for name in _INS}
    given["consts"], given["late"], given["onehot"] = constant_tables()
    for name, a in given.items():
        arrays[f"in_{name}_dram"] = a
        aps[name] = nc.dram_tensor(f"in_{name}_dram", a.shape, mybir.dt.from_np(a.dtype), kind="ExternalInput").ap()
    aps["bias_dram"] = nc.dram_tensor("bias_dram", (16, 128, 512), mybir.dt.float32, kind="Internal").ap()
    aps["out"] = nc.dram_tensor("out_dram", (1, SEQ, D), mybir.dt.float32, kind="ExternalOutput").ap()
    program(nc, aps)
    r = _run(nc, [arrays], core_ids=[0])
    return r.results[0]["out_dram"]
```

```python
import math
from contextlib import ExitStack

import numpy as np

import concourse.bass as bass
from concourse import mybir

D = 1024
KT = D // 128
SEQ = 256
QT = SEQ // 128
D_FF = 4096
PAIRS = D_FF // 256
RING = 4
CHUNK = 512
PARTS = 4
EXPERTS = 32
SLOTS = 64
ROUNDS = SEQ // SLOTS
STEPS = EXPERTS // 4
ALPHA = (2 * 2) ** 0.25
NEG = -1e30
LN_EPS = 1e-5
EPS = 1e-6
MLA_SCALE = (128 + 64) ** -0.5

CONST_WIDTHS = [("ident", 128), ("tri", 128), ("ones", 128), ("iota", 64), ("mask", 384), ("order", 8)]
LATE_WIDTHS = [("cos_ret", 256), ("sin_ret", 256), ("cos_mla", 256), ("sin_mla", 256), ("decay", 1024)]
CONST_AT = {}
_at = 0
for _name, _w in CONST_WIDTHS:
    CONST_AT[_name] = (_at, _at + _w)
    _at += _w
CONST_COLS = _at
LATE_AT = {}
_at = 0
for _name, _w in LATE_WIDTHS:
    LATE_AT[_name] = (_at, _at + _w)
    _at += _w

VEC = {}
_at = 0
for _name, _rows in [("ln1_g", 16), ("ln1_b", 16), ("ln2_g", 16), ("ln2_b", 16), ("norm1_2", 8), ("norm2_2", 8),
                     ("q_norm_2", 3), ("kv_norm_2", 2), ("subln_a", 1), ("c_2", 8)]:
    VEC[_name] = (_at, _rows)
    _at += _rows
VEC_ROWS = _at

B_ATT = [0, 48]
B_MLP = [16, 64]
B_C = 96
B_RQK = 100
B_UQ = 102
B_UKV = 105
B_RV = 112
B_RG = 116
B_GR = 120
B_GM = 124
B_RO = 128
B_MO = 132
B_WO = 136
B_MOE = 140
PLAIN = [0, 1, 2, 3, 10, 11, 13, 15, 36, 37, 40, 43] + list(range(64, 76))
SHIFTED_AT = [16, 20, 44, 48]
TP_LATENTS = 56


def is_split(b):
    return b < B_UQ or B_UKV < b < B_MOE


def slot_of(b):
    return b % RING


def split_index(b):
    return b if b < B_UQ else b - 4


def rqk_block(i):
    return B_RQK + i if i < 2 else B_UKV + i - 1


def whole_index(b):
    return b - B_UQ


def low_by_vector(b):
    return b < B_ATT[0] + 4 or any(a < b < a + 32 for a in B_MLP)


def low_index(b):
    n = sum(low_by_vector(x) for x in range(b))
    return n if low_by_vector(b) else split_index(b) - n


def program(nc, A):
    f32, i32, f32r = mybir.dt.float32, mybir.dt.int32, mybir.dt.float32r
    ALU, ACT, AX = mybir.AluOpType, mybir.ActivationFunctionType, mybir.AxisListType
    ctx = ExitStack()
    with ctx:
        def sb(name, shape, dt=f32):
            return ctx.enter_context(nc.sbuf_tensor(name, shape, dt))

        consts = sb("consts", [128, CONST_COLS])
        ring = sb("ring", [128, RING, 2048])
        h_tm = sb("h_tm", [128, QT, D])
        x_hi = sb("x_hi", [128, KT, SEQ], f32r)
        x_lo = sb("x_lo", [128, KT, SEQ], f32r)
        w_hi = sb("w_hi", [128, PARTS, CHUNK], f32r)
        w_lo = sb("w_lo", [128, PARTS, CHUNK], f32r)
        hid_hi = sb("hid_hi", [128, 2, 2, SEQ], f32r)
        hid_lo = sb("hid_lo", [128, 2, 2, SEQ], f32r)
        v_tm = sb("v_tm", [128, QT, D])
        q_t = sb("q_t", [128, KT, SEQ])
        k_t = sb("k_t", [128, KT, SEQ])
        o_tm = sb("o_tm", [128, QT, D])
        big = sb("big", [128, 6144])
        scr = sb("scr", [128, 2, 1536])
        mod = sb("mod", [128, 6144])
        stage = sb("stage", [128, 2, 1024])
        rows = sb("rows", [128, 2, 1024])
        rows_g, rows_b = rows[:, 0, :], rows[:, 1, :]
        pe_rope = rows[:, :, :].rearrange("p a b -> p (a b)")[:, 0:1536].rearrange("p (a t) -> p a t", a=6)
        vec_rows = sb("vec_rows", [128, 128])
        vec = sb("vec", [128, 128])
        modc = sb("modc", [128, 2, 8])
        relb = sb("relb", [33, 16])
        bias_rows = stage[0:16, 0, 0:512]
        onehot = stage[0:33, 1, 0:512]
        lam_rows = sb("lam_rows", [128, 256])
        lam_t = sb("lam_t", [128, 2, 64])
        lam_s = sb("lam_s", [128, 4])
        act_c = sb("act_c", [128, 8])
        brow = sb("brow", [1, 64])
        w_rt = sb("w_rt", [128, KT, 36])
        st6 = sb("st6", [128, 8, 2, 6])
        mv = sb("mv", [128, 8, 2])
        sv = sb("sv", [128, 8])
        sr = sb("sr", [128, 8])
        rstd = sb("rstd", [128, 8])
        head_ms = sb("head_ms", [128, QT, 8])
        head_rstd = sb("head_rstd", [128, QT, 8])
        nmax = sb("nmax", [128, 2, 4])
        esum = sb("esum", [128, 2, 4])
        rsum = sb("rsum", [128, 2, 4])

        def con(name, rows=128):
            if name in LATE_AT:
                a, b = LATE_AT[name]
                return stage[:, :, :].rearrange("p a b -> p (a b)")[:, a:b]
            a, b = CONST_AT[name]
            return consts[0:rows, a:b]

        ident = con("ident")
        bias = big[:, :].rearrange("p (h k) -> p h k", h=16)
        prob = scr[:, 0, :].rearrange("p (b m k) -> p b m k", b=2, m=2)
        prob_t = scr[:, 1, :].rearrange("p (b m k) -> p b m k", b=2, m=2)
        relu = scr[:, 0, 0:1024].rearrange("p (b n) -> p b n", b=2)
        x_f = scr[:, 1, 0:1024].rearrange("p (b c n) -> p b c n", b=2, c=4)
        qn_t = big[:, 0:2048].rearrange("p (h t) -> p h t", h=8)
        kn_t = big[:, 2048:4096].rearrange("p (h t) -> p h t", h=8)
        v_mla = big[:, 4096:6144].rearrange("p (q n) -> p q n", q=2)
        ukv = (ring[:, slot_of(B_UKV), :], big[:, 4096:6144])
        rg = big[:, 0:2048].rearrange("p (q n) -> p q n", q=2)
        gate_r = big[:, 2048:4096].rearrange("p (q n) -> p q n", q=2)
        gate_m = big[:, 4096:6144].rearrange("p (q n) -> p q n", q=2)
        merged = q_t[:, :, :].rearrange("p (q a) t -> p q (a t)", q=2)
        lat = o_tm[:, :, 0:896]
        lat_t = scr[:, 1, 0:1280].rearrange("p (c t) -> p c t", c=5)
        st_ret = scr[:, 0, :].rearrange("p (h k) -> p h k", h=4)
        o_mla = mod[:, 0:2048].rearrange("p (q n) -> p q n", q=2)

        xe = k_t
        u_hi = x_hi[:, :, :].rearrange("p (q a) t -> p q (a t)", q=2)
        u_lo = x_lo[:, :, :].rearrange("p (q a) t -> p q (a t)", q=2)
        sel = sb("sel", [128, QT, 4 * SLOTS], f32r)
        room = [0, 0]

        def carve(part, *dims):
            size = math.prod(dims)
            at = room[part]
            room[part] += size
            assert room[part] <= 1536
            names = "abc"[:len(dims)]
            piece = scr[:, part, at:at + size]
            if len(dims) == 1:
                return piece
            pattern = f"p ({' '.join(names)}) -> p {' '.join(names)}"
            return piece.rearrange(pattern, **dict(zip(names[:-1], dims[:-1])))

        gsel = carve(0, 2, QT, 128)
        hid_e = carve(0, 256)
        silu_e = carve(0, 256)
        turned = carve(0, 512)
        y_hi, y_lo, place_t = w_hi[:, 0:2, :], w_lo[:, 0:2, :], hid_hi[:, 0, 0, :]
        e_ring = [v_tm[:, :, :].rearrange("p a b -> p (a b)"), stage[:, :, :].rearrange("p a b -> p (a b)"),
                  mod[:, 0:2048], big[:, 0:2048], big[:, 2048:4096], big[:, 4096:6144]]
        e_ring += [ring[:, slot_of(B_WO + i), :] for i in range(4)]
        e_ring += [o_tm[:, :, :].rearrange("p a b -> p (a b)"), q_t[:, :, :].rearrange("p a b -> p (a b)")]
        plan = carve(1, ROUNDS * STEPS + 1, 16)
        route = carve(1, QT, 64)
        router = carve(1, QT, 80)
        gates, picked, posn = (carve(1, QT, EXPERTS) for _ in range(3))
        now = sb("now", [128, 16])
        slot_gate = sb("slot_gate", [128, 1])
        warm = sb("warm", [128, 1])
        cnt = sb("cnt", [128, 8])
        trips = sb("trips", [128, 2], i32)

        moe = v_tm

        def halves_of_tiles():
            return [(slice(4 * half, 4 * half + 4), slice(q * 128, (q + 1) * 128)) for q in range(QT)
                    for half in range(2)]

        def quarter(g):
            return slice(2 * g, 2 * g + 2), slice(0, SEQ)

        def head_bank(c, m):
            return pp[:, m, :] if c >= 6 else acc[:, 2 * (c % 2) + m, :]

        acc = ctx.enter_context(nc.psum_tensor("acc", [128, 4, 512], f32))
        pp = ctx.enter_context(nc.psum_tensor("pp", [128, 2, 512], f32))
        tp = ctx.enter_context(nc.psum_tensor("tp", [128, 2, 512], f32))

        up_bank, turn_bank, y_bank = pp[:, 0, :], pp[:, 1, :], (tp[:, 0, :], tp[:, 1, :])
        gather_bank = (turn_bank, y_bank[0], y_bank[1], turn_bank)

        def sem(name):
            return ctx.enter_context(nc.semaphore(name))

        w_full = [sem(f"w_full{i}") for i in range(RING)]
        e_full = [sem(f"e_full{i}") for i in range(12)]
        ada_full = [sem(f"ada_full{i}") for i in range(2)]
        S = {n: sem(n) for n in """
            w_used chunk_used hi_ready lo_pool lo_dve xf_ready x_split xh_ready tile_ready sq_done u_split late_in consts_in x_in relb_in vec_in lam_in onehot_in rowsg_in rowsb_in small_in badd_in
            relb_set vecrow_set bias_mm bias_copied bias_dram bias_in vec_mm vec_done
            tp_ready tp_done x_ready v_done q_done k_done sc_ready nmax_ready exp_done attw_ready o_ready o_done
            osq_ready osq_rstd o_scaled ln_stat ln_rstd ln_out h_done up_ready relu_done hid_ready hid_used
            dve_chain act_chain pool_chain lam_ready lam_exp lam_done c_silu ada_done mod_mm mod_done modc_done acc_taken
            lat_copied lat_stat lat_rstd lat_done rq_done rk_done uqr_in ukv_in kpe_done uq_ready uq_done pe_done vmla_done
            rv_done sret_ready st_ready y_ready y_done hn_stat hn_rstd rg_done gr_done yret_ready ret_merged gm_done
            mla_merged wo_done out_stored out_ready
            r_stat r_rstd r_out lg_ready lg_copied lg_max lg_exp lg_m2 lg_e2 mask_ready pos_ready trips_ready
            sel_ready gsel_ready xe_ready xe_done e_used silu_done hid_done turn_ready turned_done y0_ready y0_done y1_done y0_low y1_low gate_done
            sums_ready final_chain
            """.split()}
        block = ctx.enter_context(nc.Block())

        def w_row_tiles(w, kt, cols):
            return w[kt * 128:(kt + 2) * 128, cols].rearrange("(k p) n -> p k n", p=128)

        def w_cols(w, cols):
            return w[:, cols].rearrange("(k p) n -> p k n", p=128)

        def chunk(b, j):
            s = ring[:, slot_of(b), :]
            if b >= B_C and b < B_RQK:
                k, half = divmod(j, 2)
                return s[:, 704 * k + 384 * half:704 * k + (704 if half else 384)]
            if is_cols(b):
                c, k = divmod(j, 2)
                return s.rearrange("p (k n) -> p k n", k=8)[:, 4 * k:4 * k + 4, 128 * c:128 * c + 128]
            return s[:, CHUNK * j:CHUNK * j + CHUNK]

        def is_cols(b):
            for a in B_ATT:
                if a + 4 <= b < a + 12:
                    return True
            for a in B_MLP:
                if b == a or (a < b < a + 31 and (b - a) % 2 == 1):
                    return True
            return B_RQK <= b < B_RV

        def split_view(w, j, part):
            if len(part.shape) == 3:
                return w[:, j, :].rearrange("p (k n) -> p k n", k=part.shape[1])
            return w[:, j, 0:part.shape[1]]

        @block.sync
        def _(sp):
            def load(b, src, at=0):
                n = src.shape[1] * src.shape[2]
                if b >= RING:
                    old = b - RING
                    if is_split(old):
                        sp.wait_ge(S["lo_dve"] if low_by_vector(old) else S["lo_pool"], PARTS * (low_index(old) + 1))
                    else:
                        sp.wait_ge(S["w_used"], whole_index(old) + 1)
                dst = ring[:, slot_of(b), 0:n].rearrange("p (k n) -> p k n", k=src.shape[1])
                sp.dma_start(dst, src).then_inc(w_full[slot_of(b)], 16)

            def cols(a, n):
                return slice(a, a + n)

            sp.dma_start(consts[:, :], A["consts"]).then_inc(S["consts_in"], 16)
            sp.dma_start(h_tm[:, :, :], A["x"][0, :, :].rearrange("(q p) n -> p q n", p=128)).then_inc(S["x_in"], 16)
            for layer in range(2):
                b = B_ATT[layer]
                wv, cv = (A["w_in_a"][0, :, :], 2048) if layer == 0 else (A["w_kv_shared"], 1024)
                wq, cq = (A["w_in_a"][0, :, :], 0) if layer == 0 else (A["w_q_b"][0, :, :], 0)
                wk, ck = (A["w_in_a"][0, :, :], 1024) if layer == 0 else (A["w_kv_shared"], 0)
                wo = A["w_out_a"][0, :, :] if layer == 0 else A["w_out_b"][0, :, :]
                for i in range(4):
                    load(b + i, w_row_tiles(wv, 2 * i, cols(cv, D)))
                for i in range(4):
                    load(b + 4 + 2 * i, w_cols(wq, cols(cq + 256 * i, 256)))
                    load(b + 5 + 2 * i, w_cols(wk, cols(ck + 256 * i, 256)))
                for i in range(4):
                    load(b + 12 + i, w_row_tiles(wo, 2 * i, cols(0, D)))
                b = B_MLP[layer]
                up = A["w_up"][layer, :, :].rearrange("(k p) n -> p k n", p=128)
                down = A["w_down"][layer, :, :]

                def up_cols(j):
                    load(b + max(2 * j - 1, 0), up[:, :, 256 * j:256 * j + 256])

                def down_rows(j):
                    load(b + min(2 * j + 2, 31), down[j * 256:(j + 1) * 256, :].rearrange("(k p) n -> p k n", p=128))

                up_cols(0)
                for j in range(3):
                    up_cols(j + 1)
                    down_rows(j)
                with sp.Fori(0, 6) as t:
                    for u in range(2):
                        for part in range(2):
                            o = 7 + 2 * u + part
                            low = PARTS * (low_index(b + o - RING) + 1)
                            sp.wait_ge(S["lo_dve"], t * (4 * PARTS) + low)
                            s = slot_of(b + o)
                            if part == 0:
                                src = up[:, :, bass.ds(t * 512 + (u + 4) * 256, 256)]
                                dst = ring[:, s, :].rearrange("p (k n) -> p k n", k=8)
                            else:
                                src = down[bass.ds(t * 512 + (u + 3) * 256, 256), :]\
                                    .rearrange("(k p) n -> p k n", p=128)
                                dst = ring[:, s, :].rearrange("p (k n) -> p k n", k=2)
                            sp.dma_start(dst, src).then_inc(w_full[s], 16)
                down_rows(15)
            w_in = A["w_in_2"][0, :, :]
            for i in range(4):
                load(B_C + i, w_row_tiles(w_in, 2 * i, cols(4096, 704)))

            def load_rqk(i):
                load(rqk_block(i), w_cols(w_in, cols(1024 * (i % 2) + 256 * (i // 2), 256)))

            load_rqk(0)
            load_rqk(1)
            for i in range(3):
                w = A["w_uq_2"][0, i * 128:(i + 1) * 128, :].rearrange("p (h c) -> p h c", c=192)
                load(B_UQ + i, w[:, :, 0:128])
                for x in range(2):
                    sp.dma_start(ring[:, slot_of(B_UQ + i), 1024 + 256 * x:1280 + 256 * x]
                                 .rearrange("p (h c) -> p h c", h=8),
                                 w[:, :, 128 + 32 * x:160 + 32 * x]).then_inc(S["uqr_in"], 16)
            load(B_UKV, A["w_ukv_2"][0, 0:128, :].rearrange("(k p) n -> p k n", k=1))
            sp.dma_start(ukv[1], A["w_ukv_2"][0, 128:256, :]).then_inc(S["ukv_in"], 16)
            for i in range(2, 8):
                load_rqk(i)
            for b, w, c in ((B_RV, w_in, 2048), (B_RG, w_in, 3072), (B_GR, w_in, 4800), (B_GM, w_in, 5824),
                            (B_RO, A["w_ret_o_2"][0, :, :], 0), (B_MO, A["w_mla_o_2"][0, :, :], 0), (B_WO, A["w_out_2"][0, :, :], 0)):
                for i in range(4):
                    load(b + i, w_row_tiles(w, 2 * i, cols(c, D)))
            w1 = A["w1_2"][0, :, :, :, :].rearrange("g e (k p) f -> (g e) p k f", p=128)
            w3 = A["w3_2"][0, :, :, :, :].rearrange("g e (k p) f -> (g e) p k f", p=128)
            w2 = A["w2_2"][0, :, :, :, :].rearrange("g e (k p) n -> (g e) p k n", p=128)
            parts = [(w, 2 * pair + e) for pair in range(2) for w in (w1, w3, w2) for e in range(2)]

            def load_part(o, src):
                sp.dma_start(e_ring[o].rearrange("p (k n) -> p k n", k=src.shape[1]), src).then_inc(e_full[o], 16)

            for o, (w, e) in enumerate(parts):
                if o == 0:
                    sp.wait_ge(S["y_done"], 4)
                elif o == 2:
                    sp.wait_ge(S["xh_ready"], 20)
                elif o == 3:
                    sp.wait_ge(S["yret_ready"], QT)
                elif o == 4:
                    sp.wait_ge(S["mla_merged"], QT)
                elif 6 <= o < 10:
                    sp.wait_ge(S["lo_pool"], PARTS * (low_index(B_WO + o - 6) + 1))
                elif o == 10:
                    sp.wait_ge(S["u_split"], QT)
                    sp.wait_ge(S["lg_ready"], 1)
                load_part(o, w[e, :, :, :])
            sp.wait_ge(S["trips_ready"], 1)
            steps = sp.value_load(trips[0:1, 0:1], min_val=STEPS, max_val=ROUNDS * STEPS)
            with sp.Fori(1, steps) as i:
                for o, (w, e) in enumerate(parts):
                    sp.wait_ge(S["e_used"], i * 12 + (o - 11))
                    load_part(o, w[bass.ds((i % STEPS) * 4 + e, 1), :, :, :].rearrange("o p k n -> p (o k) n"))
            for q in range(QT):
                sp.wait_ge(S["out_ready"], q + 1)
                sp.dma_start(A["out"][0, q * 128:(q + 1) * 128, :], h_tm[:, q, :]).then_inc(S["out_stored"], 16)
            sp.wait_ge(S["out_stored"], 16 * QT)

        @block.gpsimd
        def _(pool):
            n = [0]

            def link(ins):
                n[0] += 1
                ins.then_inc(S["pool_chain"], 1)
                pool.wait_ge(S["pool_chain"], n[0])

            pool.memset(relb[:, :], NEG).then_inc(S["relb_set"], 1)
            pool.wait_ge(S["relb_set"], 1)
            pool.dma_start(relb[0:32, :], A["rel_bias"]).then_inc(S["relb_in"], 16)
            pool.dma_start(onehot, A["onehot"]).then_inc(S["onehot_in"], 16)
            pool.memset(vec_rows[:, :], 0.0).then_inc(S["vecrow_set"], 1)
            pool.wait_ge(S["vecrow_set"], 1)
            for name, (at, rows) in VEC.items():
                flat = A[name].rearrange("a (r n) -> (a r) n", n=128)
                pool.dma_start(vec_rows[at:at + rows, :], flat).then_inc(S["vec_in"], 16)
            pool.dma_start(lam_rows[:, :], bass.AP(A["lam_a"].tensor, 0, [[0, 128], [1, 256]])).then_inc(S["lam_in"], 16)
            pool.wait_ge(S["bias_copied"], 1)
            pool.dma_start(A["bias_dram"], bias_rows.unsqueeze(1).to_broadcast([16, 128, 512]))\
                .then_inc(S["bias_dram"], 16)
            pool.dma_start(brow[0:1, 0:4], A["b_grp_2"]).then_inc(S["small_in"], 16)
            pool.dma_start(brow[0:1, 4:36], A["b_exp_2"]).then_inc(S["small_in"], 16)
            pool.dma_start(w_rt[:, :, 0:4], A["w_grp_2"][0, :, :].rearrange("(k p) n -> p k n", p=128))\
                .then_inc(S["small_in"], 16)
            pool.dma_start(w_rt[:, :, 4:36], A["w_exp_2"][0, :, :].rearrange("(k p) n -> p k n", p=128))\
                .then_inc(S["small_in"], 16)
            link(pool.memset(mod[:, :], 0.0))
            pool.dma_start(mod[0:1, :], A["b_ada_2"]).then_inc(S["badd_in"], 16)
            pool.wait_ge(S["bias_dram"], 16)
            t = A["bias_dram"].tensor
            pool.dma_start(bias[:, :, 0:128], bass.AP(t, 255, [[511, 128], [128 * 512, 16], [1, 128]]))\
                .then_inc(S["bias_in"], 16)
            pool.dma_start(bias[:, :, 128:384], bass.AP(t, 127, [[511, 128], [128 * 512, 16], [1, 256]]))\
                .then_inc(S["bias_in"], 16)

            def ada(start, end):
                for i in range(start, end):
                    k, j = divmod(i, 6)
                    s = i % 2
                    if i == 0:
                        fetch(0)
                    if i + 1 < 48:
                        fetch(i + 1)
                    pool.wait_ge(ada_full[s], 16 * (i // 2 + 1))
                    link(pool.tensor_tensor(stage[:, s, :], stage[:, s, :], act_c[:, k:k + 1].to_broadcast([128, 1024]),
                                            ALU.mult))
                    part = mod[:, j * 1024:(j + 1) * 1024]
                    last = pool.tensor_tensor(part, part, stage[:, s, :], ALU.add)
                    if i == 47:
                        last.then_inc(S["ada_done"], 1)
                    else:
                        link(last)

            def fetch(i):
                k, j = divmod(i, 6)
                pool.dma_start(stage[:, i % 2, :], A["w_ada_2"][0, k * 128:(k + 1) * 128, j * 1024:(j + 1) * 1024])\
                    .then_inc(ada_full[i % 2], 16)

            done = [0]

            def low(b, n=1):
                for bb in range(b, b + n):
                    for j in range(PARTS):
                        pool.wait_ge(S["hi_ready"], PARTS * split_index(bb) + j + 1)
                        part = chunk(bb, j)
                        pool.tensor_tensor(split_view(w_lo, j, part), part, split_view(w_hi, j, part),
                                           ALU.subtract).then_inc(S["lo_pool"], 1)

            def rows(src_g, src_b, i):
                pool.dma_start(rows_g, bass.AP(src_g.tensor, i * 1024, [[0, 128], [1, 1024]]))\
                    .then_inc(S["rowsg_in"], 16)
                pool.dma_start(rows_b, bass.AP(src_b.tensor, i * 1024, [[0, 128], [1, 1024]]))\
                    .then_inc(S["rowsb_in"], 16)

            def residual(i):
                pool.wait_ge(S["rowsg_in"], 16 * (i + 1))
                pool.wait_ge(S["rowsb_in"], 16 * (i + 1))
                for q in range(QT):
                    pool.wait_ge(S["ln_out"], QT * i + q + 1)
                    link(pool.tensor_tensor(h_tm[:, q, :], o_tm[:, q, :], rows_g, ALU.mult))
                    last = pool.tensor_tensor(h_tm[:, q, :], h_tm[:, q, :], rows_b, ALU.add)
                    if q == 0:
                        link(last)
                last.then_inc(S["h_done"], 1)
                pool.wait_ge(S["h_done"], i + 1)

            rows(A["ln1_g"], A["ln1_b"], 0)
            low(B_ATT[0] + 4, 13)
            pool.wait_ge(S["c_silu"], 1)
            pool.wait_ge(S["badd_in"], 16)
            ada(0, 6)
            residual(0)
            rows(A["ln2_g"], A["ln2_b"], 0)
            ada(6, 26)
            low(B_ATT[1], 1)
            pool.wait_ge(S["h_done"], 2)
            rows(A["ln1_g"], A["ln1_b"], 1)
            low(B_ATT[1] + 1, 16)
            residual(2)
            rows(A["ln2_g"], A["ln2_b"], 1)
            ada(26, 48)
            pool.wait_ge(S["ada_done"], 1)
            pool.dma_start(stage[:, :, :].rearrange("p a b -> p (a b)"), A["late"]).then_inc(S["late_in"], 16)
            low(B_C, 6)
            low(B_UKV + 1, 6)
            pool.wait_ge(S["o_done"], 20)
            pool.dma_start(rows_g, bass.AP(A["norm2_2"].tensor, 0, [[0, 128], [1, 1024]]))\
                .then_inc(S["rowsg_in"], 16)
            pool.dma_start(rows_b, bass.AP(A["final_norm_2"].tensor, 0, [[0, 128], [1, 1024]]))\
                .then_inc(S["rowsb_in"], 16)
            low(B_RV, 28)
            pool.wait_ge(S["mla_merged"], QT)
            pool.memset(turned, 0.0).then_inc(S["turned_done"], 1)
            pool.wait_ge(S["turned_done"], 1)
            pool.wait_ge(S["chunk_used"], PARTS * (split_index(B_WO + 3) + 1))
            link(pool.tensor_copy(place_t, turned[:, 0:256]))
            pool.tensor_copy(y_lo[:, 0, :], turned).then_inc(S["y0_low"], 1)
            pool.tensor_copy(y_lo[:, 1, :], turned).then_inc(S["y1_low"], 1)

        @block.tensor
        def _(pe):
            groups = [0]

            def transposes(items):
                g = groups[0]
                groups[0] += 1
                if g >= 2:
                    pe.wait_ge(S["tp_done"], g - 1)
                for off, src in items:
                    last = pe.transpose(tp[:, g % 2, off:off + 128], src, ident)
                last.then_inc(S["tp_ready"], 1)

            def tile_to_feature_major(src, q):
                for half in range(2):
                    transposes([(128 * j, src[:, q, (4 * half + j) * 128:(4 * half + j + 1) * 128])
                                for j in range(4)])

            def to_feature_major(src):
                for q in range(QT):
                    tile_to_feature_major(src, q)

            def transposed():
                pe.wait_ge(S["tp_done"], groups[0])

            inputs = [0]

            def input_split():
                if groups[0] - 1 in PLAIN:
                    transposed()
                else:
                    inputs[0] += 4
                    pe.wait_ge(S["x_split"], inputs[0])

            def columns_to_feature_major(src, g):
                transposes([(256 * k + 128 * q, src[:, q, 256 * g + 128 * k:256 * g + 128 * k + 128])
                            for k in range(2) for q in range(QT)])

            def product(out, lhs, rhs, start, stop):
                pe.matmul(out, lhs[0], rhs[0], start=start, stop=False)
                pe.matmul(out, lhs[0], rhs[1], start=False, stop=False)
                return pe.matmul(out, lhs[1], rhs[0], start=False, stop=stop)

            def chunk_ready(b, j, t=None, per=0):
                sem_ = S["lo_dve"] if low_by_vector(b) else S["lo_pool"]
                n = PARTS * low_index(b) + j + 1
                pe.wait_ge(sem_, n if t is None else t * per + n)

            def x_parts(kt, cols=slice(0, SEQ)):
                return x_hi[:, kt, cols], x_lo[:, kt, cols]

            def w_parts(j, cols=slice(0, CHUNK)):
                return w_hi[:, j, cols], w_lo[:, j, cols]

            def arrive(b):
                pe.wait_ge(w_full[slot_of(b)], 16 * (b // RING + 1))

            def tokens_out(b, freed=None, by_tile=False, before=lambda i, j: None):

                def part(i, j, q):
                    k, half = divmod(j, 2)
                    kt = 2 * i + k
                    return product(acc[:, 2 * q + half, :], x_parts(kt, slice(q * 128, (q + 1) * 128)),
                                   w_parts(j), start=(kt == 0), stop=(kt == 7))

                for i in range(3 if by_tile else 4):
                    for j in range(PARTS):
                        before(i, j)
                        chunk_ready(b + i, j)
                        if freed and i == 0 and j < 2:
                            pe.wait_ge(S[freed], 2 * (j + 1))
                        for q in range(QT):
                            last = part(i, j, q)
                        last.then_inc(S["chunk_used"], 1)
                if by_tile:
                    before(3, 0)
                    for j in range(PARTS):
                        chunk_ready(b + 3, j)
                        last = part(3, j, 0)
                    last.then_inc(S["tile_ready"], 1)
                    for j in range(PARTS):
                        part(3, j, 1).then_inc(S["chunk_used"], 1)

            def features_out(b, bank, t=None, before=lambda j: None):
                for j in range(PARTS):
                    c, k = divmod(j, 2)
                    before(j)
                    chunk_ready(b, j, t, 4 * PARTS)
                    for i in range(4):
                        kt = 4 * k + i
                        last = product(bank[:, 256 * c:256 * c + 256], w_parts(j, slice(128 * i, 128 * i + 128)),
                                       x_parts(kt), start=(kt == 0), stop=(kt == KT - 1))
                    last.then_inc(S["chunk_used"], 1)

            def scores(n, c):
                pe.wait_ge(S["q_done"], n // 2 + 1)
                pe.wait_ge(S["k_done"], n // 2 + 1)
                if c == 7:
                    pe.wait_ge(S["o_done"], n)
                elif 2 <= c < 6:
                    pe.wait_ge(S["o_done"], n - 1)
                for m in range(2):
                    p = slice(64 * m, 64 * m + 64)
                    bank = head_bank(c, m)
                    pe.matmul(bank[:, 0:128], q_t[p, c, 0:128], k_t[p, c, 0:128], start=True, stop=True)
                    last = pe.matmul(bank[:, 128:384], q_t[p, c, 128:256], k_t[p, c, :], start=True, stop=True)
                last.then_inc(S["sc_ready"], 1)

            def att_turn(layer, n, c):
                pe.wait_ge(S["attw_ready"], n + 1)
                for m in range(layer + 1):
                    transposes([(128 * j, prob[:, c % 2, m, 128 * j:128 * j + 128]) for j in range(3)])

            def att_out(layer, n, c, turned=False):
                if not turned:
                    att_turn(layer, n, c)
                transposed()
                maps = (0,) if layer == 0 else (0, 1)
                pe.wait_ge(S["v_done"], layer + 1)
                for m in maps:
                    w = 128 if layer == 0 else 64
                    cols = slice(128 * c + w * m, 128 * c + w * m + w)
                    for q in range(QT):
                        out = head_bank(c, q)[:, 384 + w * m:384 + w * m + w]
                        for kb in range(q + 1):
                            j = 0 if q == 0 else 1 + kb
                            last = pe.matmul(out, prob_t[:, c % 2, m, 128 * j:128 * j + 128], v_tm[:, kb, cols],
                                             start=(kb == 0), stop=(kb == q))
                last.then_inc(S["o_ready"], 1)

            def attention(layer):
                b = B_ATT[layer]
                tokens_out(b)
                if layer == 0:
                    pe.wait_ge(S["vec_in"], 16 * len(VEC))
                    pe.transpose(pp[:, 1, 0:128], vec_rows[:, :], ident).then_inc(S["vec_mm"], 1)
                    pe.wait_ge(S["bias_copied"], 1)
                    pe.wait_ge(S["vec_done"], 1)
                pe.wait_ge(S["v_done"], layer + 1)

                def queries(i):
                    if layer + i:
                        pe.wait_ge(S["q_done"], 4 * layer + i)
                    features_out(b + 4 + 2 * i, pp[:, 0, :])

                def keys(i, before=lambda j: None):
                    if layer + i:
                        pe.wait_ge(S["k_done"], 4 * layer + i)
                    features_out(b + 5 + 2 * i, pp[:, 1, :], before=before)

                n = 8 * layer
                queries(0)
                keys(0)
                for i in range(1, 4):
                    queries(i)
                    if i >= 2:
                        att_turn(layer, n + 2 * i - 3, 2 * i - 3)
                    scores(n + 2 * i - 2, 2 * i - 2)
                    if i >= 2:
                        att_out(layer, n + 2 * i - 3, 2 * i - 3, turned=True)

                    def between(j):
                        if j == 1:
                            scores(n + 2 * i - 1, 2 * i - 1)
                        elif j == 3:
                            att_turn(layer, n + 2 * i - 2, 2 * i - 2)

                    keys(i, between)
                    att_out(layer, n + 2 * i - 2, 2 * i - 2, turned=True)
                scores(n + 6, 6)
                att_out(layer, n + 5, 5)

                def normed(chunks, count):
                    if layer == 0:
                        pe.wait_ge(S["o_scaled"], count)
                    pe.wait_ge(S["o_done"], n + chunks)

                def before(i, j):
                    if (i, j) == (0, 3):
                        att_turn(layer, n + 6, 6)
                    elif (i, j) == (1, 0):
                        att_out(layer, n + 6, 6, turned=True)
                        normed(6, 2)
                        columns_to_feature_major(o_tm, 2)
                    elif (i, j) == (1, 1):
                        scores(n + 7, 7)
                    elif (i, j) == (2, 0):
                        input_split()
                    elif layer == 1 and (i, j) == (2, 2):
                        att_turn(layer, n + 7, 7)
                    elif layer == 1 and (i, j) == (2, 3):
                        att_out(layer, n + 7, 7, turned=True)
                    elif (i, j) == (3, 0):
                        if layer == 0:
                            att_out(layer, n + 7, 7)
                        normed(8, 3)
                        columns_to_feature_major(o_tm, 3)
                        input_split()

                normed(4, 1)
                for g in range(2):
                    columns_to_feature_major(o_tm, g)
                input_split()
                pe.wait_ge(S["o_done"], n + 6)
                tokens_out(b + 12, by_tile=True, before=before)

            def norm_transposes(i):
                for q in range(QT):
                    pe.wait_ge(S["ln_out"], QT * i + q + 1)
                    for half in range(2):
                        transposes([(128 * j, o_tm[:, q, (4 * half + j) * 128:(4 * half + j + 1) * 128])
                                    for j in range(4)])
                input_split()

            def mlp(layer):
                b = B_MLP[layer]

                def up(o, v, t=None):
                    j = PAIRS * layer + v
                    if v >= 2 or t is not None:
                        pe.wait_ge(S["relu_done"], j - 1 if t is None else t * 2 + (j - 1))
                    features_out(b + o, pp[:, v % 2, :], t)

                def down_part(c, v, q, first=False, final=False):
                    f, half = divmod(c, 2)
                    tok = slice(q * 128, (q + 1) * 128)
                    return product(acc[:, 2 * q + half, :], (hid_hi[:, v % 2, f, tok], hid_lo[:, v % 2, f, tok]),
                                   w_parts(c), start=(first and f == 0), stop=(final and f == 1))

                def down(o, v, t=None, first=False):
                    j = PAIRS * layer + v
                    pe.wait_ge(S["hid_ready"], j + 1 if t is None else t * 2 + (j + 1))
                    for c in range(PARTS):
                        chunk_ready(b + o, c, t, 4 * PARTS)
                        for q in range(QT):
                            last = down_part(c, v, q, first)
                        last.then_inc(S["chunk_used"], 1)

                up(0, 0)
                for v in range(3):
                    up(2 * v + 1, v + 1)
                    if v == 0:
                        pe.wait_ge(S["acc_taken"], 2 * layer + 1)
                    down(2 * v + 2, v, first=(v == 0))
                with pe.Fori(0, 6) as t:
                    for u in range(2):
                        up(7 + 2 * u, 4 + u, t)
                        down(8 + 2 * u, 3 + u, t)
                pe.wait_ge(S["hid_ready"], PAIRS * (layer + 1))
                for c in range(PARTS):
                    chunk_ready(b + 31, c)
                    last = down_part(c, 15, 0, final=True)
                last.then_inc(S["tile_ready"], 1)
                for c in range(PARTS):
                    down_part(c, 15, 1, final=True).then_inc(S["chunk_used"], 1)

            pe.wait_ge(S["consts_in"], 16)
            pe.wait_ge(S["x_in"], 16)
            to_feature_major(h_tm)
            pe.wait_ge(S["relb_in"], 16)
            pe.wait_ge(S["onehot_in"], 16)
            pe.matmul(pp[0:16, 0, :], relb[:, :], onehot, start=True, stop=True).then_inc(S["bias_mm"], 1)
            input_split()

            for layer in range(2):
                attention(layer)
                norm_transposes(2 * layer)
                mlp(layer)
                if layer == 0:
                    norm_transposes(1)

            pe.wait_ge(S["ada_done"], 1)
            pe.wait_ge(S["relu_done"], 2 * PAIRS)
            for part in range(2):
                for j in range(8):
                    at = 1024 * part + 128 * j
                    last = pe.matmul(pp[:, 0, 8 * part + j:8 * part + j + 1], mod[:, at:at + 128],
                                     con("ones")[:, 0:1], start=True, stop=True)
            last.then_inc(S["mod_mm"], 1)

            def mod_rows(part):
                if part:
                    pe.wait_ge(S["mod_done"], 2 * part)
                for half in range(2):
                    at = 2048 + 1024 * part + 512 * half
                    pe.matmul(pp[:, half, :], con("ones"), mod[:, at:at + 512], start=True, stop=True)\
                        .then_inc(S["mod_mm"], 1)

            for q in range(QT):
                pe.wait_ge(S["r_out"], q + 1)
                for half in range(2):
                    transposes([(128 * j, o_tm[:, q, (4 * half + j) * 128:(4 * half + j + 1) * 128])
                                for j in range(4)])
            input_split()
            for i in range(4):
                for j in range(PARTS):
                    k, part = divmod(j, 2)
                    kt = 2 * i + k
                    n = 320 if part else 384
                    chunk_ready(B_C + i, j)
                    for q in range(QT):
                        last = product(acc[:, 2 * q + part, 0:n], x_parts(kt, slice(q * 128, (q + 1) * 128)),
                                       w_parts(j, slice(0, n)), start=(kt == 0), stop=(kt == 7))
                    last.then_inc(S["chunk_used"], 1)

            def rqk(i):
                if i >= 2:
                    pe.wait_ge(S["rk_done" if i % 2 else "rq_done"], i // 2)
                features_out(rqk_block(i), pp[:, i % 2, :])

            rqk(0)
            rqk(1)
            for q in range(QT):
                pe.wait_ge(S["lat_done"], q + 1)
                transposes([(128 * j, lat[:, q, 128 * j:128 * j + 128]) for j in range(3)])
                transposes([(128 * j, lat[:, q, 384 + 128 * j:512 + 128 * j]) for j in range(4)])
            transposed()
            pe.wait_ge(S["rq_done"], 1)
            pe.wait_ge(S["rk_done"], 1)
            for i in range(3):
                arrive(B_UQ + i)
            pe.wait_ge(S["uqr_in"], 16 * 6)
            n = 0

            def uq_bank():
                if n >= 2:
                    pe.wait_ge(S["uq_done"], n - 1)
                return pp[:, n % 2, :]

            for pair in range(6):
                bank = uq_bank()
                for c in range(2):
                    for kt in range(3):
                        at = 128 * (2 * pair + c) if pair < 4 else 1024 + 256 * c + 128 * (pair - 4)
                        lhs = ring[:, slot_of(B_UQ + kt), at:at + 128]
                        last = pe.matmul(bank[:, 256 * c:256 * c + 256], lhs, lat_t[:, kt, :],
                                         start=(kt == 0), stop=(kt == 2))
                last.then_inc(S["uq_ready"], 1)
                n += 1
            arrive(B_UKV)
            for pair in range(4):
                bank = uq_bank()
                for c in range(2):
                    for kt in range(2):
                        if pair == 0 and c == 0 and kt == 1:
                            last.then_inc(S["w_used"], 3)
                            pe.wait_ge(S["ukv_in"], 16)
                        at = 256 * (2 * pair + c)
                        last = pe.matmul(bank[:, 256 * c:256 * c + 256], ukv[kt][:, at:at + 128],
                                         lat_t[:, 3 + kt, :], start=(kt == 0), stop=(kt == 1))
                last.then_inc(S["uq_ready"], 1)
                n += 1
            for kt in range(2):
                w = ukv[kt].rearrange("p (h c) -> p h c", c=256)
                for q in range(QT):
                    for half in range(2):
                        last = pe.matmul(acc[:, 2 * q + half, :], lat_t[:, 3 + kt, q * 128:(q + 1) * 128],
                                         w[:, 4 * half:4 * half + 4, 128:256], start=(kt == 0), stop=(kt == 1))
            last.then_inc(S["w_used"], 1)
            def mla_scores(c):
                if c >= 2:
                    pe.wait_ge(S["o_done"], 16 + c - 1)
                for m in range(2):
                    hd = 2 * c + m
                    a, p = hd // 4, slice(32 * (hd % 4), 32 * (hd % 4) + 32)
                    bank = acc[:, 2 * (c % 2) + m, :]
                    for q in range(QT):
                        out = bank[:, 0:128] if q == 0 else bank[:, 128:384]
                        keys = slice(0, 128 * (q + 1))
                        tok = slice(128 * q, 128 * q + 128)
                        pe.matmul(out, qn_t[:, hd, tok], kn_t[:, hd, keys], start=True, stop=False)
                        pe.matmul(out, pe_rope[p, 2 * a, tok], pe_rope[p, 4, keys], start=False, stop=False)
                        last = pe.matmul(out, pe_rope[p, 2 * a + 1, tok], pe_rope[p, 5, keys],
                                         start=False, stop=True)
                last.then_inc(S["sc_ready"], 1)

            def mla_out(c):
                pe.wait_ge(S["attw_ready"], 16 + c + 1)
                for m in range(2):
                    transposes([(128 * j, prob[:, c % 2, m, 128 * j:128 * j + 128]) for j in range(3)])
                transposed()
                for q in range(QT):
                    for m in range(2):
                        hd = 2 * c + m
                        out = acc[:, 2 * (c % 2) + q, 128 * m:128 * m + 128]
                        for kb in range(q + 1):
                            j = 0 if q == 0 else 1 + kb
                            last = pe.matmul(out, prob_t[:, c % 2, m, 128 * j:128 * j + 128],
                                             v_mla[:, kb, 128 * hd:128 * hd + 128], start=(kb == 0), stop=(kb == q))
                last.then_inc(S["o_ready"], 1)

            pe.wait_ge(S["uq_done"], 10)
            rqk(2)
            pe.wait_ge(S["vmla_done"], 4)
            mla_scores(0)
            mla_scores(1)
            rqk(3)
            mla_out(0)
            mla_scores(2)
            rqk(4)
            mla_out(1)
            mla_scores(3)
            rqk(5)
            mla_out(2)
            rqk(6)
            mla_out(3)
            rqk(7)
            pe.wait_ge(S["o_done"], 20)
            tokens_out(B_RV)
            pe.wait_ge(S["rv_done"], 1)
            pe.wait_ge(S["rq_done"], 4)
            pe.wait_ge(S["rk_done"], 4)
            for h in range(4):
                bank = acc[:, h, :]
                for c in range(2):
                    pe.matmul(bank[:, 0:256], k_t[:, 2 * h + c, 0:128], q_t[:, 2 * h + c, :],
                              start=(c == 0), stop=(c == 1))
                for c in range(2):
                    last = pe.matmul(bank[:, 256:384], k_t[:, 2 * h + c, 128:256], q_t[:, 2 * h + c, 128:256],
                                     start=(c == 0), stop=(c == 1))
                last.then_inc(S["sret_ready"], 1)
            for h in range(4):
                pe.wait_ge(S["st_ready"], h + 1)
                cols = slice(256 * h, 256 * h + 256)
                pe.matmul(acc[:, h, 0:256], st_ret[:, h, 0:128], v_tm[:, 0, cols], start=True, stop=True)
                pe.matmul(acc[:, h, 256:512], st_ret[:, h, 128:256], v_tm[:, 0, cols], start=True, stop=False)
                pe.matmul(acc[:, h, 256:512], st_ret[:, h, 256:384], v_tm[:, 1, cols], start=False, stop=True)\
                    .then_inc(S["y_ready"], 1)
            pe.wait_ge(S["y_done"], 4)

            pe.wait_ge(S["rq_done"], 4)
            pe.wait_ge(S["rk_done"], 4)
            tokens_out(B_RG)
            mod_rows(0)
            tokens_out(B_GR, freed="rg_done")
            mod_rows(1)
            tokens_out(B_GM, freed="gr_done")
            mod_rows(2)
            for q in range(QT):
                pe.wait_ge(S["yret_ready"], q + 1)
                tile_to_feature_major(o_tm, q)
            input_split()
            tokens_out(B_RO, freed="gm_done")
            mod_rows(3)
            to_feature_major(o_mla)
            input_split()
            tokens_out(B_MO, freed="ret_merged")
            for q in range(QT):
                pe.wait_ge(S["mla_merged"], q + 1)
                tile_to_feature_major(merged, q)
            input_split()
            tokens_out(B_WO, by_tile=True)

            pe.wait_ge(S["small_in"], 64)
            for q in range(QT):
                pe.wait_ge(S["r_out"], 2 + q + 1)
                tile_to_feature_major(o_tm, q)
                transposed()
                for kt in range(KT):
                    pe.matmul(pp[:, q, 0:36], q_t[:, kt, q * 128:(q + 1) * 128], w_rt[:, kt, :],
                              start=(kt == 0), stop=False)
                last = pe.matmul(pp[:, q, 0:36], con("ones", 1), brow[0:1, 0:36], start=False, stop=True)
            last.then_inc(S["lg_ready"], 1)
            pe.wait_ge(S["y0_low"], 1)
            for i in range(2 * QT):
                pe.matmul(acc[:, i, :], place_t[:, 0:128], y_lo[:, 0, :], start=True, stop=False)
            pe.wait_ge(S["mask_ready"], 1)
            pe.matmul(pp[:, 0, 0:32], con("tri"), picked[:, 0, :], start=True, stop=True)
            pe.matmul(pp[:, 0, 32:64], con("ones"), picked[:, 0, :], start=True, stop=False)
            pe.matmul(pp[:, 0, 32:64], con("tri"), picked[:, 1, :], start=False, stop=True)
            pe.matmul(pp[:, 0, 64:96], con("ones"), picked[:, 0, :], start=True, stop=False)
            pe.matmul(pp[:, 0, 64:96], con("ones"), picked[:, 1, :], start=False, stop=True).then_inc(S["pos_ready"], 1)

            def gather(g):
                for c in range(2):
                    f = slice(256 * g + 128 * c, 256 * g + 128 * c + 128)
                    out = gather_bank[g][:, 256 * c:256 * c + 256]
                    for q in range(QT):
                        pe.matmul(out, u_hi[:, q, f], sel[:, q, :], start=(q == 0), stop=False)
                        last = pe.matmul(out, u_lo[:, q, f], sel[:, q, :], start=False, stop=(q == 1))
                last.then_inc(S["xe_ready"], 1)

            pe.wait_ge(S["u_split"], QT)
            pe.wait_ge(S["sel_ready"], 1)
            for g in range(4):
                if g == 3:
                    pe.wait_ge(S["xe_done"], 1)
                gather(g)
            pe.wait_ge(S["trips_ready"], 1)
            steps = pe.value_load(trips[0:1, 0:1], min_val=STEPS, max_val=ROUNDS * STEPS)

            def combine(half, stop=False, tiles=range(QT)):
                for q in tiles:
                    for y in (y_hi, y_lo):
                        last = pe.matmul(acc[:, 2 * q + half, :], place_t[:, 128 * q:128 * q + 128], y[:, half, :],
                                         start=False, stop=stop and y is y_lo)
                return last

            with pe.Fori(0, steps) as i:
                for pair in range(2):
                    for w in range(2):
                        for e in range(2):
                            o = 6 * pair + 2 * w + e
                            pe.wait_ge(e_full[o], i * 16 + 16)
                            if o == 0:
                                pe.wait_ge(S["xe_done"], i * 4 + 4)
                        for kt in range(KT):
                            for e in range(2):
                                x = slice(128 * pair + 64 * e, 128 * pair + 64 * e + 64)
                                last = pe.matmul(up_bank[64 * e:64 * e + 64, 256 * w:256 * w + 256], xe[:, kt, x],
                                                 e_ring[6 * pair + 2 * w + e][:, 256 * kt:256 * kt + 256],
                                                 start=(kt == 0), stop=(kt == KT - 1))
                        last.then_inc(S["e_used"], 2)
                    if pair == 1:
                        pe.wait_ge(S["sel_ready"], i + 2)
                        gather(0)
                    pe.wait_ge(S["y0_low"], i * 2 + (pair + 1))
                    combine(0)
                    if pair == 1:
                        gather(1)
                    pe.wait_ge(S["y1_low"], i * 2 + (pair + 1))
                    combine(1)
                    pe.wait_ge(S["gsel_ready"], i + 1)
                    pe.wait_ge(S["hid_done"], i * 2 + (pair + 1))
                    if pair == 1:
                        pe.wait_ge(S["xe_done"], i * 4 + 5)
                    for q in range(QT):
                        pe.matmul(up_bank[:, 0:1], gsel[:, pair, q, :], con("ones")[:, 0:1],
                                  start=(q == 0), stop=(q == QT - 1))
                    for f in range(2):
                        pe.transpose(turn_bank[:, 128 * f:128 * f + 128], hid_e[:, 128 * f:128 * f + 128], ident)
                    for q in range(QT):
                        last = pe.transpose(turn_bank[:, 256 + 128 * q:384 + 128 * q], gsel[:, pair, q, :], ident)
                    last.then_inc(S["turn_ready"], 1)
                    if pair == 1:
                        gather(2)
                    pe.wait_ge(S["turned_done"], i * 2 + (pair + 2))
                    pe.wait_ge(S["gate_done"], i * 2 + (pair + 1))
                    for half in range(2):
                        if pair == 1:
                            pe.wait_ge(S["xe_done"], i * 4 + (6 + half))
                        for f in range(2):
                            for e in range(2):
                                o = 6 * pair + 4 + e
                                if half == 0 and f == 0:
                                    pe.wait_ge(e_full[o], i * 16 + 16)
                                last = pe.matmul(y_bank[half][64 * e:64 * e + 64, :],
                                                 turned[:, 128 * f + 64 * e:128 * f + 64 * e + 64],
                                                 e_ring[o][:, 1024 * f + 512 * half:1024 * f + 512 * half + 512],
                                                 start=(f == 0), stop=(f == 1))
                        if half == 0:
                            last.then_inc(S["y0_ready"], 1)
                            if pair == 1:
                                gather(3)
                        else:
                            last.then_inc(S["e_used"], 2)
            pe.wait_ge(S["y0_low"], steps * 2 + 1)
            combine(0, stop=True)
            pe.wait_ge(S["y1_low"], steps * 2 + 1)
            for q in range(QT):
                combine(1, stop=True, tiles=[q]).then_inc(S["sums_ready"], 1)

        @block.scalar
        def _(act):
            groups = [0]

            def copied(dsts, scales=None, shifts=None):
                g = groups[0]
                groups[0] += 1
                act.wait_ge(S["tp_ready"], g + 1)
                off = 0
                for i, dst in enumerate(dsts):
                    n = dst.shape[1] if len(dst.shape) == 2 else dst.shape[1] * dst.shape[2]
                    src = tp[:, g % 2, off:off + n]
                    if len(dst.shape) == 3:
                        src = src.rearrange("p (a b) -> p a b", a=dst.shape[1])
                    if scales is None:
                        last = act.activation(dst, src, ACT.Copy)
                    elif shifts is None:
                        last = act.activation(dst, src, ACT.Identity, scale=scales[i])
                    else:
                        last = act.activation(dst, src, ACT.Identity, scale=scales[i], bias=shifts[i])
                    off += n
                last.then_inc(S["tp_done"], 1)

            def to_feature_major(dst, scale=None, shift=None, fast=True):
                for q in range(QT):
                    for half in range(2):
                        fs = range(4 * half, 4 * half + 4)
                        if scale is None:
                            copied([dst[:, 4 * half:4 * half + 4, q * 128:(q + 1) * 128]])
                        else:
                            copied([dst[:, f, q * 128:(q + 1) * 128] for f in fs], [scale(f) for f in fs],
                                   None if shift is None else [shift(f) for f in fs])

            inputs = [0]

            plain = [0]

            def to_input_plain(scale=None, parts=None):
                for place in (halves_of_tiles() if parts is None else map(quarter, parts)):
                    g = groups[0]
                    groups[0] += 1
                    assert g == PLAIN[plain[0]]
                    plain[0] += 1
                    act.wait_ge(S["tp_ready"], g + 1)
                    dst = x_hi[(slice(None),) + place]
                    src = tp[:, g % 2, :].rearrange("p (a b) -> p a b", a=dst.shape[1])
                    if scale is None:
                        last = act.activation(dst, src, ACT.Copy)
                    else:
                        last = act.activation(dst, src, ACT.Identity, scale=scale)
                    last.then_inc(S["xh_ready"], 1)

            def to_input(scale, shift, halves=(0, 1)):
                for half in halves:
                    n = inputs[0]
                    inputs[0] += 1
                    assert groups[0] == SHIFTED_AT[n // 4] + n % 4
                    if n >= 2:
                        act.wait_ge(S["x_split"], n - 1)
                    fs = range(4 * half, 4 * half + 4)
                    copied([x_f[:, n % 2, f % 4, :] for f in fs], [scale(f) for f in fs], [shift(f) for f in fs])

            def high(b, t=None, n=1, chunks=range(PARTS)):
                for bb in range(b, b + n):
                    full = 16 * (bb // RING + 1)
                    act.wait_ge(w_full[slot_of(bb)], full if t is None else t * 16 + full)
                    for j in chunks:
                        c = PARTS * split_index(bb) + j
                        if c >= PARTS:
                            at = c - PARTS + 1
                            act.wait_ge(S["chunk_used"], at if t is None else t * (4 * PARTS) + at)
                        part = chunk(bb, j)
                        act.activation(split_view(w_hi, j, part), part, ACT.Copy).then_inc(S["hi_ready"], 1)

            def column(name, i=0):
                at = VEC[name][0] + i
                return vec[:, at:at + 1]

            def used(b):
                if is_split(b):
                    act.wait_ge(S["chunk_used"], PARTS * (split_index(b) + 1))
                else:
                    act.wait_ge(S["w_used"], whole_index(b) + 1)

            to_input_plain()
            high(B_ATT[0])
            act.wait_ge(S["bias_mm"], 1)
            act.activation(bias_rows, pp[0:16, 0, :], ACT.Copy).then_inc(S["bias_copied"], 1)

            def exps(n, b):
                act.wait_ge(S["nmax_ready"], n + 1)
                for m in range(2):
                    for q in range(QT):
                        cols = slice(0, 128) if q == 0 else slice(128, 384)
                        last = act.activation(prob[:, b, m, cols], prob[:, b, m, cols], ACT.Exp,
                                              bias=nmax[:, b, 2 * q + m:2 * q + m + 1],
                                              accum_out=esum[:, b, 2 * q + m:2 * q + m + 1])
                last.then_inc(S["exp_done"], 1)

            def attention(layer):
                b = B_ATT[layer]
                high(b + 1, n=4)
                used(b + 3)
                act.activation(v_tm[:, 0, :], acc[:, 0:2, :].rearrange("p a b -> p (a b)"), ACT.Copy)
                act.activation(v_tm[:, 1, :], acc[:, 2:4, :].rearrange("p a b -> p (a b)"), ACT.Copy)\
                    .then_inc(S["v_done"], 1)
                if layer == 0:
                    act.wait_ge(S["vec_mm"], 1)
                    act.activation(vec[:, :], pp[:, 1, 0:128], ACT.Copy).then_inc(S["vec_done"], 1)
                    act.wait_ge(S["vec_done"], 1)
                    at = VEC["c_2"][0]
                    act.activation(act_c[:, :], vec[:, at:at + 8], ACT.Silu).then_inc(S["c_silu"], 1)
                    act.wait_ge(S["lam_ready"], 1)
                    act.activation(lam_s[:, 2:4], lam_s[:, 0:2], ACT.Exp).then_inc(S["lam_exp"], 1)

                def queries(i):
                    used(b + 4 + 2 * i)
                    act.activation(q_t[:, 2 * i:2 * i + 2, :].rearrange("p a b -> p (a b)"), pp[:, 0, :], ACT.Copy)\
                        .then_inc(S["q_done"], 1)

                def weights_turned(c):
                    for m in range(1 if layer == 0 else 2):
                        copied([prob_t[:, c % 2, m, :]])

                def out(c):
                    if layer == 0:
                        act.wait_ge(S["o_ready"], c + 1)
                        banks = pp if c >= 6 else acc[:, 2 * (c % 2):2 * (c % 2) + 2, :]
                        act.activation(o_tm[:, :, 128 * c:128 * c + 128], banks[:, :, 384:512], ACT.Copy)\
                            .then_inc(S["o_done"], 1)

                n = 8 * layer
                high(b + 5)
                queries(0)
                high(b + 6)
                for i in range(1, 4):
                    high(b + 5 + 2 * i)
                    queries(i)
                    if i >= 2:
                        weights_turned(2 * i - 3)
                        out(2 * i - 3)
                    exps(n + 2 * i - 2, 0)
                    high(b + 6 + 2 * i, chunks=range(3))
                    weights_turned(2 * i - 2)
                    high(b + 6 + 2 * i, chunks=[3])
                    exps(n + 2 * i - 1, 1)
                    out(2 * i - 2)

                def heads_root(first, last, count):
                    if layer == 0:
                        act.wait_ge(S["osq_ready"], count)
                        act.activation(head_rstd[:, :, first:last], head_ms[:, :, first:last], ACT.Sqrt)\
                            .then_inc(S["osq_rstd"], 1)

                scale = lam_s[:, 1:2] if layer == 0 else None
                heads_root(0, 4, 1)
                weights_turned(5)
                out(5)
                to_input_plain(scale, range(2))
                exps(n + 6, 0)
                heads_root(4, 6, 2)
                high(b + 13, chunks=range(3))
                weights_turned(6)
                high(b + 13, chunks=[3])
                out(6)
                to_input_plain(scale, [2])
                high(b + 14)
                exps(n + 7, 1)
                early = PARTS if layer == 0 else 2
                high(b + 15, chunks=range(early))
                weights_turned(7)
                out(7)
                high(b + 15, chunks=range(early, PARTS))
                heads_root(6, 8, 3)
                to_input_plain(scale, [3])
                high(B_MLP[layer])

            def norm_root(i, q):
                act.wait_ge(S["ln_stat"], QT * i + q + 1)
                act.activation(rstd[:, q:q + 1], sr[:, q:q + 1], ACT.Sqrt).then_inc(S["ln_rstd"], 1)

            def norm_input(i, gain, shift):

                def scaled(*halves):
                    to_input(lambda f: column(gain, 8 * (i // 2) + f), lambda f: column(shift, 8 * (i // 2) + f),
                             halves)

                norm_root(i, 0)
                scaled(0)
                norm_root(i, 1)
                scaled(1)
                scaled(0, 1)

            def mlp(layer):
                b = B_MLP[layer]

                def relus(o, v, t=None):
                    j = PAIRS * layer + v
                    at = PARTS * (split_index(b + o) + 1)
                    act.wait_ge(S["chunk_used"], at if t is None else t * (4 * PARTS) + at)
                    if v >= 2 or layer:
                        act.wait_ge(S["hid_ready"], j - 1 if t is None else t * 2 + (j - 1))
                    act.activation(relu[:, v % 2, :], pp[:, v % 2, :], ACT.Relu).then_inc(S["relu_done"], 1)

                high(b + 1)
                relus(0, 0)
                high(b + 2)
                for v in range(1, 3):
                    relus(2 * v - 1, v)
                    high(b + 2 * v + 1)
                    high(b + 2 * v + 2)
                with act.Fori(0, 6) as t:
                    for u in range(2):
                        relus(5 + 2 * u, 3 + u, t)
                        high(b + 7 + 2 * u, t)
                        high(b + 8 + 2 * u, t)
                relus(29, 15)
                high(b + 31)
                high(B_ATT[1] if layer == 0 else B_C)

            def banks_out(dst, function, done):
                for half in range(2):
                    for q in range(QT):
                        act.activation(dst[:, q, 512 * half:512 * half + 512], acc[:, 2 * q + half, :], function)\
                            .then_inc(done, 1)

            def mod_rows(part):
                for half in range(2):
                    at = 2048 + 1024 * part + 512 * half
                    act.wait_ge(S["mod_mm"], 2 * part + half + 2)
                    act.activation(mod[:, at:at + 512], pp[:, half, :], ACT.Copy).then_inc(S["mod_done"], 1)

            for layer in range(2):
                attention(layer)
                norm_input(2 * layer, "ln1_g", "ln1_b")
                mlp(layer)
                if layer == 0:
                    norm_input(1, "ln2_g", "ln2_b")

            norm_root(3, 0)

            def mixer_root(q):
                act.wait_ge(S["r_stat"], q + 1)
                act.activation(rstd[:, q:q + 1], sr[:, q:q + 1], ACT.Sqrt).then_inc(S["r_rstd"], 1)

            def mixer_input(*halves):
                to_input(lambda f: modc[:, 1, f:f + 1], lambda f: modc[:, 0, f:f + 1], halves)

            mixer_root(0)
            norm_root(3, 1)
            act.wait_ge(S["modc_done"], 1)
            mixer_input(0, 1)
            mixer_root(1)
            mixer_input(0, 1)
            high(B_C + 1, n=4)
            used(B_C + 3)
            for q in range(QT):
                act.activation(lat[:, q, 0:384], acc[:, 2 * q, 0:384], ACT.Copy)
                act.activation(lat[:, q, 384:640], acc[:, 2 * q + 1, 0:256], ACT.Copy)
                for x in range(2):
                    last = act.activation(lat[:, q, 640 + 128 * x:768 + 128 * x].rearrange("p (r c) -> p r c", r=4),
                                          acc[:, 2 * q + 1, 256 + 32 * x:288 + 32 * x].unsqueeze(1)
                                          .to_broadcast([128, 4, 32]), ACT.Copy)
            last.then_inc(S["lat_copied"], 1)
            act.wait_ge(S["lat_stat"], 1)
            act.activation(rstd[:, 0:4], sr[:, 0:4], ACT.Sqrt).then_inc(S["lat_rstd"], 1)
            high(B_RQK + 1)
            for q in range(QT):
                tok = slice(q * 128, (q + 1) * 128)
                copied([lat_t[:, j, tok] for j in range(3)], [column("q_norm_2", j) for j in range(3)])
                copied([lat_t[:, 3 + j, tok] for j in range(2)] + [pe_rope[:, 4 + x, tok] for x in range(2)],
                       [column("kv_norm_2", j) for j in range(2)] + [1.0, 1.0])
            assert groups[0] == TP_LATENTS
            for pair in range(4):
                act.wait_ge(S["uq_ready"], pair + 1)
                act.activation(qn_t[:, 2 * pair:2 * pair + 2, :].rearrange("p a b -> p (a b)"), pp[:, pair % 2, :],
                               ACT.Copy).then_inc(S["uq_done"], 1)
            act.wait_ge(S["uq_done"], 6)
            for pair in range(4):
                act.wait_ge(S["uq_ready"], 6 + pair + 1)
                act.activation(kn_t[:, 2 * pair:2 * pair + 2, :].rearrange("p a b -> p (a b)"), pp[:, pair % 2, :],
                               ACT.Copy).then_inc(S["uq_done"], 1)
            high(rqk_block(2))
            used(B_UKV)
            banks_out(v_mla, ACT.Copy, S["vmla_done"])

            def mla_out(c):
                copied([prob_t[:, c % 2, 0, :]])
                copied([prob_t[:, c % 2, 1, :]])

            high(rqk_block(3))
            exps(16, 0)
            exps(17, 1)
            high(rqk_block(4))
            mla_out(0)
            high(rqk_block(5))
            mla_out(1)
            exps(18, 0)
            high(rqk_block(6))
            mla_out(2)
            exps(19, 1)
            high(rqk_block(7))
            mla_out(3)
            high(B_RV, n=5)
            used(B_RV + 3)
            act.wait_ge(S["rk_done"], 4)
            act.activation(v_tm[:, :, :].rearrange("p a b -> p (a b)"), acc[:, :, :].rearrange("p a b -> p (a b)"),
                           ACT.Copy).then_inc(S["rv_done"], 1)
            for h in range(4):
                act.wait_ge(S["y_ready"], h + 1)
                act.activation(o_tm[:, :, 256 * h:256 * h + 256], acc[:, h, :].rearrange("p (a b) -> p a b", a=2),
                               ACT.Copy).then_inc(S["y_done"], 1)
            act.wait_ge(S["hn_stat"], 1)
            act.activation(rstd[:, :], sr[:, :], ACT.Sqrt).then_inc(S["hn_rstd"], 1)
            high(B_RG + 1, n=4)
            used(B_RG + 3)
            banks_out(rg, ACT.Silu, S["rg_done"])
            mod_rows(0)
            high(B_GR + 1, n=4)
            used(B_GR + 3)
            banks_out(gate_r, ACT.Sigmoid, S["gr_done"])
            mod_rows(1)
            high(B_GM + 1, n=4)
            used(B_GM + 3)
            banks_out(gate_m, ACT.Sigmoid, S["gm_done"])
            mod_rows(2)
            to_input_plain()
            high(B_RO + 1, n=4)
            mod_rows(3)
            to_input_plain()
            high(B_MO + 1, n=4)
            to_input_plain()
            high(B_WO + 1, n=3)
            for q in range(QT):
                act.wait_ge(S["r_stat"], 2 + q + 1)
                act.activation(rstd[:, q:q + 1], sr[:, q:q + 1], ACT.Sqrt).then_inc(S["r_rstd"], 1)
                for half in range(2):
                    copied([q_t[:, 4 * half:4 * half + 4, q * 128:(q + 1) * 128]])
            act.wait_ge(S["lg_max"], 1)
            for q in range(QT):
                last = act.activation(route[:, q, 40:44], route[:, q, 0:4], ACT.Exp, bias=route[:, q, 36:37],
                                      accum_out=route[:, q, 37:38])
            last.then_inc(S["lg_exp"], 1)
            act.wait_ge(S["lg_m2"], 1)
            for q in range(QT):
                last = act.activation(route[:, q, 39:40], route[:, q, 38:39], ACT.Exp)
            last.then_inc(S["lg_e2"], 1)
            act.wait_ge(S["trips_ready"], 1)
            steps = act.value_load(trips[0:1, 0:1], min_val=STEPS, max_val=ROUNDS * STEPS)

            def take_gathered(g):
                act.activation(xe[:, 2 * g:2 * g + 2, :].rearrange("p a b -> p (a b)"), gather_bank[g],
                               ACT.Copy).then_inc(S["xe_done"], 1)

            for g in range(4):
                act.wait_ge(S["xe_ready"], g + 1)
                take_gathered(g)
            with act.Fori(0, steps) as i:
                for pair in range(2):
                    act.wait_ge(S["e_used"], i * 12 + (6 * pair + 4))
                    act.activation(silu_e, up_bank[:, 0:256], ACT.Silu).then_inc(S["silu_done"], 1)
                    if pair == 1:
                        for g in range(2):
                            act.wait_ge(S["xe_ready"], i * 4 + (5 + g))
                            take_gathered(g)
                    act.wait_ge(S["turn_ready"], i * 2 + (pair + 1))
                    act.activation(turned, turn_bank, ACT.Copy).then_inc(S["turned_done"], 1)
                    if pair == 1:
                        act.wait_ge(S["xe_ready"], i * 4 + 7)
                        take_gathered(2)
                    act.wait_ge(S["gate_done"], i * 2 + (pair + 1))
                    act.wait_ge(S["y0_ready"], i * 2 + (pair + 1))
                    act.activation(y_hi[:, 0, :], y_bank[0], ACT.Identity, scale=slot_gate[:, 0:1])\
                        .then_inc(S["y0_done"], 1)
                    if pair == 1:
                        act.wait_ge(S["xe_ready"], i * 4 + 8)
                        take_gathered(3)
                    act.wait_ge(S["e_used"], i * 12 + (6 * pair + 6))
                    act.activation(y_hi[:, 1, :], y_bank[1], ACT.Identity, scale=slot_gate[:, 0:1])\
                        .then_inc(S["y1_done"], 1)
            act.activation(warm[:, :], slot_gate[:, :], ACT.Sqrt)
            for q in range(QT):
                act.wait_ge(S["r_stat"], 4 + q + 1)
                act.activation(rstd[:, q:q + 1], sr[:, q:q + 1], ACT.Sqrt).then_inc(S["r_rstd"], 1)

        @block.vector
        def _(dve):
            n = [0]

            def link(ins):
                n[0] += 1
                ins.then_inc(S["dve_chain"], 1)
                dve.wait_ge(S["dve_chain"], n[0])

            def column(name, i=0):
                at = VEC[name][0] + i
                return vec[:, at:at + 1]

            def used(b):
                if is_split(b):
                    dve.wait_ge(S["chunk_used"], PARTS * (split_index(b) + 1))
                else:
                    dve.wait_ge(S["w_used"], whole_index(b) + 1)

            inputs = [0]

            input_groups = [g + i for g in SHIFTED_AT for i in range(4)]

            plain = [0]

            def split_plain(scale=None, parts=None):
                for place in (halves_of_tiles() if parts is None else map(quarter, parts)):
                    g = PLAIN[plain[0]]
                    plain[0] += 1
                    dve.wait_ge(S["xh_ready"], plain[0])
                    hi, lo = x_hi[(slice(None),) + place], x_lo[(slice(None),) + place]
                    src = tp[:, g % 2, :].rearrange("p (a b) -> p a b", a=hi.shape[1])
                    if scale is None:
                        last = dve.tensor_tensor(lo, src, hi, ALU.subtract)
                    else:
                        last = dve.scalar_tensor_tensor(lo, src, scale, hi, ALU.mult, ALU.subtract)
                    last.then_inc(S["tp_done"], 1)

            def split_input():
                for q in range(QT):
                    for half in range(2):
                        n, g = inputs[0], input_groups[inputs[0]]
                        inputs[0] += 1
                        dve.wait_ge(S["tp_done"], g + 1)
                        at = slice(4 * half, 4 * half + 4), slice(q * 128, (q + 1) * 128)
                        link(dve.tensor_copy(x_hi[:, at[0], at[1]], x_f[:, n % 2, :, :]))
                        dve.tensor_tensor(x_lo[:, at[0], at[1]], x_f[:, n % 2, :, :], x_hi[:, at[0], at[1]],
                                          ALU.subtract).then_inc(S["x_split"], 1)

            def low(b, t=None):
                for j in range(PARTS):
                    at = PARTS * split_index(b) + j + 1
                    dve.wait_ge(S["hi_ready"], at if t is None else t * (4 * PARTS) + at)
                    part = chunk(b, j)
                    dve.tensor_tensor(split_view(w_lo, j, part), part, split_view(w_hi, j, part),
                                      ALU.subtract).then_inc(S["lo_dve"], 1)

            split_plain()
            for i in range(4):
                low(B_ATT[0] + i)
            dve.wait_ge(S["lam_in"], 16)
            rows = lam_rows[:, :].rearrange("p (a b d) -> p a b d", a=2, b=2)
            link(dve.tensor_tensor(lam_t[:, :, :], rows[:, :, 0, :], rows[:, :, 1, :], ALU.mult))
            dve.tensor_reduce(lam_s[:, 0:2], lam_t[:, :, :], AX.X, ALU.add).then_inc(S["lam_ready"], 1)
            dve.wait_ge(S["lam_exp"], 1)
            link(dve.tensor_tensor(lam_s[:, 0:1], lam_s[:, 3:4], lam_s[:, 2:3], ALU.subtract))
            lam_init = 0.8 - 0.6 * math.exp(-0.3 * 0)
            link(dve.tensor_scalar(lam_s[:, 0:1], lam_s[:, 0:1], -lam_init, None, ALU.add))
            dve.wait_ge(S["vec_done"], 1)
            link(dve.tensor_scalar(lam_s[:, 1:2], column("subln_a"), 1.0 - lam_init, None, ALU.mult))

            def soft_first(k, b, bias_of, scale, bank_of):
                dve.wait_ge(S["sc_ready"], k + 1)
                if k >= 2:
                    dve.wait_ge(S["o_ready"], k - 1)
                for m in range(2):
                    last = dve.scalar_tensor_tensor(prob[:, b, m, :], bank_of(m)[:, 0:384], scale, bias_of(m),
                                                    ALU.mult, ALU.add)
                link(last)
                dve.tensor_reduce(nmax[:, b, 0:2], prob[:, b, :, 0:128], AX.X, ALU.max)
                link(dve.tensor_reduce(nmax[:, b, 2:4], prob[:, b, :, 128:384], AX.X, ALU.max))
                dve.tensor_scalar(nmax[:, b, :], nmax[:, b, :], -1.0, None, ALU.mult).then_inc(S["nmax_ready"], 1)

            def attention(layer):
                bl = B_ATT[layer]

                def keys(i):
                    used(bl + 5 + 2 * i)
                    dve.tensor_copy(k_t[:, 2 * i:2 * i + 2, :].rearrange("p a b -> p (a b)"), pp[:, 1, :])\
                        .then_inc(S["k_done"], 1)

                def first(c):
                    soft_first(8 * layer + c, c % 2, lambda m: bias[:, 2 * c + m, :], 0.125,
                               lambda m: head_bank(c, m))

                def second(c):
                    b = c % 2
                    dve.wait_ge(S["exp_done"], 8 * layer + c + 1)
                    if layer == 1:
                        dve.reciprocal(rsum[:, b, :], esum[:, b, :]).then_inc(S["attw_ready"], 1)
                        return
                    link(dve.reciprocal(rsum[:, b, :], esum[:, b, :]))
                    for q in range(QT):
                        r1 = rsum[:, b, 2 * q + 1:2 * q + 2]
                        last = dve.tensor_tensor(r1, r1, lam_s[:, 0:1], ALU.mult)
                    link(last)
                    for q in range(QT):
                        cols = slice(0, 128) if q == 0 else slice(128, 384)
                        last = dve.tensor_scalar(prob[:, b, 0, cols], prob[:, b, 0, cols],
                                                 rsum[:, b, 2 * q:2 * q + 1], None, ALU.mult)
                    link(last)
                    for q in range(QT):
                        cols = slice(0, 128) if q == 0 else slice(128, 384)
                        last = dve.scalar_tensor_tensor(prob[:, b, 0, cols], prob[:, b, 1, cols],
                                                        rsum[:, b, 2 * q + 1:2 * q + 2], prob[:, b, 0, cols],
                                                        ALU.mult, ALU.add)
                    last.then_inc(S["attw_ready"], 1)

                def out(c):
                    if layer == 0:
                        return
                    b = c % 2
                    dve.wait_ge(S["o_ready"], 8 + c + 1)
                    for q in range(QT):
                        for m in range(2):
                            at = 128 * c + 64 * m
                            last = dve.tensor_scalar(o_tm[:, q, at:at + 64],
                                                     head_bank(c, q)[:, 384 + 64 * m:448 + 64 * m],
                                                     rsum[:, b, 2 * q + m:2 * q + m + 1], None, ALU.mult)
                    last.then_inc(S["o_done"], 1)

                def squares(c):
                    if layer == 1:
                        return
                    dve.wait_ge(S["o_done"], c + 1)
                    o = o_tm[:, :, 128 * c:128 * c + 128]
                    sq = lam_rows[:, :].rearrange("p (a b) -> p a b", a=2)
                    link(dve.tensor_tensor(sq, o, o, ALU.mult))
                    link(dve.tensor_reduce(head_ms[:, :, c:c + 1], sq, AX.X, ALU.add))

                if layer == 1:
                    dve.wait_ge(S["rowsg_in"], 32)
                    dve.wait_ge(S["rowsb_in"], 32)
                    dve.wait_ge(S["ln_out"], 4)
                    gain_rows(2)
                keys(0)
                for i in range(1, 4):
                    if layer == 0 and i == 1:
                        dve.wait_ge(S["bias_in"], 32)
                    first(2 * i - 2)
                    if i >= 2:
                        out(2 * i - 3)
                    second(2 * i - 2)
                    first(2 * i - 1)
                    keys(i)
                    out(2 * i - 2)
                    second(2 * i - 1)
                    if i >= 2:
                        squares(2 * i - 4)
                        squares(2 * i - 3)

                def heads_stat(first, last):
                    if layer == 0:
                        ms = head_ms[:, :, first:last]
                        link(dve.tensor_scalar(ms, ms, 1.0 / 128, LN_EPS, ALU.mult, ALU.add))
                        dve.reciprocal(ms, ms).then_inc(S["osq_ready"], 1)

                def heads_scale(first, last, count):
                    if layer == 0:
                        dve.wait_ge(S["osq_rstd"], count)
                        for q in range(QT):
                            o3 = o_tm[:, q, 128 * first:128 * last].rearrange("p (h d) -> p h d", d=128)
                            r = head_rstd[:, q, first:last].unsqueeze(2).to_broadcast([128, last - first, 128])
                            ins = dve.tensor_tensor(o3, o3, r, ALU.mult)
                        ins.then_inc(S["o_scaled"], 1)

                scale = lam_s[:, 1:2] if layer == 0 else None
                heads_stat(0, 4)
                first(6)
                heads_scale(0, 4, 1)
                out(5)
                split_plain(scale, range(2))
                squares(4)
                squares(5)
                heads_stat(4, 6)
                second(6)
                heads_scale(4, 6, 2)
                out(6)
                squares(6)
                split_plain(scale, [2])
                first(7)
                second(7)
                out(7)
                squares(7)
                heads_stat(6, 8)
                heads_scale(6, 8, 3)
                split_plain(scale, [3])

            def gain_rows(count):
                for q in range(QT):
                    link(dve.tensor_tensor(h_tm[:, q, :], o_tm[:, q, :], rows_g, ALU.mult))
                    last = dve.tensor_tensor(h_tm[:, q, :], h_tm[:, q, :], rows_b, ALU.add)
                    if q == 0:
                        link(last)
                last.then_inc(S["h_done"], 1)
                dve.wait_ge(S["h_done"], count)

            def row_stats(q, src, eps, done, rms=False):
                for a in range(2):
                    last = dve.bn_stats(st6[:, q, a, :], src[:, 512 * a:512 * a + 512])
                link(last)
                link(dve.bn_aggr(mv[:, q, :], st6[:, q, :, :].rearrange("p a b -> p (a b)")))
                if rms:
                    link(dve.scalar_tensor_tensor(sv[:, q:q + 1], mv[:, q, 0:1], mv[:, q, 0:1], mv[:, q, 1:2],
                                                  ALU.mult, ALU.add))
                    link(dve.tensor_scalar(sv[:, q:q + 1], sv[:, q:q + 1], eps, None, ALU.add))
                else:
                    link(dve.tensor_scalar(sv[:, q:q + 1], mv[:, q, 1:2], eps, None, ALU.add))
                dve.reciprocal(sr[:, q:q + 1], sv[:, q:q + 1]).then_inc(done, 1)

            def layer_norm(i, b):
                if i:
                    dve.wait_ge(S["h_done"], i)

                def rows_sum(q):
                    bank = acc[:, 2 * q:2 * q + 2, :].rearrange("p a b -> p (a b)")
                    return dve.scalar_tensor_tensor(o_tm[:, q, :], h_tm[:, q, :], ALPHA, bank, ALU.mult, ALU.add)

                def normalise(q):
                    dve.wait_ge(S["ln_rstd"], QT * i + q + 1)
                    dve.tensor_scalar(o_tm[:, q, :], o_tm[:, q, :], mv[:, q, 0:1], rstd[:, q:q + 1],
                                      ALU.subtract, ALU.mult).then_inc(S["ln_out"], 1)

                dve.wait_ge(S["tile_ready"], i + 1)
                link(rows_sum(0))
                row_stats(0, o_tm[:, 0, :], LN_EPS, S["ln_stat"])
                normalise(0)
                used(b)
                rows_sum(1).then_inc(S["acc_taken"], 1)
                dve.wait_ge(S["acc_taken"], i + 1)
                row_stats(1, o_tm[:, 1, :], LN_EPS, S["ln_stat"])
                normalise(1)

            def mlp(layer):
                b = B_MLP[layer]

                def square(v, t=None):
                    j = PAIRS * layer + v
                    dve.wait_ge(S["relu_done"], j + 1 if t is None else t * 2 + (j + 1))
                    if v >= 2:
                        at = PARTS * (split_index(b + 2 * (v - 2) + 2) + 1)
                        dve.wait_ge(S["chunk_used"], at if t is None else t * (4 * PARTS) + at)
                    h = relu[:, v % 2, :]
                    hi = hid_hi[:, v % 2, :, :].rearrange("p a b -> p (a b)")
                    dve.tensor_tensor(h, h, h, ALU.mult).then_inc(S["sq_done"], 1)
                    dve.wait_ge(S["sq_done"], 2 * j + 1 if t is None else t * 4 + (2 * j + 1))
                    dve.tensor_copy(hi, h).then_inc(S["sq_done"], 1)
                    dve.wait_ge(S["sq_done"], 2 * j + 2 if t is None else t * 4 + (2 * j + 2))
                    dve.tensor_tensor(hid_lo[:, v % 2, :, :].rearrange("p a b -> p (a b)"), h, hi,
                                      ALU.subtract).then_inc(S["hid_ready"], 1)

                split_input()
                low(b + 1)
                square(0)
                low(b + 2)
                for v in range(1, 3):
                    square(v)
                    low(b + 2 * v + 1)
                    low(b + 2 * v + 2)
                with dve.Fori(0, 6) as t:
                    for u in range(2):
                        square(3 + u, t)
                        low(b + 7 + 2 * u, t)
                        low(b + 8 + 2 * u, t)
                square(15)
                low(b + 31)

            for layer in range(2):
                attention(layer)
                layer_norm(2 * layer, B_ATT[layer] + 15)
                mlp(layer)
                if layer == 0:
                    layer_norm(1, B_MLP[0] + 31)
                    split_input()

            b = B_MLP[1] + 31

            def last_sum(q):
                bank = acc[:, 2 * q:2 * q + 2, :].rearrange("p a b -> p (a b)")
                link(dve.scalar_tensor_tensor(o_tm[:, q, :], h_tm[:, q, :], ALPHA, bank, ALU.mult, ALU.add))

            def last_norm(q):
                link(dve.scalar_tensor_tensor(o_tm[:, q, :], o_tm[:, q, :], mv[:, q, 0:1], rows_g,
                                              ALU.subtract, ALU.mult))
                dve.wait_ge(S["ln_rstd"], 7 + q)
                link(dve.scalar_tensor_tensor(h_tm[:, q, :], o_tm[:, q, :], rstd[:, q:q + 1], rows_b,
                                              ALU.mult, ALU.add))

            def mixer_rows(q):
                dve.wait_ge(S["r_rstd"], q + 1)
                dve.tensor_scalar(o_tm[:, q, :], h_tm[:, q, :], rstd[:, q:q + 1], None, ALU.mult)\
                    .then_inc(S["r_out"], 1)

            dve.wait_ge(S["h_done"], 3)
            dve.wait_ge(S["rowsg_in"], 64)
            dve.wait_ge(S["rowsb_in"], 64)
            dve.wait_ge(S["tile_ready"], 4)
            last_sum(0)
            row_stats(0, o_tm[:, 0, :], LN_EPS, S["ln_stat"])
            last_norm(0)
            row_stats(0, h_tm[:, 0, :], EPS, S["r_stat"], rms=True)
            used(b)
            last_sum(1)
            row_stats(1, o_tm[:, 1, :], LN_EPS, S["ln_stat"])
            mixer_rows(0)
            dve.wait_ge(S["mod_mm"], 1)
            link(dve.tensor_copy(modc[:, :, :].rearrange("p a b -> p (a b)"), pp[:, 0, 0:16]))
            at = VEC["norm1_2"][0]
            dve.scalar_tensor_tensor(modc[:, 1, :], modc[:, 1, :], 1.0, vec[:, at:at + 8], ALU.add, ALU.mult)\
                .then_inc(S["modc_done"], 1)
            last_norm(1)
            row_stats(1, h_tm[:, 1, :], EPS, S["r_stat"], rms=True)
            mixer_rows(1)
            split_input()

            def rotate(out1, out2, bank, cos, sin, done, count, tmp):
                x = bank.rearrange("p (a b) -> p a b", a=2)
                a = tmp[:, 0, :].rearrange("p (a b) -> p a b", a=2)
                b = tmp[:, 1, :].rearrange("p (a b) -> p a b", a=2)
                dve.tensor_tensor(a, x, cos.unsqueeze(1).to_broadcast([128, 2, 256]), ALU.mult)
                link(dve.tensor_tensor(b, x, sin.unsqueeze(1).to_broadcast([128, 2, 256]), ALU.mult))
                dve.tensor_tensor(out1, a[:, 0, :], b[:, 1, :], ALU.subtract)
                dve.tensor_tensor(out2, a[:, 1, :], b[:, 0, :], ALU.add).then_inc(done, 1)
                dve.wait_ge(done, count)

            tmp = v_tm[:, 0, :].rearrange("p (a b) -> p a b", a=2)
            dve.wait_ge(S["late_in"], 16)
            dve.wait_ge(S["lat_copied"], 1)
            for q in range(QT):
                dve.bn_stats(st6[:, q, 0, :], lat[:, q, 0:384])
                last = dve.bn_stats(st6[:, q, 1, :], lat[:, q, 384:640])
            link(last)
            for q in range(QT):
                for a in range(2):
                    last = dve.bn_aggr(mv[:, 2 * q + a, :], st6[:, q, a, :])
            link(last)
            link(dve.tensor_tensor(sv[:, 0:4], mv[:, 0:4, 0], mv[:, 0:4, 0], ALU.mult))
            link(dve.scalar_tensor_tensor(sv[:, 0:4], sv[:, 0:4], EPS, mv[:, 0:4, 1], ALU.add, ALU.add))
            dve.reciprocal(sr[:, 0:4], sv[:, 0:4]).then_inc(S["lat_stat"], 1)
            dve.wait_ge(S["lat_rstd"], 1)
            for q in range(QT):
                dve.tensor_scalar(lat[:, q, 0:384], lat[:, q, 0:384], rstd[:, 2 * q:2 * q + 1], None, ALU.mult)
                dve.tensor_scalar(lat[:, q, 384:640], lat[:, q, 384:640], rstd[:, 2 * q + 1:2 * q + 2], None,
                                  ALU.mult).then_inc(S["lat_done"], 1)

            def rotate_rqk(i):
                used(rqk_block(i))
                dst = k_t if i % 2 else q_t
                h = i // 2
                rotate(dst[:, 2 * h, :], dst[:, 2 * h + 1, :], pp[:, i % 2, :], con("cos_ret"), con("sin_ret"),
                       S["rk_done" if i % 2 else "rq_done"], h + 1, tmp)

            rotate_rqk(0)
            rotate_rqk(1)
            dve.wait_ge(S["tp_done"], TP_LATENTS)
            rotate(pe_rope[:, 4, :], pe_rope[:, 5, :], pe_rope[:, 4:6, :].rearrange("p a b -> p (a b)"),
                   con("cos_mla"), con("sin_mla"), S["kpe_done"], 1, tmp)
            for a in range(2):
                dve.wait_ge(S["uq_ready"], 4 + a + 1)
                dve.wait_ge(S["uq_done"], 4 + a)
                rotate(pe_rope[:, 2 * a, :], pe_rope[:, 2 * a + 1, :], pp[:, a, :], con("cos_mla"), con("sin_mla"),
                       S["uq_done"], 5 + a, tmp)
            def second(c):
                dve.wait_ge(S["exp_done"], 16 + c + 1)
                dve.reciprocal(rsum[:, c % 2, :], esum[:, c % 2, :]).then_inc(S["attw_ready"], 1)

            def out(c):
                dve.wait_ge(S["o_ready"], 16 + c + 1)
                for q in range(QT):
                    for m in range(2):
                        at = 256 * c + 128 * m
                        last = dve.tensor_scalar(o_mla[:, q, at:at + 128],
                                                 acc[:, 2 * (c % 2) + q, 128 * m:128 * m + 128],
                                                 rsum[:, c % 2, 2 * q + m:2 * q + m + 1], None, ALU.mult)
                last.then_inc(S["o_done"], 1)

            def first(c):
                soft_first(16 + c, c % 2, lambda m: con("mask"), MLA_SCALE, lambda m: acc[:, 2 * (c % 2) + m, :])

            rotate_rqk(2)
            first(0)
            first(1)
            second(0)
            second(1)
            rotate_rqk(3)
            out(0)
            first(2)
            rotate_rqk(4)
            out(1)
            second(2)
            first(3)
            rotate_rqk(5)
            out(2)
            second(3)
            rotate_rqk(6)
            out(3)
            rotate_rqk(7)
            for h in range(4):
                dve.wait_ge(S["sret_ready"], h + 1)
                decay = con("decay")[:, 256 * h:256 * h + 256]
                link(dve.tensor_tensor(st_ret[:, h, 0:256], acc[:, h, 0:256], decay, ALU.mult))
                dve.tensor_tensor(st_ret[:, h, 256:384], acc[:, h, 256:384], decay[:, 0:128], ALU.mult)\
                    .then_inc(S["st_ready"], 1)

            dve.wait_ge(S["y_done"], 4)
            for q in range(QT):
                for h in range(4):
                    last = dve.bn_stats(st6[:, 4 * q + h, 0, :], o_tm[:, q, 256 * h:256 * h + 256])
            link(last)
            for j in range(8):
                last = dve.bn_aggr(mv[:, j, :], st6[:, j, 0, :])
            link(last)
            link(dve.tensor_scalar(sv[:, :], mv[:, :, 1], EPS, None, ALU.add))
            dve.reciprocal(sr[:, :], sv[:, :]).then_inc(S["hn_stat"], 1)
            dve.wait_ge(S["hn_rstd"], 1)
            for q in range(QT):
                for h in range(4):
                    j = 4 * q + h
                    cols = slice(256 * h, 256 * h + 256)
                    last = dve.tensor_scalar(o_tm[:, q, cols], o_tm[:, q, cols], mv[:, j, 0:1], rstd[:, j:j + 1],
                                             ALU.subtract, ALU.mult)
            link(last)
            dve.wait_ge(S["rg_done"], 4)
            for q in range(QT):
                dve.tensor_tensor(o_tm[:, q, :], o_tm[:, q, :], rg[:, q, :], ALU.mult).then_inc(S["yret_ready"], 1)
            split_plain()
            used(B_RO + 3)
            dve.wait_ge(S["gr_done"], 4)
            for half in range(2):
                for q in range(QT):
                    cols = slice(512 * half, 512 * half + 512)
                    dve.tensor_tensor(merged[:, q, cols], acc[:, 2 * q + half, :], gate_r[:, q, cols], ALU.mult)\
                        .then_inc(S["ret_merged"], 1)
            split_plain()
            dve.wait_ge(S["mod_done"], 8)
            dve.wait_ge(S["rowsg_in"], 80)
            link(dve.scalar_tensor_tensor(mod[:, 4096:5120], mod[:, 4096:5120], 1.0, rows_g, ALU.add, ALU.mult))
            used(B_MO + 3)
            dve.wait_ge(S["gm_done"], 4)
            dve.wait_ge(S["ret_merged"], 4)
            for q in range(QT):
                bank = acc[:, 2 * q:2 * q + 2, :].rearrange("p a b -> p (a b)")
                link(dve.tensor_tensor(gate_m[:, q, :], bank, gate_m[:, q, :], ALU.mult))
                dve.tensor_tensor(merged[:, q, :], merged[:, q, :], gate_m[:, q, :], ALU.add)\
                    .then_inc(S["mla_merged"], 1)
            split_plain()

            def residual(q):
                bank = acc[:, 2 * q:2 * q + 2, :].rearrange("p a b -> p (a b)")
                link(dve.tensor_tensor(o_tm[:, q, :], bank, mod[:, 2048:3072], ALU.mult))
                link(dve.tensor_tensor(h_tm[:, q, :], h_tm[:, q, :], o_tm[:, q, :], ALU.add))

            def modulate(q):
                dve.wait_ge(S["r_rstd"], 2 + q + 1)
                link(dve.scalar_tensor_tensor(o_tm[:, q, :], h_tm[:, q, :], rstd[:, q:q + 1], mod[:, 4096:5120],
                                              ALU.mult, ALU.mult))
                dve.tensor_tensor(o_tm[:, q, :], o_tm[:, q, :], mod[:, 3072:4096], ALU.add).then_inc(S["r_out"], 1)

            dve.wait_ge(S["tile_ready"], 5)
            residual(0)
            row_stats(0, h_tm[:, 0, :], EPS, S["r_stat"], rms=True)
            modulate(0)
            used(B_WO + 3)
            residual(1)
            row_stats(1, h_tm[:, 1, :], EPS, S["r_stat"], rms=True)
            modulate(1)
            dve.wait_ge(S["r_out"], 4)
            for q in range(QT):
                link(dve.tensor_copy(u_hi[:, q, :], o_tm[:, q, :]))
                dve.tensor_tensor(u_lo[:, q, :], o_tm[:, q, :], u_hi[:, q, :], ALU.subtract).then_inc(S["u_split"], 1)

            dve.wait_ge(S["lg_ready"], 1)
            link(dve.tensor_copy(route[:, :, 0:36], pp[:, :, 0:36]))
            link(dve.tensor_reduce(route[:, :, 36:37], route[:, :, 0:4], AX.X, ALU.max))
            dve.tensor_scalar(route[:, :, 36:37], route[:, :, 36:37], -1.0, None, ALU.mult).then_inc(S["lg_max"], 1)
            dve.wait_ge(S["lg_max"], 1)
            dve.wait_ge(S["lg_exp"], 1)

            def both(step):
                for q in range(QT):
                    last = step(route[:, q, :], router[:, q, :], q)
                link(last)

            def first_max(out, src, width, top):
                order = con("order")[:, 0:width]

                def at(w):
                    return w[:, out:out + width]

                both(lambda r, w, q: dve.tensor_reduce(w[:, top:top + 1], src(r, w), AX.X, ALU.max))
                both(lambda r, w, q: dve.scalar_tensor_tensor(at(w), src(r, w), w[:, top:top + 1], order,
                                                              ALU.is_equal, ALU.mult))
                both(lambda r, w, q: dve.tensor_reduce(w[:, 34:35], at(w), AX.X, ALU.max))
                both(lambda r, w, q: dve.tensor_scalar(at(w), at(w), w[:, 34:35], None, ALU.is_equal))

            def picks(w):
                return w[:, 0:4].unsqueeze(2).to_broadcast([128, 4, 8])

            def prods(w):
                return w[:, 48:80].rearrange("p (g e) -> p g e", g=4)

            first_max(0, lambda r, w: r[:, 0:4], 4, 32)
            both(lambda r, w, q: dve.tensor_tensor(prods(w), r[:, 4:36].rearrange("p (g e) -> p g e", g=4), picks(w),
                                                   ALU.mult))
            both(lambda r, w, q: dve.tensor_reduce(w[:, 8:16], prods(w).rearrange("p g e -> p e g"), AX.X, ALU.add))
            first_max(16, lambda r, w: w[:, 8:16], 8, 32)
            both(lambda r, w, q: dve.scalar_tensor_tensor(w[:, 40:48], w[:, 16:24], NEG, w[:, 8:16],
                                                          ALU.mult, ALU.add))
            first_max(24, lambda r, w: w[:, 40:48], 8, 33)
            for q in range(QT):
                w = router[:, q, :]
                last = dve.tensor_tensor(route[:, q, 38:39], w[:, 33:34], w[:, 32:33], ALU.subtract)
            last.then_inc(S["lg_m2"], 1)
            both(lambda r, w, q: dve.tensor_tensor(w[:, 8:16], w[:, 16:24], w[:, 24:32], ALU.add))
            for q in range(QT):
                w = router[:, q, :]
                m3 = picked[:, q, :].rearrange("p (g e) -> p g e", g=4)
                last = dve.tensor_tensor(m3, picks(w), w[:, 8:16].unsqueeze(1).to_broadcast([128, 4, 8]), ALU.mult)
            last.then_inc(S["mask_ready"], 1)
            dve.wait_ge(S["lg_e2"], 1)
            both(lambda r, w, q: dve.reciprocal(w[:, 35:36], r[:, 37:38]))
            both(lambda r, w, q: dve.tensor_scalar(w[:, 36:37], r[:, 39:40], 1.0, None, ALU.add))
            both(lambda r, w, q: dve.reciprocal(w[:, 36:37], w[:, 36:37]))
            both(lambda r, w, q: dve.tensor_tensor(w[:, 36:37], w[:, 36:37], w[:, 35:36], ALU.mult))
            both(lambda r, w, q: dve.tensor_tensor(w[:, 37:38], w[:, 36:37], r[:, 39:40], ALU.mult))
            both(lambda r, w, q: dve.tensor_scalar(w[:, 40:48], w[:, 24:32], w[:, 37:38], None, ALU.mult))
            both(lambda r, w, q: dve.scalar_tensor_tensor(w[:, 40:48], w[:, 16:24], w[:, 36:37], w[:, 40:48],
                                                          ALU.mult, ALU.add))
            both(lambda r, w, q: dve.tensor_tensor(gates[:, q, :].rearrange("p (g e) -> p g e", g=4), picks(w),
                                                   w[:, 40:48].unsqueeze(1).to_broadcast([128, 4, 8]), ALU.mult))
            dve.wait_ge(S["pos_ready"], 1)
            pos = pp[:, 0, 0:64].rearrange("p (q e) -> p q e", q=2)
            link(dve.scalar_tensor_tensor(posn[:, :, :], pos, 1.0, picked[:, :, :], ALU.add, ALU.mult))
            link(dve.tensor_scalar(posn[:, :, :], posn[:, :, :], -1.0, None, ALU.add))
            iota = con("iota")

            def select():
                for q in range(QT):
                    for e in range(4):
                        last = dve.tensor_scalar(sel[:, q, 64 * e:64 * e + 64], iota,
                                                 now[:, 4 * q + e:4 * q + e + 1], None, ALU.is_equal)
                last.then_inc(S["sel_ready"], 1)

            for q in range(QT):
                dve.tensor_copy(now[:, 4 * q:4 * q + 4], posn[:, q, 0:4])
                last = dve.tensor_copy(now[:, 8 + 4 * q:12 + 4 * q], gates[:, q, 0:4])
            link(last)
            select()
            link(dve.tensor_reduce(cnt[:, 0:1], pp[:, 0, 64:96], AX.X, ALU.max))
            for r in range(1, ROUNDS):
                link(dve.tensor_scalar(cnt[:, r:r + 1], cnt[:, 0:1], float(SLOTS * r), None, ALU.is_gt))
            link(dve.tensor_reduce(cnt[:, 4:5], cnt[:, 1:4], AX.X, ALU.add))
            link(dve.tensor_scalar(cnt[:, 4:5], cnt[:, 4:5], 1.0, None, ALU.add))
            link(dve.tensor_scalar(cnt[:, 5:6], cnt[:, 4:5], float(STEPS), None, ALU.mult))
            link(dve.tensor_copy(trips[:, 1:2], cnt[:, 4:5]))
            dve.tensor_copy(trips[:, 0:1], cnt[:, 5:6]).then_inc(S["trips_ready"], 1)
            dve.wait_ge(S["trips_ready"], 1)
            link(dve.memset(plan[:, ROUNDS * STEPS, :], -1.0))
            for r in range(ROUNDS):
                part = plan[:, r * STEPS:(r + 1) * STEPS, :].rearrange("p s (w q e) -> p s w q e", w=2, q=2)
                for q in range(QT):
                    src = posn[:, q, :].rearrange("p (s e) -> p s e", e=4)
                    dve.tensor_scalar(part[:, :, 0, q, :], src, float(-SLOTS * r), None, ALU.add)
                    last = dve.tensor_copy(part[:, :, 1, q, :], gates[:, q, :].rearrange("p (s e) -> p s e", e=4))
                link(last)
            steps = dve.value_load(trips[0:1, 0:1], min_val=STEPS, max_val=ROUNDS * STEPS)
            base = n[0]
            with dve.Fori(0, steps) as i:
                for pair in range(2):
                    for q in range(QT):
                        for e in range(2):
                            at = 4 * q + 2 * pair + e
                            last = dve.tensor_scalar(gsel[:, pair, q, 64 * e:64 * e + 64], iota, now[:, at:at + 1],
                                                     now[:, 8 + at:9 + at], ALU.is_equal, ALU.mult)
                last.then_inc(S["gsel_ready"], 1)
                dve.wait_ge(S["gsel_ready"], i + 1)
                dve.tensor_copy(now[:, :], plan[:, bass.ds(i + 1, 1), :].rearrange("p a b -> p (a b)"))\
                    .then_inc(S["dve_chain"], 1)
                dve.wait_ge(S["dve_chain"], i + (base + 1))
                dve.wait_ge(S["xe_ready"], i * 4 + 4)
                select()
                for pair in range(2):
                    dve.wait_ge(S["silu_done"], i * 2 + (pair + 1))
                    dve.tensor_tensor(hid_e, silu_e, up_bank[:, 256:512], ALU.mult).then_inc(S["hid_done"], 1)
                    dve.wait_ge(S["turn_ready"], i * 2 + (pair + 1))
                    dve.tensor_copy(slot_gate[:, :], up_bank[:, 0:1]).then_inc(S["gate_done"], 1)
                    dve.wait_ge(S["turned_done"], i * 2 + (pair + 2))
                    dve.tensor_scalar(place_t, turned[:, 256:512], 0.0, None, ALU.is_gt)
                    dve.wait_ge(S["gate_done"], i * 2 + (pair + 1))
                    for half in range(2):
                        dve.wait_ge(S[f"y{half}_done"], i * 2 + (pair + 1))
                        dve.scalar_tensor_tensor(y_lo[:, half, :], y_bank[half], slot_gate[:, 0:1], y_hi[:, half, :],
                                                 ALU.mult, ALU.subtract).then_inc(S[f"y{half}_low"], 1)
            dve.wait_ge(S["rowsb_in"], 80)
            fin = [0]

            def flink(ins):
                fin[0] += 1
                ins.then_inc(S["final_chain"], 1)
                dve.wait_ge(S["final_chain"], fin[0])

            def final_sum(q):
                dve.wait_ge(S["sums_ready"], q + 1)
                sums = acc[:, 2 * q:2 * q + 2, :].rearrange("p a b -> p (a b)")
                flink(dve.tensor_tensor(moe[:, q, :], sums, mod[:, 5120:6144], ALU.mult))
                flink(dve.tensor_tensor(h_tm[:, q, :], h_tm[:, q, :], moe[:, q, :], ALU.add))

            def final_stats(q):
                for a in range(2):
                    last = dve.bn_stats(st6[:, q, a, :], h_tm[:, q, 512 * a:512 * a + 512])
                flink(last)
                flink(dve.bn_aggr(mv[:, q, :], st6[:, q, :, :].rearrange("p a b -> p (a b)")))
                flink(dve.scalar_tensor_tensor(sv[:, q:q + 1], mv[:, q, 0:1], mv[:, q, 0:1], mv[:, q, 1:2],
                                               ALU.mult, ALU.add))
                flink(dve.tensor_scalar(sv[:, q:q + 1], sv[:, q:q + 1], EPS, None, ALU.add))
                dve.reciprocal(sr[:, q:q + 1], sv[:, q:q + 1]).then_inc(S["r_stat"], 1)

            def final_rows(q):
                dve.wait_ge(S["r_rstd"], 4 + q + 1)
                dve.scalar_tensor_tensor(h_tm[:, q, :], h_tm[:, q, :], rstd[:, q:q + 1], rows_b,
                                         ALU.mult, ALU.mult).then_inc(S["out_ready"], 1)

            final_sum(0)
            final_stats(0)
            final_sum(1)
            final_rows(0)
            final_stats(1)
            final_rows(1)


def constant_tables():
    f = np.float32
    t = {"ident": np.eye(128, dtype=f)}
    pos = np.arange(SEQ, dtype=f)

    def rope(dim, copies):
        inv = (f(10000.0) ** (-np.arange(0, dim, 2, dtype=f) / f(dim))).astype(f)
        angle = pos[None, :] * inv[:, None]
        return [np.tile(fn(angle.astype(f)).astype(f), (copies, 1)) for fn in (np.cos, np.sin)]

    t["cos_ret"], t["sin_ret"] = rope(256, 1)
    t["cos_mla"], t["sin_mla"] = rope(64, 4)
    log_gamma = np.log1p(-np.exp2(-5.0 - np.arange(4, dtype=f))).astype(f)
    rel = np.arange(SEQ, dtype=f)[None, :] - np.arange(128, dtype=f)[:, None]
    decay = [np.where(rel >= 0, np.exp(g * np.maximum(rel, 0)), 0) * 256 ** -0.5 for g in log_gamma]
    t["decay"] = np.concatenate(decay, axis=1)
    i = np.arange(128)
    t["tri"] = (i[:, None] < i[None, :]).astype(f)
    t["ones"] = np.ones((128, 128), f)
    t["iota"] = np.tile(np.arange(64, dtype=f), (128, 1))
    k = np.arange(SEQ)
    t["mask"] = np.concatenate([np.where(k[None, :128] > i[:, None], NEG, 0),
                                np.where(k[None, :] > 128 + i[:, None], NEG, 0)], axis=1)
    t["order"] = np.tile(100.0 - np.arange(8), (128, 1))
    table = np.concatenate([t[name].astype(f) for name, _ in CONST_WIDTHS], axis=1)
    late = np.ascontiguousarray(np.concatenate([t[name].astype(f) for name, _ in LATE_WIDTHS], axis=1))
    n = 255 - np.arange(512)
    nf = np.maximum(n, 16).astype(f)
    large = 16 + (np.log(nf / f(16)) / f(math.log(128 / 16)) * f(16)).astype(np.int32)
    bucket = np.where(n < 0, 32, np.where(n < 16, n, np.minimum(large, 31)))
    onehot = (np.arange(33)[:, None] == bucket[None, :]).astype(f)
    return np.ascontiguousarray(table), late, onehot


_INS = ["x", "w_in_a", "lam_a", "subln_a", "w_out_a", "w_kv_shared", "w_q_b", "w_out_b", "rel_bias", "ln1_g", "ln1_b",
        "ln2_g", "ln2_b", "w_up", "w_down", "c_2", "w_ada_2", "b_ada_2", "norm1_2", "norm2_2", "w_in_2", "w_ret_o_2",
        "q_norm_2", "kv_norm_2", "w_uq_2", "w_ukv_2", "w_mla_o_2", "w_out_2", "w_grp_2", "b_grp_2", "w_exp_2",
        "b_exp_2", "w1_2", "w3_2", "w2_2", "final_norm_2"]


def kernel(**inputs):
    import concourse.bacc as _bacc
    from concourse.bass_utils import run_bass_kernel_spmd as _run

    nc = _bacc.Bacc("TRN2", target_bir_lowering=False, num_devices=1)
    arrays, aps = {}, {}
    given = {name: np.ascontiguousarray(inputs[name]) for name in _INS}
    given["consts"], given["late"], given["onehot"] = constant_tables()
    for name, a in given.items():
        arrays[f"in_{name}_dram"] = a
        aps[name] = nc.dram_tensor(f"in_{name}_dram", a.shape, mybir.dt.from_np(a.dtype), kind="ExternalInput").ap()
    aps["bias_dram"] = nc.dram_tensor("bias_dram", (16, 128, 512), mybir.dt.float32, kind="Internal").ap()
    aps["out"] = nc.dram_tensor("out_dram", (1, SEQ, D), mybir.dt.float32, kind="ExternalOutput").ap()
    program(nc, aps)
    r = _run(nc, [arrays], core_ids=[0])
    return r.results[0]["out_dram"]
```
